# Optimizing a Trainium2 kernel written in Bass

```python
import math
import jax, jax.numpy as jnp
from jax import lax
import numpy as np

D_MODEL = 1024
BATCH = 1
SEQ = 256
DEPTH = 2

N_A_LAYERS = DEPTH // 2
N_B_LAYERS = DEPTH - N_A_LAYERS
D_FF = 4 * D_MODEL
NORM_EPS = 1e-6
NEG = -1e30

DIFF_HEAD_DIM = 64
DIFF_HEADS = D_MODEL // (2 * DIFF_HEAD_DIM)
Q_BLOCK = 128

REL_BUCKETS = 32
REL_MAX_DIST = 128
REL_HEADS = 2 * DIFF_HEADS

NSA_HEAD_DIM = 64
NSA_HEADS = D_MODEL // NSA_HEAD_DIM
NSA_KV_HEADS = 4
NSA_GROUP = NSA_HEADS // NSA_KV_HEADS
CMP_LEN = 32
CMP_STRIDE = 16
CMP_HIDDEN = 256
SLC_LEN = 64
SLC_TOPK = 16
SLC_FORCED_LOCAL = 2
FORCE_BONUS = 1e4
WINDOW = 512
NSA_Q_BLOCK = 32
NSA_IN_COLS = NSA_HEADS * NSA_HEAD_DIM + 3 * NSA_HEADS
KV_COLS = 6 * NSA_KV_HEADS * NSA_HEAD_DIM


def rms_norm(x, g):
    xf = x.astype(jnp.float32)
    y = xf * lax.rsqrt(jnp.mean(xf * xf, axis=-1, keepdims=True) + NORM_EPS)
    return (y * g.astype(jnp.float32)).astype(x.dtype)

def modulate(h, shift, scale):
    return h * (1 + scale) + shift

def t5_bucket(dist):
    n = jnp.maximum(dist, 0)
    max_exact = REL_BUCKETS // 2
    nf = jnp.maximum(n, 1).astype(jnp.float32)
    large = max_exact + (jnp.log(nf / max_exact) / math.log(REL_MAX_DIST / max_exact)
                         * (REL_BUCKETS - max_exact)).astype(jnp.int32)
    large = jnp.minimum(large, REL_BUCKETS - 1)
    return jnp.where(n < max_exact, n, large)

def squared_relu_mlp(h, w1, w2):
    return jnp.square(jax.nn.relu(h @ w1)) @ w2

def diff_attention(h, w_in, w_out, lam, subln, rel_bias, layer_idx):
    B, T, _ = h.shape
    H, d = DIFF_HEADS, DIFF_HEAD_DIM
    q, k, v = jnp.split(h @ w_in, 3, axis=-1)
    q = q.reshape(B, T, H, 2, d)
    k = k.reshape(B, T, H, 2, d)
    v = v.reshape(B, T, H, 2 * d)
    lam_init = 0.8 - 0.6 * math.exp(-0.3 * layer_idx)
    lf = lam.astype(jnp.float32)
    lam_full = jnp.exp(jnp.sum(lf[0] * lf[1])) - jnp.exp(jnp.sum(lf[2] * lf[3])) + lam_init
    bias_tab = rel_bias.reshape(REL_BUCKETS, H, 2).astype(jnp.float32)
    k_pos = jnp.arange(T)
    scale = d ** -0.5
    nblk = T // Q_BLOCK
    qb = q.reshape(B, nblk, Q_BLOCK, H, 2, d).transpose(1, 0, 2, 3, 4, 5)

    def block(args):
        qi, blk = args
        q_pos = blk * Q_BLOCK + jnp.arange(Q_BLOCK)
        dist = q_pos[:, None] - k_pos[None, :]
        bias = bias_tab[t5_bucket(dist)].transpose(2, 3, 0, 1)
        s = jnp.einsum('bqhmd,bkhmd->bhmqk', qi, k,
                       preferred_element_type=jnp.float32) * scale + bias[None]
        s = jnp.where((dist >= 0)[None, None, None], s, NEG)
        p = jax.nn.softmax(s, axis=-1)
        a = p[:, :, 0] - lam_full * p[:, :, 1]
        return jnp.einsum('bhqk,bkhe->bqhe', a.astype(v.dtype), v)

    o = lax.map(block, (qb, jnp.arange(nblk)))
    o = o.transpose(1, 0, 2, 3, 4).reshape(B, T, H, 2 * d)
    o = rms_norm(o, subln) * (1 - lam_init)
    return o.reshape(B, T, H * 2 * d) @ w_out

def nsa_shared_kv(h, w_kv, cmp_pos, cmp_w1, cmp_w2):
    B, T, _ = h.shape
    G, d = NSA_KV_HEADS, NSA_HEAD_DIM
    kv = (h @ w_kv).reshape(B, T, 6, G, d).transpose(2, 0, 3, 1, 4)
    n_cmp = (T - CMP_LEN) // CMP_STRIDE + 1
    idx = jnp.arange(n_cmp)[:, None] * CMP_STRIDE + jnp.arange(CMP_LEN)[None, :]
    blocks = kv[0:2][:, :, :, idx] + cmp_pos[:, None, None, None]
    flat = blocks.reshape(2, B, G, n_cmp, CMP_LEN * d)
    hid = jax.nn.gelu(jnp.einsum('sbgnf,sfh->sbgnh', flat, cmp_w1))
    cmp = jnp.einsum('sbgnh,shd->sbgnd', hid, cmp_w2)
    return (cmp[0], cmp[1], kv[2], kv[3], kv[4], kv[5])

def nsa_attention(h, w_in, w_out, rel_bias, k_cmp, v_cmp, k_slc, v_slc, k_win, v_win):
    B, T, _ = h.shape
    H, G, R, d = NSA_HEADS, NSA_KV_HEADS, NSA_GROUP, NSA_HEAD_DIM
    proj = h @ w_in
    q = proj[..., :H * d].reshape(B, T, G, R, d)
    gates = jax.nn.sigmoid(proj[..., H * d:].astype(jnp.float32)).reshape(B, T, G, R, 3)
    scale = d ** -0.5
    bias_tab = rel_bias.reshape(REL_BUCKETS, G, R).astype(jnp.float32)
    bias_tab_g = bias_tab.transpose(1, 0, 2)
    n_cmp = k_cmp.shape[2]
    n_slc = T // SLC_LEN
    top_k = min(SLC_TOPK, n_slc)
    cmp_start = jnp.arange(n_cmp) * CMP_STRIDE
    cmp_end = cmp_start + CMP_LEN - 1
    slc_start = jnp.arange(n_slc) * SLC_LEN
    overlap = ((cmp_start[:, None] < slc_start[None, :] + SLC_LEN)
               & (cmp_end[:, None] >= slc_start[None, :])).astype(jnp.float32)
    k_slc_blk = k_slc.reshape(B, G, n_slc, SLC_LEN, d)
    v_slc_blk = v_slc.reshape(B, G, n_slc, SLC_LEN, d)
    k_win_pad = jnp.pad(k_win, ((0, 0), (0, 0), (WINDOW, 0), (0, 0)))
    v_win_pad = jnp.pad(v_win, ((0, 0), (0, 0), (WINDOW, 0), (0, 0)))
    b_idx = jnp.arange(B)[:, None, None, None]
    g_idx = jnp.arange(G)[None, :, None, None]
    j_idx = jnp.arange(n_slc)
    in_offs = jnp.arange(SLC_LEN)
    nblk = T // NSA_Q_BLOCK
    qb = q.reshape(B, nblk, NSA_Q_BLOCK, G, R, d).transpose(1, 0, 2, 3, 4, 5)
    gb = gates.reshape(B, nblk, NSA_Q_BLOCK, G, R, 3).transpose(1, 0, 2, 3, 4, 5)

    def block(args):
        qi, gi, blk = args
        q_pos = blk * NSA_Q_BLOCK + jnp.arange(NSA_Q_BLOCK)
        s_c = jnp.einsum('bqgrd,bgnd->bgrqn', qi, k_cmp,
                         preferred_element_type=jnp.float32) * scale
        valid_c = cmp_end[None, :] <= q_pos[:, None]
        p_c = jax.nn.softmax(jnp.where(valid_c, s_c, NEG), axis=-1) * valid_c
        o_c = jnp.einsum('bgrqn,bgnd->bqgrd', p_c.astype(v_cmp.dtype), v_cmp)
        imp = jnp.einsum('bgrqn,nj->bgqj', p_c, overlap)
        q_blk = q_pos // SLC_LEN
        forced = (j_idx[None, :] == 0) | ((j_idx[None, :] <= q_blk[:, None])
                                          & (j_idx[None, :] > q_blk[:, None] - SLC_FORCED_LOCAL))
        imp = jnp.where(forced[None, None], FORCE_BONUS, imp)
        imp = jnp.where((j_idx[None, :] <= q_blk[:, None])[None, None], imp, NEG)
        _, sel = lax.top_k(imp, top_k)
        ks = k_slc_blk[b_idx, g_idx, sel].reshape(B, G, NSA_Q_BLOCK, top_k * SLC_LEN, d)
        vs = v_slc_blk[b_idx, g_idx, sel].reshape(B, G, NSA_Q_BLOCK, top_k * SLC_LEN, d)
        pos_s = (sel[..., None] * SLC_LEN + in_offs).reshape(B, G, NSA_Q_BLOCK, top_k * SLC_LEN)
        dist_s = q_pos[None, None, :, None] - pos_s
        bias_s = bias_tab_g[g_idx, t5_bucket(dist_s)].transpose(0, 1, 4, 2, 3)
        s_s = jnp.einsum('bqgrd,bgqkd->bgrqk', qi, ks,
                         preferred_element_type=jnp.float32) * scale + bias_s
        s_s = jnp.where((dist_s >= 0)[:, :, None], s_s, NEG)
        p_s = jax.nn.softmax(s_s, axis=-1)
        o_s = jnp.einsum('bgrqk,bgqkd->bqgrd', p_s.astype(vs.dtype), vs)
        start = blk * NSA_Q_BLOCK
        kw = lax.dynamic_slice_in_dim(k_win_pad, start, WINDOW + NSA_Q_BLOCK, axis=2)
        vw = lax.dynamic_slice_in_dim(v_win_pad, start, WINDOW + NSA_Q_BLOCK, axis=2)
        k_pos = start - WINDOW + jnp.arange(WINDOW + NSA_Q_BLOCK)
        dist_w = q_pos[:, None] - k_pos[None, :]
        valid_w = (dist_w >= 0) & (dist_w < WINDOW) & (k_pos[None, :] >= 0)
        bias_w = bias_tab[t5_bucket(dist_w)].transpose(2, 3, 0, 1)
        s_w = jnp.einsum('bqgrd,bgkd->bgrqk', qi, kw,
                         preferred_element_type=jnp.float32) * scale + bias_w[None]
        p_w = jax.nn.softmax(jnp.where(valid_w[None, None, None], s_w, NEG), axis=-1)
        o_w = jnp.einsum('bgrqk,bgkd->bqgrd', p_w.astype(vw.dtype), vw)
        o = gi[..., 0:1] * o_c + gi[..., 1:2] * o_s + gi[..., 2:3] * o_w
        return o.astype(qi.dtype)

    o = lax.map(block, (qb, gb, jnp.arange(nblk)))
    o = o.transpose(1, 0, 2, 3, 4, 5).reshape(B, T, H * d)
    return o @ w_out

def first_inputs(seed: int = 0) -> dict:
    key = jax.random.key(seed)
    ks = jax.random.split(key, 24)
    f32 = jnp.float32
    D, d_a, d_n = D_MODEL, DIFF_HEAD_DIM, NSA_HEAD_DIM
    nrm = lambda k, shape, s: jax.random.normal(k, shape, f32) * s
    gain = lambda k, shape: 1.0 + 0.02 * jax.random.normal(k, shape, f32)
    return {
        "x": nrm(ks[0], (BATCH, SEQ, D), 1.0),
        "c": nrm(ks[1], (BATCH, D), 1.0),
        "rel_bias": nrm(ks[2], (REL_BUCKETS, REL_HEADS), 0.5),
        "ada_w": nrm(ks[3], (DEPTH, D, 6 * D), D ** -0.5),
        "ada_b": nrm(ks[4], (DEPTH, 6 * D), 0.02),
        "attn_norm": gain(ks[5], (DEPTH, D)),
        "mlp_norm": gain(ks[6], (DEPTH, D)),
        "mlp_w1": nrm(ks[7], (DEPTH, D, D_FF), D ** -0.5),
        "mlp_w2": nrm(ks[8], (DEPTH, D_FF, D), D_FF ** -0.5),
        "a_w_in": nrm(ks[9], (N_A_LAYERS, D, 3 * D), D ** -0.5),
        "a_w_out": nrm(ks[10], (N_A_LAYERS, D, D), D ** -0.5),
        "a_lambda": nrm(ks[11], (N_A_LAYERS, 4, d_a), 0.1),
        "a_subln": gain(ks[12], (N_A_LAYERS, 2 * d_a)),
        "kv_ada_w": nrm(ks[13], (D, 2 * D), D ** -0.5),
        "kv_ada_b": nrm(ks[14], (2 * D,), 0.02),
        "kv_norm": gain(ks[15], (D,)),
        "w_kv": nrm(ks[16], (D, KV_COLS), D ** -0.5),
        "cmp_pos": nrm(ks[17], (2, CMP_LEN, d_n), 0.1),
        "cmp_w1": nrm(ks[18], (2, CMP_LEN * d_n, CMP_HIDDEN), (CMP_LEN * d_n) ** -0.5),
        "cmp_w2": nrm(ks[19], (2, CMP_HIDDEN, d_n), CMP_HIDDEN ** -0.5),
        "b_w_in": nrm(ks[20], (N_B_LAYERS, D, NSA_IN_COLS), D ** -0.5),
        "b_w_out": nrm(ks[21], (N_B_LAYERS, D, D), D ** -0.5),
        "final_norm": gain(ks[22], (D,)),
    }

def first_block(x, c, rel_bias, ada_w, ada_b, attn_norm, mlp_norm, mlp_w1, mlp_w2,
              a_w_in, a_w_out, a_lambda, a_subln, kv_ada_w, kv_ada_b, kv_norm, w_kv,
              cmp_pos, cmp_w1, cmp_w2, b_w_in, b_w_out, final_norm):
    c_act = jax.nn.silu(c)
    shared = None
    for layer in range(DEPTH):
        mod = (c_act @ ada_w[layer] + ada_b[layer])[:, None, :]
        sh_a, sc_a, gt_a, sh_m, sc_m, gt_m = jnp.split(mod, 6, axis=-1)
        h = modulate(rms_norm(x, attn_norm[layer]), sh_a, sc_a)
        if layer < N_A_LAYERS:
            mix = diff_attention(h, a_w_in[layer], a_w_out[layer], a_lambda[layer],
                                 a_subln[layer], rel_bias, layer)
        else:
            i = layer - N_A_LAYERS
            mix = nsa_attention(h, b_w_in[i], b_w_out[i], rel_bias, *shared)
        x = x + gt_a * mix
        h = modulate(rms_norm(x, mlp_norm[layer]), sh_m, sc_m)
        x = x + gt_m * squared_relu_mlp(h, mlp_w1[layer], mlp_w2[layer])
        if layer == N_A_LAYERS - 1:
            kv_mod = (c_act @ kv_ada_w + kv_ada_b)[:, None, :]
            sh_kv, sc_kv = jnp.split(kv_mod, 2, axis=-1)
            h_kv = modulate(rms_norm(x, kv_norm), sh_kv, sc_kv)
            shared = nsa_shared_kv(h_kv, w_kv, cmp_pos, cmp_w1, cmp_w2)
    return rms_norm(x, final_norm)


N_MIXERS = 2
MLA_HEADS = 8
MLA_Q_RANK = 384
MLA_KV_RANK = 256
MLA_NOPE_DIM = 128
MLA_ROPE_DIM = 64
MLA_V_DIM = 128
ROPE_THETA = 10000.0
MOBA_HEADS = 8
MOBA_HEAD_DIM = D_MODEL // MOBA_HEADS
MOBA_BLOCK = 256
MOBA_TOP_K = 3
REL_MAX_DISTANCE = 1024
D_FF_2 = 4 * D_MODEL
RMS_EPS = 1e-6
N_MLA_LAYERS = (DEPTH + 1) // 2
N_MOBA_LAYERS = DEPTH // 2


def rms_norm_2(x, g):
    xf = x.astype(jnp.float32)
    y = xf * lax.rsqrt(jnp.mean(xf * xf, axis=-1, keepdims=True) + RMS_EPS)
    return (y * g.astype(jnp.float32)).astype(x.dtype)

def rope_tables(positions):
    inv_freq = ROPE_THETA ** (-jnp.arange(0, MLA_ROPE_DIM, 2, dtype=jnp.float32) / MLA_ROPE_DIM)
    ang = positions.astype(jnp.float32)[..., None] * inv_freq
    return jnp.cos(ang), jnp.sin(ang)

def rope(x, cos, sin):
    half = x.shape[-1] // 2
    x1 = x[..., :half].astype(jnp.float32)
    x2 = x[..., half:].astype(jnp.float32)
    return jnp.concatenate([x1 * cos - x2 * sin, x2 * cos + x1 * sin], axis=-1).astype(x.dtype)

def t5_bucket_2(dist):
    n = jnp.maximum(dist, 0)
    max_exact = REL_BUCKETS // 2
    nf = jnp.maximum(n, 1).astype(jnp.float32)
    large = max_exact + (jnp.log(nf / max_exact) / math.log(REL_MAX_DISTANCE / max_exact)
                         * (REL_BUCKETS - max_exact)).astype(jnp.int32)
    large = jnp.minimum(large, REL_BUCKETS - 1)
    return jnp.where(n < max_exact, n, large)

def sq_relu_mlp(h, w_in, w_out):
    a = jax.nn.relu(h @ w_in)
    return (a * a) @ w_out

def mla_attention(q_nope, q_pe, k_nope, k_pe, v):
    B, H, S, _ = q_nope.shape
    nqb = S // Q_BLOCK
    scale = 1.0 / math.sqrt(MLA_NOPE_DIM + MLA_ROPE_DIM)
    k_idx = jnp.arange(S)

    def to_blocks(t):
        return jnp.moveaxis(t.reshape(B, H, nqb, Q_BLOCK, t.shape[-1]), 2, 0)

    def body(args):
        qn, qp, c = args
        logits = (jnp.einsum('bhqd,bhkd->bhqk', qn, k_nope)
                  + jnp.einsum('bhqd,bkd->bhqk', qp, k_pe)).astype(jnp.float32) * scale
        q_idx = c * Q_BLOCK + jnp.arange(Q_BLOCK)
        causal = k_idx[None, :] <= q_idx[:, None]
        logits = jnp.where(causal, logits, -jnp.inf)
        p = jax.nn.softmax(logits, axis=-1).astype(v.dtype)
        return jnp.einsum('bhqk,bhkd->bhqd', p, v)

    out = lax.map(body, (to_blocks(q_nope), to_blocks(q_pe), jnp.arange(nqb, dtype=jnp.int32)))
    return jnp.moveaxis(out, 0, 2).reshape(B, H, S, v.shape[-1])

def mla_mixer(h, w_in, q_a_norm, kv_a_norm, w_uq, w_ukv, q_nope_norm, q_rope_norm,
              k_nope_norm, k_rope_norm, w_o, cos, sin):
    B, S, _ = h.shape
    proj = h @ w_in
    c_q = proj[..., :MLA_Q_RANK]
    c_kv = proj[..., MLA_Q_RANK:MLA_Q_RANK + MLA_KV_RANK]
    k_pe = proj[..., MLA_Q_RANK + MLA_KV_RANK:]
    q = (rms_norm_2(c_q, q_a_norm) @ w_uq).reshape(B, S, MLA_HEADS, MLA_NOPE_DIM + MLA_ROPE_DIM)
    kv = (rms_norm_2(c_kv, kv_a_norm) @ w_ukv).reshape(B, S, MLA_HEADS, MLA_NOPE_DIM + MLA_V_DIM)
    q_nope = rms_norm_2(q[..., :MLA_NOPE_DIM], q_nope_norm)
    q_pe = rope(rms_norm_2(q[..., MLA_NOPE_DIM:], q_rope_norm), cos[:, :, None, :], sin[:, :, None, :])
    k_nope = rms_norm_2(kv[..., :MLA_NOPE_DIM], k_nope_norm)
    v = kv[..., MLA_NOPE_DIM:]
    k_pe = rope(rms_norm_2(k_pe, k_rope_norm), cos, sin)
    out = mla_attention(q_nope.transpose(0, 2, 1, 3), q_pe.transpose(0, 2, 1, 3),
                        k_nope.transpose(0, 2, 1, 3), k_pe, v.transpose(0, 2, 1, 3))
    return out.transpose(0, 2, 1, 3).reshape(B, S, MLA_HEADS * MLA_V_DIM) @ w_o

def moba_attention(q, k, v, positions, rel_bias_table):
    B, H, S, dh = q.shape
    nb = -(-S // MOBA_BLOCK)
    pad = nb * MOBA_BLOCK - S
    n_sel = min(MOBA_TOP_K, nb - 1)
    nqb = S // Q_BLOCK
    scale = 1.0 / math.sqrt(dh)
    kb = jnp.pad(k, ((0, 0), (0, 0), (0, pad), (0, 0))).reshape(B, H, nb, MOBA_BLOCK, dh)
    vb = jnp.pad(v, ((0, 0), (0, 0), (0, pad), (0, 0))).reshape(B, H, nb, MOBA_BLOCK, dh)
    k_mean = jnp.mean(kb.astype(jnp.float32), axis=3)
    pos_b = jnp.pad(positions, ((0, 0), (0, pad)), mode='edge').reshape(B, nb, MOBA_BLOCK)
    pos_q = jnp.moveaxis(positions.reshape(B, nqb, Q_BLOCK), 1, 0)
    q_blocks = jnp.moveaxis(q.reshape(B, H, nqb, Q_BLOCK, dh), 2, 0)
    table_h = rel_bias_table.T
    b_i = jnp.arange(B)[:, None, None]
    h_i = jnp.arange(H)[None, :, None]
    h_i4 = jnp.arange(H)[None, :, None, None]
    blk_ids = jnp.arange(nb)
    t_ids = jnp.arange(MOBA_BLOCK)

    def rel_bias(pq, pk):
        return table_h[h_i4, t5_bucket_2(pq - pk)].astype(jnp.float32)

    def body(args):
        qi, pq, c = args
        q_start = c * Q_BLOCK
        own = q_start // MOBA_BLOCK
        q_idx = q_start + jnp.arange(Q_BLOCK)
        pq4 = pq[:, None, :, None]
        parts = []
        sel = None
        if n_sel > 0:
            gate = jnp.einsum('bhqd,bhnd->bhqn', qi.astype(jnp.float32), k_mean)
            gate = jnp.where(blk_ids < own, gate, -jnp.inf)
            _, sel = lax.top_k(gate, n_sel)
            for r in range(n_sel):
                sel_r = sel[..., r]
                k_sel = kb[b_i, h_i, sel_r]
                lg = (jnp.einsum('bhqd,bhqtd->bhqt', qi, k_sel).astype(jnp.float32) * scale
                      + rel_bias(pq4, pos_b[b_i, sel_r]))
                parts.append(jnp.where(r < own, lg, -jnp.inf))
        k_own = lax.dynamic_index_in_dim(kb, own, axis=2, keepdims=False)
        v_own = lax.dynamic_index_in_dim(vb, own, axis=2, keepdims=False)
        pos_own = lax.dynamic_index_in_dim(pos_b, own, axis=1, keepdims=False)
        lg_own = (jnp.einsum('bhqd,bhtd->bhqt', qi, k_own).astype(jnp.float32) * scale
                  + rel_bias(pq4, pos_own[:, None, None, :]))
        causal = (own * MOBA_BLOCK + t_ids)[None, :] <= q_idx[:, None]
        parts.append(jnp.where(causal, lg_own, -jnp.inf))
        p = jax.nn.softmax(jnp.concatenate(parts, axis=-1), axis=-1).astype(v.dtype)
        p = p.reshape(B, H, Q_BLOCK, n_sel + 1, MOBA_BLOCK)
        out = jnp.einsum('bhqt,bhtd->bhqd', p[..., n_sel, :], v_own)
        for r in range(n_sel):
            v_sel = vb[b_i, h_i, sel[..., r]]
            out = out + jnp.einsum('bhqt,bhqtd->bhqd', p[..., r, :], v_sel)
        return out

    out = lax.map(body, (q_blocks, pos_q, jnp.arange(nqb, dtype=jnp.int32)))
    return jnp.moveaxis(out, 0, 2).reshape(B, H, S, dh)

def moba_mixer(h, w_qkv, q_norm, k_norm, w_o, positions, rel_bias_table):
    B, S, _ = h.shape
    qkv = (h @ w_qkv).reshape(B, S, 3, MOBA_HEADS, MOBA_HEAD_DIM)
    q = rms_norm_2(qkv[:, :, 0], q_norm).transpose(0, 2, 1, 3)
    k = rms_norm_2(qkv[:, :, 1], k_norm).transpose(0, 2, 1, 3)
    v = qkv[:, :, 2].transpose(0, 2, 1, 3)
    out = moba_attention(q, k, v, positions, rel_bias_table)
    return out.transpose(0, 2, 1, 3).reshape(B, S, MOBA_HEADS * MOBA_HEAD_DIM) @ w_o

def second_inputs(seed: int = 0) -> dict:
    key = jax.random.key(seed)
    ks = jax.random.split(key, 24)

    def nrm(k, shape, scale):
        return scale * jax.random.normal(k, shape, jnp.float32)

    def gain(k, shape):
        return 1.0 + 0.05 * jax.random.normal(k, shape, jnp.float32)

    qk_dim = MLA_NOPE_DIM + MLA_ROPE_DIM
    offset = jax.random.randint(ks[1], (BATCH,), 0, 4096, dtype=jnp.int32)
    positions = offset[:, None] + jnp.arange(SEQ, dtype=jnp.int32)[None, :]
    return {
        "x": nrm(ks[0], (BATCH, SEQ, D_MODEL), 1.0),
        "positions": positions,
        "rel_bias_table": nrm(ks[2], (REL_BUCKETS, MOBA_HEADS), 0.5),
        "attn_norm": gain(ks[3], (DEPTH, D_MODEL)),
        "mlp_norm": gain(ks[4], (DEPTH, D_MODEL)),
        "mla_w_in": nrm(ks[5], (N_MLA_LAYERS, D_MODEL, MLA_Q_RANK + MLA_KV_RANK + MLA_ROPE_DIM), D_MODEL ** -0.5),
        "mla_q_a_norm": gain(ks[6], (N_MLA_LAYERS, MLA_Q_RANK)),
        "mla_kv_a_norm": gain(ks[7], (N_MLA_LAYERS, MLA_KV_RANK)),
        "mla_w_uq": nrm(ks[8], (N_MLA_LAYERS, MLA_Q_RANK, MLA_HEADS * qk_dim), MLA_Q_RANK ** -0.5),
        "mla_w_ukv": nrm(ks[9], (N_MLA_LAYERS, MLA_KV_RANK, MLA_HEADS * (MLA_NOPE_DIM + MLA_V_DIM)), MLA_KV_RANK ** -0.5),
        "mla_q_nope_norm": gain(ks[10], (N_MLA_LAYERS, MLA_NOPE_DIM)),
        "mla_q_rope_norm": gain(ks[11], (N_MLA_LAYERS, MLA_ROPE_DIM)),
        "mla_k_nope_norm": gain(ks[12], (N_MLA_LAYERS, MLA_NOPE_DIM)),
        "mla_k_rope_norm": gain(ks[13], (N_MLA_LAYERS, MLA_ROPE_DIM)),
        "mla_w_o": nrm(ks[14], (N_MLA_LAYERS, MLA_HEADS * MLA_V_DIM, D_MODEL), (MLA_HEADS * MLA_V_DIM) ** -0.5),
        "moba_w_qkv": nrm(ks[15], (N_MOBA_LAYERS, D_MODEL, 3 * MOBA_HEADS * MOBA_HEAD_DIM), D_MODEL ** -0.5),
        "moba_q_norm": gain(ks[16], (N_MOBA_LAYERS, MOBA_HEAD_DIM)),
        "moba_k_norm": gain(ks[17], (N_MOBA_LAYERS, MOBA_HEAD_DIM)),
        "moba_w_o": nrm(ks[18], (N_MOBA_LAYERS, MOBA_HEADS * MOBA_HEAD_DIM, D_MODEL), (MOBA_HEADS * MOBA_HEAD_DIM) ** -0.5),
        "mlp_w_in": nrm(ks[19], (DEPTH, D_MODEL, D_FF_2), D_MODEL ** -0.5),
        "mlp_w_out": nrm(ks[20], (DEPTH, D_FF_2, D_MODEL), D_FF_2 ** -0.5),
    }

def second_block(x, positions, rel_bias_table, attn_norm, mlp_norm, mla_w_in, mla_q_a_norm, mla_kv_a_norm,
              mla_w_uq, mla_w_ukv, mla_q_nope_norm, mla_q_rope_norm, mla_k_nope_norm, mla_k_rope_norm,
              mla_w_o, moba_w_qkv, moba_q_norm, moba_k_norm, moba_w_o, mlp_w_in, mlp_w_out):
    cos, sin = rope_tables(positions)
    for i in range(DEPTH):
        h = rms_norm_2(x, attn_norm[i])
        j = i // N_MIXERS
        if i % N_MIXERS == 0:
            x = x + mla_mixer(h, mla_w_in[j], mla_q_a_norm[j], mla_kv_a_norm[j], mla_w_uq[j], mla_w_ukv[j],
                              mla_q_nope_norm[j], mla_q_rope_norm[j], mla_k_nope_norm[j], mla_k_rope_norm[j],
                              mla_w_o[j], cos, sin)
        else:
            x = x + moba_mixer(h, moba_w_qkv[j], moba_q_norm[j], moba_k_norm[j], moba_w_o[j],
                               positions, rel_bias_table)
        h = rms_norm_2(x, mlp_norm[i])
        x = x + sq_relu_mlp(h, mlp_w_in[i], mlp_w_out[i])
    return x


def setup_inputs(seed=0):
    out = dict(first_inputs(seed))
    for name, value in second_inputs(seed + 1).items():
        if name != "x":
            out[name + "_2"] = value
    return out


def reference(
    x, c, rel_bias, ada_w, ada_b, attn_norm, mlp_norm, mlp_w1, mlp_w2, a_w_in, a_w_out,
    a_lambda, a_subln, kv_ada_w, kv_ada_b, kv_norm, w_kv, cmp_pos, cmp_w1, cmp_w2, b_w_in,
    b_w_out, final_norm, positions_2, rel_bias_table_2, attn_norm_2, mlp_norm_2, mla_w_in_2,
    mla_q_a_norm_2, mla_kv_a_norm_2, mla_w_uq_2, mla_w_ukv_2, mla_q_nope_norm_2,
    mla_q_rope_norm_2, mla_k_nope_norm_2, mla_k_rope_norm_2, mla_w_o_2, moba_w_qkv_2,
    moba_q_norm_2, moba_k_norm_2, moba_w_o_2, mlp_w_in_2, mlp_w_out_2,
):
    x = first_block(
        x, c, rel_bias, ada_w, ada_b, attn_norm, mlp_norm, mlp_w1, mlp_w2, a_w_in, a_w_out,
        a_lambda, a_subln, kv_ada_w, kv_ada_b, kv_norm, w_kv, cmp_pos, cmp_w1, cmp_w2, b_w_in,
        b_w_out, final_norm,
    )
    return second_block(
        x, positions_2, rel_bias_table_2, attn_norm_2, mlp_norm_2, mla_w_in_2, mla_q_a_norm_2,
        mla_kv_a_norm_2, mla_w_uq_2, mla_w_ukv_2, mla_q_nope_norm_2, mla_q_rope_norm_2,
        mla_k_nope_norm_2, mla_k_rope_norm_2, mla_w_o_2, moba_w_qkv_2, moba_q_norm_2,
        moba_k_norm_2, moba_w_o_2, mlp_w_in_2, mlp_w_out_2,
    )


_drawn_inputs = setup_inputs


def setup_inputs(seed=0):
    import zlib

    import numpy as np

    out = dict(_drawn_inputs(seed))
    spreads = {}
    factors = {'attn_norm': 4.466,
     'a_subln': 5.865,
     'kv_ada_b': 5.941,
     'kv_norm': 8.0,
     'cmp_pos': 4.32,
     'mla_q_a_norm_2': 8.0,
     'mla_q_nope_norm_2': 8.0,
     'mla_q_rope_norm_2': 8.0,
     'mla_k_nope_norm_2': 8.0,
     'mla_k_rope_norm_2': 8.0,
     'moba_q_norm_2': 8.0,
     'moba_k_norm_2': 8.0}
    for name, (base, spread) in spreads.items():
        noise = np.random.default_rng([zlib.crc32(name.encode()), seed]).standard_normal(out[name].shape)
        drawn = base * np.exp(spread * noise) if base else spread * noise
        out[name] = __import__('jax').numpy.asarray(drawn.astype(out[name].dtype))
    for name, factor in factors.items():
        out[name] = (out[name] * factor).astype(out[name].dtype)
    return out
```

```python
from contextlib import ExitStack
import math

import numpy as np

import concourse.bass as bass
from concourse import mybir

F32 = mybir.dt.float32
I32 = mybir.dt.int32
ALU = mybir.AluOpType
ACT = mybir.ActivationFunctionType
AX = mybir.AxisListType.X

P = 128
D = 1024
T = 256
TT = T // P
KT = D // P
FF = 4 * D
W = 512
SLOTS = 4
SLOT = KT * W
EPS = 1e-6
NEG = -1e30
HEADS = 16
BUCKETS = 32
NCMP = (T - 32) // 16 + 1
LAM_INIT = 0.8 - 0.6 * math.exp(-0.3 * 0)
GELU_C = math.sqrt(2.0 / math.pi)
BANKS = 4
TWO_PI = 2.0 * math.pi
STRIP = 3 * P
ATT = 4

PARAM_ROWS = [("c", 8), ("ada_b0", 48), ("ada_b1", 48), ("kv_b", 16),
              ("an0", 8), ("an1", 8), ("mn0", 8), ("mn1", 8), ("kvn", 8),
              ("an2_0", 8), ("an2_1", 8), ("mn2_0", 8), ("mn2_1", 8),
              ("subln", 1), ("qan", 3), ("kvan", 2), ("qnn", 1), ("knn", 1), ("mqn", 1), ("mkn", 1)]


def param_columns():
    col, at = {}, 0
    for name, n in PARAM_ROWS:
        col[name] = at
        at += n
    return col, at


def pow2_split(value, bits, parts):
    out = []
    for _ in range(parts - 1):
        e = math.floor(math.log2(abs(value))) if value else 0
        q = 2.0 ** (e - bits + 1)
        head = math.floor(value / q) * q
        out.append(head)
        value -= head
    return out + [value]


def weight_plan():
    plan = []

    def mat(name, k, n):
        return [((name, c), "mat", (name, c * W), k // P, min(W, n - c * W)) for c in range(-(-n // W))]

    def ada(layer, cs):
        return [((f"ada{layer}", c), "mat", (f"ada{layer}", c * W), KT, W) for c in cs]

    def mlp(tag):
        w1 = mat(f"{tag}_w1", D, FF)
        w2 = [((f"{tag}_w2", n, q), "mlp2", (f"{tag}_w2", n * W, q * KT), KT, W) for n in range(2) for q in range(4)]
        return w1 + w2

    def mix(a, b):
        out = []
        for i in range(max(len(a), len(b))):
            out += a[i:i + 1] + b[i:i + 1]
        return out

    plan += ada(0, range(4))
    plan += mix(mat("a_in", D, 3 * D), ada(0, range(4, 12)))
    plan += mat("a_out", D, D)
    plan += mix(mlp("m0"), ada("kv", range(4)) + ada(1, range(12)))
    plan += mat("w_kv", D, 1536)
    plan += [(("cmp_w1", s), "cmp", ("cmp_w1", s), 16, 256) for s in range(2)]
    plan += mat("b_in", D, 1072) + mat("b_out", D, D) + mlp("m1")
    plan += mat("l_in", D, 704) + mat("l_uq", 384, 1536) + mat("l_ukv", 256, 2048) + mat("l_o", D, D)
    plan += mlp("m2") + mat("o_qkv", D, 3 * D) + mat("o_o", D, D) + mlp("m3")
    return plan


def build(nc, dram, out):
    col, n_cols = param_columns()
    plan = weight_plan()
    chunk_index = {c[0]: i for i, c in enumerate(plan)}
    chunk_of = {c[0]: c for c in plan}

    with ExitStack() as ctx:
        def sb(name, shape, dt=F32):
            return ctx.enter_context(nc.sbuf_tensor(name, shape, dt))

        sems = {}

        def sem(name):
            if name not in sems:
                sems[name] = ctx.enter_context(nc.semaphore(name))
            return sems[name]

        wring = sb("wring", [P, SLOTS, SLOT])
        x_res = sb("x_res", [P, TT, D])
        h_t = sb("h_t", [P, KT, T])
        arena = sb("arena", [P, 32 * T])
        g_t = arena[:, :].rearrange("p (f t) -> p f t", t=T)
        q_t = arena[:, 0:2048].rearrange("p (h t) -> p h t", t=T)
        k_t = arena[:, 2048:4096].rearrange("p (h t) -> p h t", t=T)
        v_tok = arena[:, 4096:6144].rearrange("p (t c) -> p t c", t=TT)
        o_tok = arena[:, 6144:8192].rearrange("p (t c) -> p t c", t=TT)
        bias1 = sb("bias1", [P, HEADS * STRIP])
        bias1_v = bias1[:, :].rearrange("p (h c) -> p h c", c=STRIP)
        xn = sb("xn", [P, TT, D])
        o_t = xn[:, :, :].rearrange("p t (a c) -> p (t a) c", c=T)
        extra = sb("extra", [P, 4096])
        gate_row = sb("gate_row", [P, D])
        sc = sb("sc", [P, 2, STRIP])
        ex = sb("ex", [P, ATT, STRIP])
        pt = sb("pt", [P, 2, STRIP])
        tmp = sb("tmp", [P, 2, W])
        acc = sb("acc", [P, 2, W])
        prow = acc[:, 0, 0:2 * P].rearrange("p (i c) -> p i c", i=2)
        params = sb("params", [P, n_cols])
        mod = sb("mod", [P, 112])
        gs = sb("gs", [P, KT])
        gs2 = sb("gs2", [P, KT])
        c_col = sb("c_col", [P, KT])
        c_tmp = sb("c_tmp", [P, KT])
        ident = sb("ident", [P, P])
        flip = sb("flip", [P, P])
        ones = sb("ones", [P, 1])
        mhalf = sb("mhalf", [P, 32])
        mask = sb("mask", [P, STRIP])
        stat = sb("stat", [P, 32])
        nmax = sb("nmax", [P, 16, 2])
        rsum = sb("rsum", [P, 16, 2])
        rinv = sb("rinv", [P, 16, 2])
        lam_in = sb("lam_in", [P, 4, 64])
        lam = sb("lam", [P, 8])
        ss = sb("ss", [P, 64])
        rs = sb("rs", [P, 64])
        fn_row = sb("fn_row", [P, D])
        h_kv = extra[:, 0:2048].rearrange("p (k t) -> p k t", t=T)
        kv_raw = extra[:, 2048:4096].rearrange("p (s g t) -> p s g t", s=2, t=T)
        k_nsa = arena[:, 2048:4096].rearrange("p (w g t) -> p w g t", w=2, t=T)
        v_nsa = arena[:, 4096:5120].rearrange("p (w t c) -> p w t c", w=2, t=TT)
        blocks = arena[:, 5120:5120 + 16 * 4 * NCMP].rearrange("p (l c) -> p l c", l=16)
        p_cmp = extra[:, 0:1024].rearrange("p (t g c) -> p t g c", t=TT, c=P)
        pt_cmp = extra[:, 1024:2048].rearrange("p (t g c) -> p t g c", t=TT, c=P)
        v_cmp = extra[:, 2048:3072].rearrange("p (g c) -> p g c", g=4)
        s_cmp = extra[:, 3072:3584].rearrange("p (t h n) -> p t h n", t=TT, n=16)
        s_cmp2 = extra[:, 3584:4096].rearrange("p (t h n) -> p t h n", t=TT, n=16)
        cmp_hid = sb("cmp_hid", [P, 2, 2, P])
        cmp_w2 = sb("cmp_w2", [P, 2, 2, 64])
        k_cmp = sb("k_cmp", [P, 4, 32])
        pos_cmp = sb("pos_cmp", [P, 2, 16])
        cmask = sb("cmask", [P, 2, TT, NCMP])
        gates = sb("gates", [P, TT, 48])
        gel = tmp[:, :, :].rearrange("p a c -> p (a c)")[:, 0:24 * NCMP].rearrange("p (a i c) -> p a i c", a=3, i=2)
        c_stat = sb("c_stat", [P, TT, HEADS])
        lat = extra[:, 0:TT * 704].rearrange("p (t c) -> p t c", t=TT)
        lat_t = extra[:, 1408:1408 + 5 * T].rearrange("p (k t) -> p k t", t=T)
        qpe_tok = extra[:, 2688:3712].rearrange("p (t h c) -> p t h c", t=TT, c=64)
        lq = bias1[:, 0:TT * 1536].rearrange("p (t h c) -> p t h c", t=TT, c=192)
        lk = xn[:, :, :].rearrange("p t (h c) -> p t h c", c=P)
        qpe_t = bias1[0:64, 3072:5120].rearrange("p (h t) -> p h t", t=T)
        kpe_t = bias1[0:64, 5120:5376]
        bias2 = bias1[:, 0:8 * STRIP].rearrange("p (h c) -> p h c", c=STRIP)
        dist = bias1[:, 3072:3456]
        ge = bias1[:, 3456:4224].rearrange("p (i c) -> p i c", i=2)
        onehot = bias1[:, 4224:4608]
        pos_i = sb("pos_i", [P, T + TT], I32)
        pos_h = sb("pos_h", [P, 2, T + TT], I32)
        pos_f = sb("pos_f", [P, 3, T + TT])
        table2 = sb("table2", [P, BUCKETS * 8])
        inv_freq = sb("inv_freq", [P, 32])
        trig = sb("trig", [P, 2, TT, 32])
        ang = sb("ang", [P, 2, TT, 32])
        pe_gain = sb("pe_gain", [P, 2, 64])
        kpe_n = gate_row[:, 0:128].rearrange("p (t c) -> p t c", t=TT)
        kpe_tok = gate_row[:, 128:256].rearrange("p (t c) -> p t c", t=TT)

        def lq_nope(t, h):
            return lq[:, t, h, 0:P]

        def lk_nope(t, h):
            return lk[:, t, h, :]

        bank = ctx.enter_context(nc.psum_tensor("bank", [P, BANKS, W], F32))
        ps_s = ctx.enter_context(nc.psum_tensor("ps_s", [P, 2, W], F32))
        ps_p = ctx.enter_context(nc.psum_tensor("ps_p", [P, 2, W], F32))

        bias_scratch = nc.dram_tensor("bias_scratch", [HEADS, 384], F32, kind="Internal").ap()

        chunk_in = [sem(f"chunk_in{i}") for i in range(SLOTS)]
        filled = [sem(f"filled{i}") for i in range(BANKS)]
        drained = [sem(f"drained{i}") for i in range(BANKS)]
        matvec_done = sem("matvec_done")
        mod_filled = sem("mod_filled")
        mod_drained = sem("mod_drained")
        x_ready = sem("x_ready")
        ss_ready = sem("ss_ready")
        rstd_ready = sem("rstd_ready")
        chunk_free = {}

        def slot_of(key):
            return chunk_index[key] % SLOTS

        def chunk(key):
            kt, w = chunk_of[key][3:]
            return wring[:, slot_of(key), 0:kt * w].rearrange("p (k n) -> p k n", n=w)

        def chunk_wait(eng, key):
            i = chunk_index[key]
            eng.wait_ge(chunk_in[i % SLOTS], 16 * (i // SLOTS + 1))

        uses = {}
        n_uses = [0]
        owed = [0] * BANKS

        def bank_take(pe, key, readers=1):
            b = n_uses[0] % BANKS
            if owed[b]:
                pe.wait_ge(drained[b], owed[b])
            owed[b] += readers
            uses[key] = (b, n_uses[0] // BANKS + 1, owed[b])
            n_uses[0] += 1
            return b

        def bank_full(eng, key):
            b, n, _ = uses[key]
            eng.wait_ge(filled[b], n)
            return bank[:, b, :]

        def bank_emptied(eng, key):
            b, _, n = uses[key]
            eng.wait_ge(drained[b], n)

        ada_order = [k for k, *_ in plan if k[0].startswith("ada")]

        def ada_index(key):
            return ada_order.index(key)


        block = ctx.enter_context(nc.Block())

        @block.tensor
        def _(pe):
            def mod_columns(key):
                i = ada_index(key)
                pe.wait_ge(matvec_done, i + 1)
                if i >= 2:
                    pe.wait_ge(mod_drained, i - 1)
                for j in range(4):
                    last = nc.tensor.matmul(ps_p[:, i % 2, j:j + 1], acc[:, i % 2, j * P:(j + 1) * P], ones[:, 0:1],
                                            start=True, stop=True)
                last.then_inc(mod_filled, 1)

            def turn(name, readers):
                pe.wait_ge(sem(f"{name}_normed"), TT)
                for g in range(KT // 2):
                    b = bank_take(pe, (name, "turn", g), readers)
                    for i in range(2):
                        for t in range(TT):
                            j = 2 * g + i
                            last = nc.tensor.transpose(bank[:, b, i * T + t * P:i * T + t * P + P],
                                                       xn[:, t, j * P:(j + 1) * P], ident[:, :])
                    last.then_inc(filled[b], 1)

            def turned(name):
                for g in range(KT // 2):
                    bank_emptied(pe, (name, "turn", g))

            def by_feature(key, src, kt, lo=0, hi=W, name=None):
                w = chunk(key)
                chunk_wait(pe, key)
                for g in range((hi - lo) // T):
                    use = (name or key, g) if name else key + (g,)
                    b = bank_take(pe, use)
                    for i in range(2):
                        for k in range(kt):
                            last = nc.tensor.matmul(bank[:, b, i * T:(i + 1) * T],
                                                    w[:, k, lo + g * T + i * P:lo + g * T + (i + 1) * P],
                                                    src[:, k, :], start=(k == 0), stop=(k == kt - 1))
                    last.then_inc(filled[b], 1)
                    chunk_free[key] = (filled[b], uses[use][1])

            def by_token(key, src, kt, readers=1, lo=0, hi=None):
                w = chunk(key)
                hi = hi or chunk_of[key][4]
                chunk_wait(pe, key)
                for t in range(TT):
                    b = bank_take(pe, key + ("tok", t), readers)
                    for k in range(kt):
                        last = nc.tensor.matmul(bank[:, b, 0:hi - lo], src[:, k, t * P:(t + 1) * P], w[:, k, lo:hi],
                                                start=(k == 0), stop=(k == kt - 1))
                    last.then_inc(filled[b], 1)
                    chunk_free[key] = (filled[b], uses[key + ("tok", t)][1])

            def gate_rows(name, first):
                pe.wait_ge(mod_drained, first // 4 + 2)
                for g in range(2):
                    b = bank_take(pe, (name, "gate", g))
                    for j in range(4):
                        c = first + 4 * g + j
                        last = nc.tensor.matmul(bank[:, b, j * P:(j + 1) * P], mod[:, c:c + 1].to_broadcast([P, P]),
                                                ident[:, :], start=True, stop=True)
                    last.then_inc(filled[b], 1)

            def attention(name, units, q_parts, pairs, v, dv):
                outs = units // 2 if pairs else units
                scored, biased = sem(f"{name}_scored"), sem(f"{name}_biased")
                weights, turned_, copied = sem(f"{name}_weights"), sem(f"{name}_turned"), sem(f"{name}_copied")

                def scores(u):
                    if u >= 2:
                        pe.wait_ge(biased, u - 1)
                    parts = q_parts(u)
                    for t in range(TT):
                        lo, n = (0, P) if t == 0 else (P, T)
                        for i, (q, k) in enumerate(parts):
                            last = nc.tensor.matmul(ps_s[:, u % 2, lo:lo + n], q[:, t * P:(t + 1) * P], k[:, 0:n],
                                                    start=(i == 0), stop=(i == len(parts) - 1))
                    last.then_inc(scored, 1)

                def turns(v_):
                    if pairs:
                        pe.wait_ge(weights, v_ + 1)
                    else:
                        pe.wait_ge(sem(f"{name}_exped"), 2 * v_ + 2)
                    if v_ >= 2:
                        pe.wait_ge(copied, v_ - 1)
                    e = (2 * v_ if pairs else v_) % ATT
                    for i in range(3):
                        last = nc.tensor.transpose(ps_p[:, v_ % 2, i * P:(i + 1) * P], ex[:, e, i * P:(i + 1) * P],
                                                   ident[:, :])
                    last.then_inc(turned_, 1)

                def mix(v_):
                    pe.wait_ge(copied, v_ + 1)
                    b = bank_take(pe, (name, "o", v_))
                    vv = v(v_)
                    p_ = pt[:, v_ % 2, :]
                    nc.tensor.matmul(bank[:, b, 0:dv], p_[:, 0:P], vv[:, 0, :], start=True, stop=True)
                    nc.tensor.matmul(bank[:, b, dv:2 * dv], p_[:, P:2 * P], vv[:, 0, :], start=True, stop=False)
                    nc.tensor.matmul(bank[:, b, dv:2 * dv], p_[:, 2 * P:3 * P], vv[:, 1, :], start=False,
                                     stop=True).then_inc(filled[b], 1)

                if pairs:
                    for h in range(outs + 2):
                        if h < outs:
                            scores(2 * h)
                            scores(2 * h + 1)
                        if 1 <= h <= outs:
                            turns(h - 1)
                        if h >= 2:
                            mix(h - 2)
                else:
                    for u in range(units + 2):
                        if u < units:
                            scores(u)
                        if 1 <= u <= units:
                            turns(u - 1)
                        if u >= 2:
                            mix(u - 2)

            def turn_o(name):
                if name == "diff":
                    pe.wait_ge(sem("diff_o_ready"), TT)
                else:
                    bank_emptied(pe, ("win", "o", HEADS - 1) if name == "nsa" else (name, "o", 7))
                for g in range(KT // 2):
                    b = bank_take(pe, (name, "turn_o", g), 1)
                    for i in range(2):
                        for t in range(TT):
                            j = 2 * g + i
                            last = nc.tensor.transpose(bank[:, b, i * T + t * P:i * T + t * P + P],
                                                       o_tok[:, t, j * P:(j + 1) * P], ident[:, :])
                    last.then_inc(filled[b], 1)
                for g in range(KT // 2):
                    bank_emptied(pe, (name, "turn_o", g))

            def mlp(tag, ada=()):
                ada = list(ada)
                for c in range(FF // W):
                    by_feature((f"{tag}_w1", c), h_t, KT)
                    if ada:
                        mod_columns(ada.pop(0))
                pe.wait_ge(sem(f"{tag}_squared"), 2 * FF // W)
                for n in range(2):
                    bs = []
                    for t in range(TT):
                        bs.append(bank_take(pe, (tag, "y", n, t)))
                    for q in range(4):
                        key = (f"{tag}_w2", n, q)
                        w = chunk(key)
                        chunk_wait(pe, key)
                        for t in range(TT):
                            for k in range(KT):
                                kk = q * KT + k
                                last = nc.tensor.matmul(bank[:, bs[t], :], g_t[:, kk, t * P:(t + 1) * P], w[:, k, :],
                                                        start=(kk == 0), stop=(kk == 4 * KT - 1))
                            if q == 3:
                                last.then_inc(filled[bs[t]], 1)
                        if q < 3:
                            last.then_inc(sem("w2_read"), 1)
                            n_w2[0] += 1
                            chunk_free[key] = (sem("w2_read"), n_w2[0])
                        else:
                            chunk_free[key] = (filled[bs[1]], uses[(tag, "y", n, 1)][1])
                        if ada:
                            mod_columns(ada.pop(0))

            n_w2 = [0]

            pe.wait_ge(sem("const_in"), 16 * 5)
            pe.wait_ge(sem("param_in"), 16 * len(PARAM_ROWS))
            b = bank_take(pe, "params")
            nc.tensor.transpose(bank[:, b, 0:P], prow[:, 0, :], ident[:, :])
            nc.tensor.transpose(bank[:, b, P:n_cols], prow[0:n_cols - P, 1, :],
                                ident[0:n_cols - P, 0:n_cols - P]).then_inc(filled[b], 1)
            pe.wait_ge(sem("table_in"), 32)
            b = bank_take(pe, "bias_rows")
            nc.tensor.matmul(bank[0:HEADS, b, 0:384], sc[0:BUCKETS, 0, 0:HEADS], sc[0:BUCKETS, 1, :], start=True,
                             stop=True).then_inc(filled[b], 1)
            for c in range(4):
                mod_columns(("ada0", c))
            pe.wait_ge(sem("bias_back"), 32)
            for h in range(HEADS):
                b = bank_take(pe, ("bias", h))
                nc.tensor.matmul(bank[:, b, 0:STRIP], flip[:, :], bias1_v[:, h, :], start=True,
                                 stop=True).then_inc(filled[b], 1)
            turn("a0", 2)
            turned("a0")
            extra_ada = [("ada0", c) for c in range(4, 12)]
            for c in range(6):
                if c < 4:
                    by_feature(("a_in", c), h_t, KT)
                else:
                    by_token(("a_in", c), h_t, KT)
                mod_columns(extra_ada.pop(0))
            while extra_ada:
                mod_columns(extra_ada.pop(0))
            gate_rows("a0", 16)
            for t in range(TT):
                for c in (4, 5):
                    bank_emptied(pe, ("a_in", c, "tok", t))

            def diff_q(u):
                h, m = u // 2, u % 2
                return [(q_t[64 * m:64 * m + 64, h, :], k_t[64 * m:64 * m + 64, h, :])]

            attention("diff", 16, diff_q, True, lambda v_: v_tok[:, :, v_ * P:(v_ + 1) * P], P)
            turn_o("diff")
            for c in range(2):
                by_token(("a_out", c), o_t, KT)
            turn("m0", 2)
            turned("m0")
            gate_rows("m0", 40)
            mlp("m0", ada_order[12:])

            turn("kv", 4)
            turned("kv")
            by_feature(("w_kv", 0), h_kv, KT)
            by_feature(("w_kv", 1), h_kv, KT, 0, 256, name="k_slc")
            by_token(("w_kv", 1), h_kv, KT, 1, 256, 512)
            by_feature(("w_kv", 2), h_kv, KT, 0, 256, name="k_win")
            by_token(("w_kv", 2), h_kv, KT, 1, 256, 512)
            for s in range(2):
                chunk_wait(pe, ("cmp_w1", s))
                pe.wait_ge(sem("blocks_ready"), s + 1)
                w = chunk(("cmp_w1", s))
                b = bank_take(pe, ("cmp_hidden", s))
                for ht in range(2):
                    for l in range(16):
                        last = nc.tensor.matmul(bank[:, b, ht * 64:ht * 64 + 4 * NCMP], w[:, l, ht * P:(ht + 1) * P],
                                                blocks[:, l, :], start=(l == 0), stop=(l == 15))
                last.then_inc(filled[b], 1)
                chunk_free[("cmp_w1", s)] = (filled[b], uses[("cmp_hidden", s)][1])
            pe.wait_ge(sem("cmp_act"), 2)
            pe.wait_ge(sem("cmp_w2_in"), 32)
            b = bank_take(pe, "k_cmp")
            for ht in range(2):
                for rep in range(2):
                    last = nc.tensor.matmul(bank[64 * rep:64 * rep + 64, b, 0:P], cmp_w2[:, 0, ht, :],
                                            cmp_hid[:, 0, ht, :], start=(ht == 0), stop=(ht == 1),
                                            skip_group_check=True)
            last.then_inc(filled[b], 1)
            b = bank_take(pe, "v_cmp")
            for g in range(4):
                for ht in range(2):
                    hid = cmp_hid[:, 1, ht, g * 32:(g + 1) * 32]
                    for r in range(4):
                        last = nc.tensor.matmul(bank[32 * r:32 * r + 32, b, g * 64:(g + 1) * 64], hid,
                                                cmp_w2[:, 1, ht, :], start=(ht == 0), stop=(ht == 1),
                                                skip_group_check=True)
            last.then_inc(filled[b], 1)

            for c in range(2):
                by_feature(("b_in", c), h_t, KT)
            by_token(("b_in", 2), h_t, KT)
            gate_rows("n1", 64 + 16)
            for c in range(2):
                for g in range(2):
                    bank_emptied(pe, ("b_in", c, g))
            bank_emptied(pe, "k_cmp")
            for m in range(2):
                b = bank_take(pe, ("cmp_scores", m), TT)
                for t in range(TT):
                    for j in range(HEADS // 2):
                        at = (t * (HEADS // 2) + j) * 16
                        last = nc.tensor.matmul(bank[:, b, at:at + NCMP],
                                                q_t[64 * m:64 * m + 64, j, t * P:(t + 1) * P],
                                                k_cmp[64 * m:64 * m + 64, j // 2, 0:NCMP], start=True, stop=True)
                last.then_inc(filled[b], 1)
            pe.wait_ge(sem("cmp_weights"), 1)
            for t in range(TT):
                b = bank_take(pe, ("cmp_turn", t))
                for g in range(4):
                    last = nc.tensor.transpose(bank[:, b, g * P:(g + 1) * P], p_cmp[:, t, g, :], ident[:, :])
                last.then_inc(filled[b], 1)
            bank_emptied(pe, "v_cmp")
            pe.wait_ge(sem("v_cmp_ready"), 1)
            for t in range(TT):
                bank_emptied(pe, ("cmp_turn", t))
                for half in range(2):
                    b = bank_take(pe, ("cmp_o", t, half))
                    for g in range(2):
                        last = nc.tensor.matmul(bank[:, b, g * T:(g + 1) * T], pt_cmp[:, t, 2 * half + g, :],
                                                v_cmp[:, 2 * half + g, :], start=True, stop=True)
                    last.then_inc(filled[b], 1)

            def nsa_q(which):
                def parts(u):
                    lo = 64 * (u % 2)
                    return [(q_t[lo:lo + 64, u // 2, :], k_nsa[lo:lo + 64, which, u // 4, :])]
                return parts

            for which, name in enumerate(("slc", "win")):
                attention(name, HEADS, nsa_q(which), False,
                          lambda v_, w_=which: v_nsa[:, w_, :, (v_ // 4) * 64:(v_ // 4) * 64 + 64], 64)
            turn_o("nsa")
            for c in range(2):
                by_token(("b_out", c), o_t, KT)
            turn("m1", 2)
            turned("m1")
            gate_rows("m1", 64 + 40)
            mlp("m1")

            turn("l", 2)
            turned("l")
            for c in range(2):
                by_token(("l_in", c), h_t, KT)
            pe.wait_ge(sem("latent_normed"), 1)
            for g, (j0, n) in enumerate(((0, 2), (2, 2), (4, 1))):
                b = bank_take(pe, ("latent_turn", g))
                for i in range(n):
                    for t in range(TT):
                        last = nc.tensor.transpose(bank[:, b, i * T + t * P:i * T + t * P + P],
                                                   lat[:, t, (j0 + i) * P:(j0 + i + 1) * P], ident[:, :])
                last.then_inc(filled[b], 1)
            b = bank_take(pe, "kpe_turn")
            pe.wait_ge(sem("kpe_ready"), 1)
            for t in range(TT):
                last = nc.tensor.transpose(bank[0:64, b, t * P:(t + 1) * P], kpe_tok[:, t, :], ident[:, :])
            last.then_inc(filled[b], 1)
            for g in range(3):
                bank_emptied(pe, ("latent_turn", g))
            for c in range(3):
                by_token(("l_uq", c), lat_t, 3)
            for c in range(4):
                by_token(("l_ukv", c), lat_t[:, 3:5, :], 2, readers=2)
            for what, n_h, ready in (("q", 8, "lq_normed"), ("k", 8, "lk_normed")):
                pe.wait_ge(sem(ready), 1)
                src = lq_nope if what == "q" else lk_nope
                for g in range(4):
                    b = bank_take(pe, ("l_turn", what, g))
                    for i in range(2):
                        for t in range(TT):
                            last = nc.tensor.transpose(bank[:, b, i * T + t * P:i * T + t * P + P],
                                                       src(t, 2 * g + i), ident[:, :])
                    last.then_inc(filled[b], 1)
            pe.wait_ge(sem("qpe_ready"), 1)
            for g in range(4):
                b = bank_take(pe, ("qpe_turn", g))
                for i in range(2):
                    for t in range(TT):
                        last = nc.tensor.transpose(bank[0:64, b, i * T + t * P:i * T + t * P + P],
                                                   qpe_tok[:, t, 2 * g + i, :], ident[:, :])
                last.then_inc(filled[b], 1)
            for what in "qk":
                for g in range(4):
                    bank_emptied(pe, ("l_turn", what, g))
            for g in range(4):
                bank_emptied(pe, ("qpe_turn", g))
            bank_emptied(pe, "kpe_turn")
            for c in range(4):
                for t in range(TT):
                    bank_emptied(pe, ("l_ukv", c, "tok", t))
            attention("mla", 8, lambda u: [(q_t[:, u, :], k_t[:, u, :]), (qpe_t[:, u, :], kpe_t[:, :])], False,
                      lambda v_: v_tok[:, :, v_ * P:(v_ + 1) * P], P)
            turn_o("mla")
            for c in range(2):
                by_token(("l_o", c), o_t, KT)
            turn("m2", 2)
            turned("m2")
            mlp("m2")

            turn("o", 2)
            turned("o")
            for c in range(4):
                by_token(("o_qkv", c), h_t, KT, readers=2)
            for c in range(4, 6):
                by_token(("o_qkv", c), h_t, KT)
            for what in "qk":
                pe.wait_ge(sem(f"o{what}_normed"), 1)
                src = xn if what == "q" else o_tok
                for g in range(4):
                    b = bank_take(pe, ("o_turn", what, g))
                    for i in range(2):
                        for t in range(TT):
                            h = 2 * g + i
                            last = nc.tensor.transpose(bank[:, b, i * T + t * P:i * T + t * P + P],
                                                       src[:, t, h * P:(h + 1) * P], ident[:, :])
                    last.then_inc(filled[b], 1)
            for what in "qk":
                for g in range(4):
                    bank_emptied(pe, ("o_turn", what, g))
            for c in (4, 5):
                for t in range(TT):
                    bank_emptied(pe, ("o_qkv", c, "tok", t))
            attention("moba", 8, lambda u: [(q_t[:, u, :], k_t[:, u, :])], False,
                      lambda v_: v_tok[:, :, v_ * P:(v_ + 1) * P], P)
            turn_o("moba")
            for c in range(2):
                by_token(("o_o", c), o_t, KT)
            turn("m3", 2)
            turned("m3")
            mlp("m3")

        rstd_calls = []

        @block.vector
        def _(dve):
            done = sem("dve_done")
            n_done = [0]

            def link(ins):
                ins.then_inc(done, 1)
                n_done[0] += 1

            def settle():
                dve.wait_ge(done, n_done[0])

            v = nc.vector

            def signal(name):
                settle()
                v.memset(stat[:, 0:1], 0.0).then_inc(sem(name), 1)

            def matvec(key):
                i = ada_index(key)
                w = chunk(key)
                chunk_wait(dve, key)
                if i >= 2:
                    dve.wait_ge(mod_filled, i - 1)
                a = acc[:, i % 2, :]
                link(v.tensor_scalar(a, w[:, 0, :], c_col[:, 0:1], None, ALU.mult))
                for k in range(1, KT):
                    settle()
                    ins = v.scalar_tensor_tensor(a, w[:, k, :], c_col[:, k:k + 1], a, ALU.mult, ALU.add)
                    if k < KT - 1:
                        link(ins)
                ins.then_inc(matvec_done, 1)
                chunk_free[key] = (matvec_done, i + 1)

            def mod_drain(key):
                i = ada_index(key)
                name, c = key
                first = col[{"ada0": "ada_b0", "ada1": "ada_b1", "adakv": "kv_b"}[name]]
                dve.wait_ge(mod_filled, i + 1)
                v.tensor_tensor(mod[:, 4 * i:4 * i + 4], ps_p[:, i % 2, 0:4], params[:, first + 4 * c:first + 4 * c + 4],
                                ALU.add).then_inc(mod_drained, 1)

            def rstd(width, n):
                k = len(rstd_calls)
                rstd_calls.append((width, n))
                return (k % 2) * 32

            def rstd_wait():
                dve.wait_ge(rstd_ready, len(rstd_calls))

            def gain(dst, name, scale_col):
                dve.wait_ge(mod_drained, scale_col // 4 + 2)
                link(v.tensor_scalar(dst[:, :], mod[:, scale_col:scale_col + KT], 1.0, None, ALU.add))
                settle()
                v.tensor_tensor(dst[:, :], dst[:, :], params[:, col[name]:col[name] + KT],
                                ALU.mult).then_inc(sem("gains_ready"), 1)

            def norm(name, outs, gains):
                at = rstd(TT, D)
                rstd_wait()
                for t in range(TT):
                    v.tensor_scalar(xn[:, t, :], x_res[:, t, :], rs[:, at + t:at + t + 1], None,
                                    ALU.mult).then_inc(sem(f"{name}_normed"), 1)
                if gains:
                    dve.wait_ge(sem("gains_ready"), gains)
                for g in range(0, KT // 2, 2):
                    src = bank_full(dve, (name, "turn", g))
                    b = uses[(name, "turn", g)][0]
                    for dst, gn, sh in outs:
                        for i in range(2):
                            j = 2 * g + i
                            part = src[:, i * T:(i + 1) * T]
                            if sh is None:
                                ins = v.tensor_scalar(dst[:, j, :], part, gn[:, j:j + 1], None, ALU.mult)
                            else:
                                ins = v.tensor_scalar(dst[:, j, :], part, gn[:, j:j + 1], sh[:, j:j + 1],
                                                      ALU.mult, ALU.add)
                            ins.then_inc(drained[b], 1)

            def residual(key, t, n, gated):
                src = bank_full(dve, key)
                b = uses[key][0]
                x_ = x_res[:, t, n * W:(n + 1) * W]
                if gated:
                    v.tensor_tensor(tmp[:, t, :], src, gate_row[:, n * W:(n + 1) * W], ALU.mult).then_inc(drained[b], 1)
                    bank_emptied(dve, key)
                    v.tensor_tensor(x_, tmp[:, t, :], x_, ALU.add).then_inc(x_ready, 1)
                else:
                    v.tensor_tensor(x_, src, x_, ALU.add).then_inc(drained[b], 1)

            def gate(name):
                for g in range(2):
                    src = bank_full(dve, (name, "gate", g))
                    v.tensor_copy(gate_row[:, g * W:(g + 1) * W], src).then_inc(drained[uses[(name, "gate", g)][0]], 1)

            def gate_use(name):
                for g in range(2):
                    bank_emptied(dve, (name, "gate", g))

            def attention(name, units, bias, scale, pairs, output):
                scored, biased, maxed = sem(f"{name}_scored"), sem(f"{name}_biased"), sem(f"{name}_maxed")
                exped, weights = sem(f"{name}_exped"), sem(f"{name}_weights")
                outs = units // 2 if pairs else units

                def scores(u):
                    dve.wait_ge(scored, u + 1)
                    if u >= 2:
                        dve.wait_ge(exped, 2 * u - 2)
                    s = sc[:, u % 2, :]
                    v.scalar_tensor_tensor(s, ps_s[:, u % 2, 0:STRIP], scale, bias(u), ALU.mult,
                                           ALU.add).then_inc(biased, 1)
                    dve.wait_ge(biased, u + 1)
                    v.tensor_reduce(nmax[:, u, 0:1], s[:, 0:P], AX, ALU.max, negate=True).then_inc(maxed, 1)
                    v.tensor_reduce(nmax[:, u, 1:2], s[:, P:STRIP], AX, ALU.max, negate=True).then_inc(maxed, 1)

                def combine(h):
                    dve.wait_ge(exped, 4 * h + 4)
                    link(v.reciprocal(rinv[:, 2 * h:2 * h + 2, :], rsum[:, 2 * h:2 * h + 2, :]))
                    settle()
                    link(v.scalar_tensor_tensor(rinv[:, 2 * h + 1, :], rinv[:, 2 * h + 1, :], lam[:, 3:4],
                                                rsum[:, 2 * h, :], ALU.mult, ALU.mult))
                    settle()
                    a, b_ = ex[:, (2 * h) % ATT, :], ex[:, (2 * h + 1) % ATT, :]
                    v.scalar_tensor_tensor(a[:, 0:P], b_[:, 0:P], rinv[:, 2 * h + 1, 0:1], a[:, 0:P], ALU.mult, ALU.add)
                    v.scalar_tensor_tensor(a[:, P:STRIP], b_[:, P:STRIP], rinv[:, 2 * h + 1, 1:2], a[:, P:STRIP],
                                           ALU.mult, ALU.add).then_inc(weights, 1)

                if pairs:
                    for h in range(outs + 2):
                        if h < outs:
                            scores(2 * h)
                            scores(2 * h + 1)
                        if 1 <= h <= outs:
                            combine(h - 1)
                        if h >= 2:
                            output(h - 2)
                else:
                    for u in range(units + 2):
                        if u < units:
                            scores(u)
                        if u >= 2:
                            output(u - 2)

            def plain_output(name, outs, pairs):
                def output(h):
                    src = bank_full(dve, (name, "o", h))
                    b = uses[(name, "o", h)][0]
                    r = 2 * h if pairs else h
                    if not pairs:
                        link(v.reciprocal(rinv[:, r, :], rsum[:, r, :]))
                        settle()
                    for t in range(TT):
                        ins = v.tensor_scalar(o_tok[:, t, h * P:(h + 1) * P], src[:, t * P:(t + 1) * P],
                                              rinv[:, r, t:t + 1], None, ALU.mult)
                        if t == 0:
                            link(ins)
                    ins.then_inc(drained[b], 1)
                return output

            def head_scale(dst, src, at, t, heads, width):
                return v.tensor_tensor(dst, src, rs[:, at + t * heads:at + (t + 1) * heads]
                                       .unsqueeze(2).to_broadcast([P, heads, width]), ALU.mult)

            v.memset(ones[:, :], 1.0).then_inc(sem("ones_set"), 1)
            v.memset(cmp_hid[:, :, :, :], 0.0)
            src = bank_full(dve, "params")
            v.tensor_copy(params[:, :], src[:, 0:n_cols]).then_inc(drained[uses["params"][0]], 1)
            bank_emptied(dve, "params")
            dve.wait_ge(sem("silu_exp"), 1)
            link(v.tensor_scalar(c_tmp[:, :], c_tmp[:, :], 1.0, None, ALU.add))
            settle()
            link(v.reciprocal(c_tmp[:, :], c_tmp[:, :]))
            settle()
            link(v.tensor_tensor(c_col[:, :], c_tmp[:, :], params[:, 0:KT], ALU.mult))
            src = bank_full(dve, "bias_rows")
            dve.wait_ge(sem("const_in"), 16 * 5)
            v.tensor_tensor(ex[0:HEADS, 1, :], src[0:HEADS, 0:384], ex[0:HEADS, 0, :],
                            ALU.add).then_inc(drained[uses["bias_rows"][0]], 1)
            dve.wait_ge(sem("lam_in"), 16)
            link(v.tensor_tensor(lam_in[:, 0, :], lam_in[:, 0, :], lam_in[:, 1, :], ALU.mult))
            link(v.tensor_tensor(lam_in[:, 2, :], lam_in[:, 2, :], lam_in[:, 3, :], ALU.mult))
            settle()
            v.tensor_reduce(lam[:, 0:1], lam_in[:, 0, :], AX, ALU.add)
            v.tensor_reduce(lam[:, 1:2], lam_in[:, 2, :], AX, ALU.add).then_inc(sem("lam_dots"), 1)
            for c in range(4):
                settle()
                matvec(("ada0", c))
                if c:
                    mod_drain(("ada0", c - 1))
            mod_drain(("ada0", 3))
            dve.wait_ge(sem("lam_exp"), 1)
            link(v.tensor_tensor(lam[:, 2:3], lam[:, 5:6], lam[:, 4:5], ALU.subtract))
            settle()
            link(v.tensor_scalar(lam[:, 3:4], lam[:, 2:3], LAM_INIT, None, ALU.subtract))
            gain(gs, "an0", 8)
            norm("a0", [(h_t, gs, mod[:, 0:8])], 1)
            for c in range(4, 12):
                matvec(("ada0", c))
                if c > 4:
                    mod_drain(("ada0", c - 1))
            mod_drain(("ada0", 11))
            dve.wait_ge(mod_drained, 12)
            gate("a0")
            attention("diff", 16, lambda u: bias1_v[:, u, :], 0.125, True, plain_output("diff", 8, True))
            at = rstd(16, P)
            for t in range(TT):
                dve.wait_ge(sem("diff_squares"), t + 1)
                ins = v.tensor_reduce(ss[:, at + 8 * t:at + 8 * t + 8],
                                      xn[:, t, :].rearrange("p (h c) -> p h c", c=P), AX, ALU.add)
            ins.then_inc(ss_ready, 1)
            rstd_wait()
            for t in range(TT):
                o_ = o_tok[:, t, :].rearrange("p (h c) -> p h c", c=P)
                head_scale(o_, o_, at, t, 8, P).then_inc(sem("diff_o_ready"), 1)
            gate_use("a0")
            for n in range(2):
                for t in range(TT):
                    residual(("a_out", n, "tok", t), t, n, True)
            gain(gs, "mn0", 32)
            norm("m0", [(h_t, gs, mod[:, 24:32])], 2)
            gate("m0")
            gate_use("m0")
            for i in range(12, 28):
                matvec(ada_order[i])
                if i > 12:
                    mod_drain(ada_order[i - 1])
            mod_drain(ada_order[27])
            for n in range(2):
                for t in range(TT):
                    residual(("m0", "y", n, t), t, n, True)

            gain(gs, "an1", 64 + 8)
            gain(gs2, "kvn", 48 + 8)
            norm("kv", [(h_t, gs, mod[:, 64:72]), (h_kv, gs2, mod[:, 48:56])], 4)
            for s in range(2):
                src = bank_full(dve, ("w_kv", 0, s))
                for par in range(2):
                    for i in range(2):
                        for g in range(2):
                            d_ = kv_raw[64 * par:64 * par + 64, s, 2 * i + g, 0:T - par]
                            ins = v.tensor_copy(d_, src[64 * g:64 * g + 64, i * T + par:(i + 1) * T])
                            if (par, i, g) != (1, 1, 1):
                                link(ins)
                ins.then_inc(drained[uses[("w_kv", 0, s)][0]], 1)
                settle()
                bank_emptied(dve, ("w_kv", 0, s))
                dve.wait_ge(sem("pos_in"), 64)
                if s:
                    bank_full(dve, ("cmp_hidden", 0))
                for l in range(16):
                    b_ = blocks[:, l, :].rearrange("p (g n) -> p g n", g=4)
                    ins = v.tensor_scalar(b_, kv_raw[:, s, :, 2 * l:2 * l + 16 * (NCMP - 1) + 1:16],
                                          pos_cmp[:, s, l:l + 1], None, ALU.add)
                ins.then_inc(sem("blocks_ready"), 1)
            for s in range(2):
                src = bank_full(dve, ("cmp_hidden", s))
                if s:
                    settle()
                x0 = gel[:, 0, :, :]
                v.tensor_copy(x0, src[:, 0:128].rearrange("p (i c) -> p i c", i=2)[:, :, 0:4 * NCMP]).then_inc(
                    drained[uses[("cmp_hidden", s)][0]], 1)
                bank_emptied(dve, ("cmp_hidden", s))
                link(v.tensor_scalar(gel[:, 2, :, :], x0, -9.0, None, ALU.max))
                settle()
                link(v.tensor_tensor(gel[:, 1, :, :], gel[:, 2, :, :], gel[:, 2, :, :], ALU.mult))
                settle()
                link(v.tensor_scalar(gel[:, 1, :, :], gel[:, 1, :, :], 0.044715, 1.0, ALU.mult, ALU.add))
                settle()
                v.tensor_tensor(gel[:, 1, :, :], gel[:, 1, :, :], gel[:, 2, :, :], ALU.mult).then_inc(sem("gelu_arg"), 1)
                dve.wait_ge(sem("gelu_exp"), s + 1)
                link(v.tensor_scalar(gel[:, 2, :, :], gel[:, 2, :, :], 1.0, None, ALU.add))
                settle()
                link(v.reciprocal(gel[:, 2, :, :], gel[:, 2, :, :]))
                settle()
                link(v.tensor_tensor(cmp_hid[:, s, :, :].rearrange("p i (g n) -> p i g n", g=4)[:, :, :, 0:NCMP],
                                     x0.rearrange("p i (g n) -> p i g n", g=4),
                                     gel[:, 2, :, :].rearrange("p i (g n) -> p i g n", g=4), ALU.mult))
                settle()
                signal("cmp_act")
            link(v.memset(v_cmp[:, :, :], 0.0))
            link(v.memset(p_cmp[:, :, :, :], 0.0))
            src = bank_full(dve, "k_cmp")
            v.tensor_copy(k_cmp[:, :, :].rearrange("p g n -> p (g n)"), src[:, 0:P]).then_inc(
                drained[uses["k_cmp"][0]], 1)
            src = bank_full(dve, "v_cmp")
            settle()
            for r in range(4):
                rows = slice(32 * r, 32 * r + 32)
                ins = v.tensor_copy(v_cmp[rows, :, 64 * r:64 * r + 64], src[rows, 0:T].rearrange("p (g c) -> p g c", g=4))
                if r < 3:
                    link(ins)
            ins.then_inc(drained[uses["v_cmp"][0]], 1)
            bank_emptied(dve, "v_cmp")
            settle()
            signal("v_cmp_ready")
            dve.wait_ge(mod_drained, 28)
            for t in range(TT):
                bank_emptied(dve, ("b_in", 2, "tok", t))
            link(v.tensor_scalar(gates[:, :, :], gates[:, :, :], 1.0, None, ALU.add))
            settle()
            link(v.reciprocal(gates[:, :, :], gates[:, :, :]))
            gate("n1")
            gates_v = gates[:, :, :].rearrange("p t (h c) -> p t h c", c=3)
            for m in range(2):
                src = bank_full(dve, ("cmp_scores", m))[:, 0:256].rearrange("p (t j n) -> p t j n", t=TT, n=16)
                for t in range(TT):
                    v.scalar_tensor_tensor(s_cmp[:, t, m:HEADS:2, 0:NCMP], src[:, t, :, 0:NCMP], 0.125,
                                           cmask[:, 0, t, :].unsqueeze(1).to_broadcast([P, HEADS // 2, NCMP]),
                                           ALU.mult, ALU.add).then_inc(drained[uses[("cmp_scores", m)][0]], 1)
            for m in range(2):
                bank_emptied(dve, ("cmp_scores", m))
            s_ = s_cmp[:, :, :, 0:NCMP]
            e_ = s_cmp2[:, :, :, 0:NCMP]
            wide = [P, TT, HEADS, NCMP]
            link(v.tensor_reduce(c_stat[:, :, :], s_, AX, ALU.max))
            settle()
            v.tensor_tensor(s_, s_, c_stat[:, :, :].unsqueeze(3).to_broadcast(wide), ALU.subtract).then_inc(
                sem("cmp_centred"), 1)
            dve.wait_ge(sem("cmp_exped"), 1)
            link(v.tensor_reduce(c_stat[:, :, :], e_, AX, ALU.add))
            settle()
            link(v.reciprocal(c_stat[:, :, :], c_stat[:, :, :]))
            settle()
            for t in range(TT):
                link(v.tensor_tensor(e_[:, t], e_[:, t], cmask[:, 1, t, :].unsqueeze(1).to_broadcast(
                    [P, HEADS, NCMP]), ALU.mult))
            link(v.tensor_tensor(c_stat[:, :, :], c_stat[:, :, :], gates_v[:, :, :, 0], ALU.mult))
            settle()
            for t in range(TT):
                link(v.tensor_tensor(p_cmp[:, t, :, :].rearrange("p g (r n) -> p (g r) n", n=32)[:, :, 0:NCMP],
                                     e_[:, t], c_stat[:, t, :].unsqueeze(2).to_broadcast([P, HEADS, NCMP]), ALU.mult))
            settle()
            signal("cmp_weights")
            for t in range(TT):
                for half in range(2):
                    src = bank_full(dve, ("cmp_o", t, half))
                    v.tensor_copy(o_tok[:, t, half * W:(half + 1) * W], src).then_inc(
                        drained[uses[("cmp_o", t, half)][0]], 1)
            for t in range(TT):
                for half in range(2):
                    bank_emptied(dve, ("cmp_o", t, half))

            def nsa_output(name, c):
                def output(h):
                    src = bank_full(dve, (name, "o", h))
                    b = uses[(name, "o", h)][0]
                    link(v.reciprocal(rinv[:, h, :], rsum[:, h, :]))
                    settle()
                    link(v.tensor_tensor(rinv[:, h, :], rinv[:, h, :], gates_v[:, :, h, c], ALU.mult))
                    settle()
                    for t in range(TT):
                        o_ = o_tok[:, t, h * 64:(h + 1) * 64]
                        ins = v.scalar_tensor_tensor(o_, src[:, t * 64:(t + 1) * 64], rinv[:, h, t:t + 1], o_, ALU.mult,
                                                     ALU.add)
                        if t == 0:
                            link(ins)
                    ins.then_inc(drained[b], 1)
                return output

            for c, name in ((1, "slc"), (2, "win")):
                attention(name, HEADS, lambda u: bias1_v[:, u, :], 0.125, False, nsa_output(name, c))
                bank_emptied(dve, (name, "o", HEADS - 1))
                settle()
            gate_use("n1")
            for n in range(2):
                for t in range(TT):
                    residual(("b_out", n, "tok", t), t, n, True)
            gain(gs, "mn1", 64 + 32)
            norm("m1", [(h_t, gs, mod[:, 64 + 24:64 + 32])], 5)
            gate("m1")
            gate_use("m1")
            dve.wait_ge(sem("pos_in"), 64)
            dve.wait_ge(sem("late_in"), 64)
            dve.wait_ge(sem("cmp_w2_in"), 32)
            link(v.tensor_scalar(pos_h[:, 0, :], pos_i[:, :], 12, None, ALU.arith_shift_right))
            link(v.tensor_scalar(pos_h[:, 1, :], pos_i[:, :], 4095, None, ALU.bitwise_and))
            link(v.tensor_copy(pos_f[:, 2, :], pos_i[:, :]))
            settle()
            link(v.tensor_copy(pos_f[:, 0:2, :], pos_h[:, :, :]))
            a_, n_ = ang[:, 0, :, :], ang[:, 1, :, :]
            for t in range(TT):
                link(v.tensor_scalar(a_[:, t, :], inv_freq[:, :], pos_f[:, 2, T + t:T + t + 1], None, ALU.mult))
            magic = 1.5 * 2.0 ** 23
            for period in (TWO_PI * 4096, TWO_PI):
                settle()
                link(v.tensor_scalar(n_, a_, 1.0 / period, magic, ALU.mult, ALU.add))
                settle()
                link(v.tensor_scalar(n_, n_, magic, None, ALU.subtract))
                for part in pow2_split(period, 11, 4):
                    settle()
                    link(v.scalar_tensor_tensor(a_, n_, -part, a_, ALU.mult, ALU.add))
            settle()
            v.tensor_scalar(a_, a_, 3.1415925, -3.1415925, ALU.min, ALU.max).then_inc(sem("angles_ready"), 1)
            for n in range(2):
                for t in range(TT):
                    residual(("m1", "y", n, t), t, n, True)
            at = rstd(TT, D)
            rstd_wait()
            for t in range(TT):
                v.scalar_tensor_tensor(x_res[:, t, :], x_res[:, t, :], rs[:, at + t:at + t + 1], fn_row[:, :], ALU.mult,
                                       ALU.mult).then_inc(x_ready, 1)

            norm("l", [(h_t, params[:, col["an2_0"]:col["an2_0"] + KT], None)], 0)
            segs = ((0, 384), (384, 640), (640, 704))
            ats = []
            for i, (a, b_) in enumerate(segs):
                ats.append(rstd(TT, b_ - a))
                if i == 2:
                    dve.wait_ge(rstd_ready, len(rstd_calls) - 2)
                sq = arena[:, 0:TT * 704].rearrange("p (t c) -> p t c", t=TT)
                if i == 0:
                    dve.wait_ge(sem("lat_squares"), TT)
                if i == 2:
                    for t in range(TT):
                        link(v.tensor_scalar(lat[:, t, 0:384], lat[:, t, 0:384], rs[:, ats[0] + t:ats[0] + t + 1], None,
                                             ALU.mult))
                    settle()
                v.tensor_reduce(ss[:, ats[i]:ats[i] + TT], sq[:, :, a:b_], AX, ALU.add).then_inc(ss_ready, 1)
            rstd_wait()
            for t in range(TT):
                link(v.tensor_scalar(lat[:, t, 384:640], lat[:, t, 384:640], rs[:, ats[1] + t:ats[1] + t + 1], None,
                                     ALU.mult))
                link(v.scalar_tensor_tensor(kpe_n[:, t, :], lat[:, t, 640:704], rs[:, ats[2] + t:ats[2] + t + 1],
                                            pe_gain[:, 1, :], ALU.mult, ALU.mult))
            settle()
            signal("latent_normed")
            dve.wait_ge(sem("trig_ready"), 2)
            cos, sin = trig[:, 0, :, :], trig[:, 1, :, :]

            def rope(dst, src, shape, c_, s_, scratch):
                x1, x2 = src[..., 0:32], src[..., 32:64]
                for a, b_, op, to in ((x1, x2, ALU.subtract, 0), (x2, x1, ALU.add, 32)):
                    settle()
                    link(v.tensor_tensor(dst[..., to:to + 32], a, c_, ALU.mult))
                    link(v.tensor_tensor(scratch, b_, s_, ALU.mult))
                    settle()
                    link(v.tensor_tensor(dst[..., to:to + 32], dst[..., to:to + 32], scratch, op))
                settle()

            rope(kpe_tok[:, :, :], kpe_n[:, :, :], None, cos, sin, ang[:, 1, :, :])
            signal("kpe_ready")
            sq = arena[:, 0:3072].rearrange("p (t h c) -> p t h c", t=TT, c=192)
            dve.wait_ge(sem("lq_squares"), TT)
            at_n = rstd(16, P)
            v.tensor_reduce(ss[:, at_n:at_n + 16].rearrange("p (t h) -> p t h", t=TT), sq[:, :, :, 0:P], AX,
                            ALU.add).then_inc(ss_ready, 1)
            at_p = rstd(16, 64)
            v.tensor_reduce(ss[:, at_p:at_p + 16].rearrange("p (t h) -> p t h", t=TT), sq[:, :, :, P:192], AX,
                            ALU.add).then_inc(ss_ready, 1)
            rstd_wait()
            for t in range(TT):
                link(head_scale(lq[:, t, :, 0:P], lq[:, t, :, 0:P], at_n, t, 8, P))
            settle()
            signal("lq_normed")
            for t in range(TT):
                link(head_scale(lq[:, t, :, P:192], lq[:, t, :, P:192], at_p, t, 8, 64))
            settle()
            for t in range(TT):
                q_ = lq[:, t, :, P:192]
                link(v.tensor_tensor(q_, q_, pe_gain[:, 0, :].unsqueeze(1).to_broadcast([P, 8, 64]), ALU.mult))
            for t in range(TT):
                rope(qpe_tok[:, t], lq[:, t, :, P:192], None, cos[:, t, :].unsqueeze(1).to_broadcast([P, 8, 32]),
                     sin[:, t, :].unsqueeze(1).to_broadcast([P, 8, 32]),
                     tmp[:, 0, 0:256].rearrange("p (h c) -> p h c", c=32))
            signal("qpe_ready")
            dve.wait_ge(sem("lk_squares"), TT)
            sq = extra[:, 0:2048].rearrange("p (t h c) -> p t h c", t=TT, c=P)
            at = rstd(16, P)
            v.tensor_reduce(ss[:, at:at + 16].rearrange("p (t h) -> p t h", t=TT), sq, AX, ALU.add).then_inc(ss_ready, 1)
            rstd_wait()
            for t in range(TT):
                link(head_scale(lk[:, t], lk[:, t], at, t, 8, P))
            settle()
            signal("lk_normed")
            attention("mla", 8, lambda u: mask[:, :], (P + 64) ** -0.5, False, plain_output("mla", 8, False))
            for n in range(2):
                for t in range(TT):
                    residual(("l_o", n, "tok", t), t, n, False)
            norm("m2", [(h_t, params[:, col["mn2_0"]:col["mn2_0"] + KT], None)], 0)
            for t in range(TT):
                lo, n = (0, P) if t == 0 else (P, T)
                link(v.tensor_scalar(dist[:, lo:lo + n], pos_f[:, 0, 0:n], pos_f[:, 0, T + t:T + t + 1], -4096.0,
                                     ALU.subtract, ALU.mult))
                link(v.tensor_scalar(ge[:, 0, lo:lo + n], pos_f[:, 1, 0:n], pos_f[:, 1, T + t:T + t + 1], -1.0,
                                     ALU.subtract, ALU.mult))
            settle()
            link(v.tensor_tensor(dist, dist, ge[:, 0, :], ALU.add))
            settle()
            starts = list(range(17)) + [math.ceil(16 * 64.0 ** (i / 16) - 1e-6) for i in range(1, 16)]
            for b_ in range(BUCKETS):
                if b_ < BUCKETS - 1:
                    link(v.tensor_scalar(ge[:, b_ % 2, :], dist, float(starts[b_ + 1]), None, ALU.is_lt))
                    settle()
                if b_ == 0:
                    oh = ge[:, 0, :]
                elif b_ < BUCKETS - 1:
                    link(v.scalar_tensor_tensor(onehot, dist, float(starts[b_]), ge[:, b_ % 2, :], ALU.is_ge, ALU.mult))
                    oh = onehot
                else:
                    link(v.tensor_scalar(onehot, dist, float(starts[b_]), None, ALU.is_ge))
                    oh = onehot
                settle()
                for h in range(8):
                    link(v.scalar_tensor_tensor(bias2[:, h, :], oh, table2[:, b_ * 8 + h:b_ * 8 + h + 1],
                                                mask[:, :] if b_ == 0 else bias2[:, h, :], ALU.mult, ALU.add))
                settle()
            for n in range(2):
                for t in range(TT):
                    residual(("m2", "y", n, t), t, n, False)

            norm("o", [(h_t, params[:, col["an2_1"]:col["an2_1"] + KT], None)], 0)
            for what, src in (("q", xn), ("k", o_tok)):
                sq = extra[:, 0:2048] if what == "q" else extra[:, 2048:4096]
                for c in range(2):
                    for t in range(TT):
                        bank_emptied(dve, ("o_qkv", c if what == "q" else 2 + c, "tok", t))
                at = rstd(16, P)
                v.tensor_reduce(ss[:, at:at + 16].rearrange("p (t h) -> p t h", t=TT),
                                sq.rearrange("p (t h c) -> p t h c", t=TT, c=P), AX, ALU.add).then_inc(ss_ready, 1)
                rstd_wait()
                for t in range(TT):
                    s_ = src[:, t, :].rearrange("p (h c) -> p h c", c=P)
                    link(head_scale(s_, s_, at, t, 8, P))
                settle()
                signal(f"o{what}_normed")
            attention("moba", 8, lambda u: bias2[:, u, :], P ** -0.5, False, plain_output("moba", 8, False))
            for n in range(2):
                for t in range(TT):
                    residual(("o_o", n, "tok", t), t, n, False)
            norm("m3", [(h_t, params[:, col["mn2_1"]:col["mn2_1"] + KT], None)], 0)
            for n in range(2):
                for t in range(TT):
                    residual(("m3", "y", n, t), t, n, False)

        @block.scalar
        def _(act):
            a = nc.scalar

            n_squares = [0]

            def row(v_, n):
                return v_.rearrange("(a n) -> a n", a=1)[0:1, 0:n].to_broadcast([P, n])

            a.dma_start(ident[:, :], dram["ident"]).then_inc(sem("const_in"), 16)
            a.dma_start(flip[:, :], dram["flip"]).then_inc(sem("const_in"), 16)
            a.dma_start(mask[:, :], dram["mask"]).then_inc(sem("const_in"), 16)
            a.dma_start(ex[0:HEADS, 0, :], dram["negrow"]).then_inc(sem("const_in"), 16)
            a.dma_start(cmask[:, :, :, :], dram["cmask"].rearrange("p (a t n) -> p a t n", a=2, t=TT)).then_inc(
                sem("const_in"), 16)
            names = {"c": "c", "kv_b": "kv_ada_b", "kvn": "kv_norm", "subln": "a_subln", "qan": "mla_q_a_norm_2",
                     "kvan": "mla_kv_a_norm_2", "qnn": "mla_q_nope_norm_2", "knn": "mla_k_nope_norm_2",
                     "mqn": "moba_q_norm_2", "mkn": "moba_k_norm_2"}
            layered = {"ada_b0": ("ada_b", 0), "ada_b1": ("ada_b", 1), "an0": ("attn_norm", 0),
                       "an1": ("attn_norm", 1), "mn0": ("mlp_norm", 0), "mn1": ("mlp_norm", 1),
                       "an2_0": ("attn_norm_2", 0), "an2_1": ("attn_norm_2", 1), "mn2_0": ("mlp_norm_2", 0),
                       "mn2_1": ("mlp_norm_2", 1)}
            for name, n in PARAM_ROWS:
                if name in layered:
                    src = dram[layered[name][0]][layered[name][1]]
                elif name == "kv_b" or name == "kvn":
                    src = dram[names[name]]
                else:
                    src = dram[names[name]][0]
                src = src.rearrange("(k p) -> k p", p=P)
                r = col[name]
                half, r = divmod(r, P)
                assert r + n <= P
                a.dma_start(prow[r:r + n, half, :], src).then_inc(sem("param_in"), 16)
            a.dma_start(sc[0:BUCKETS, 0, 0:HEADS], dram["rel_bias"]).then_inc(sem("table_in"), 16)
            a.dma_start(sc[0:BUCKETS, 1, :], dram["onehot"]).then_inc(sem("table_in"), 16)
            a.dma_start(lam_in[:, :, :].rearrange("p a b -> p (a b)"),
                        row(dram["a_lambda"].rearrange("l a b -> (l a b)"), 256)).then_inc(sem("lam_in"), 16)
            for t in range(TT):
                a.dma_start(x_res[:, t, :], dram["x"][0, t * P:(t + 1) * P, :]).then_inc(sem("x_in"), 16)
            bank_emptied(act, "params")
            a.activation(c_tmp[:, :], params[:, 0:KT], ACT.Exp, scale=-1.0).then_inc(sem("silu_exp"), 1)
            act.wait_ge(sem("lam_dots"), 1)
            a.activation(lam[:, 4:6], lam[:, 0:2], ACT.Exp).then_inc(sem("lam_exp"), 1)
            bank_emptied(act, "bias_rows")
            a.dma_start(bias_scratch[:, :], ex[0:HEADS, 1, :]).then_inc(sem("bias_out"), 16)
            act.wait_ge(sem("bias_out"), 16)
            a.dma_start(bias1_v[:, :, 0:P], bass.AP(tensor=bias_scratch.tensor, offset=P,
                                                   ap=[[1, P], [384, HEADS], [1, P]])).then_inc(sem("bias_back"), 16)
            a.dma_start(bias1_v[:, :, P:STRIP], bass.AP(tensor=bias_scratch.tensor, offset=0,
                                                       ap=[[1, P], [384, HEADS], [1, T]])).then_inc(sem("bias_back"), 16)
            a.dma_start(cmp_w2[:, :, :, :], dram["cmp_w2"].rearrange("s (i p) d -> p s i d", p=P)).then_inc(
                sem("cmp_w2_in"), 16)
            a.dma_start(fn_row[:, :], row(dram["final_norm"], D)).then_inc(sem("cmp_w2_in"), 16)
            a.dma_start(pos_i[:, 0:T], dram["positions_2"][0:1, :].to_broadcast([P, T])).then_inc(sem("pos_in"), 16)
            a.dma_start(pos_i[:, T:T + TT], dram["positions_2"].rearrange("a (t p) -> p (a t)", p=P),
                        allow_slow_non_contiguous=True).then_inc(sem("pos_in"), 16)
            for par in range(2):
                a.dma_start(pos_cmp[64 * par:64 * par + 64, :, :],
                            dram["cmp_pos"].rearrange("s (l par) d -> par d s l", par=2)[par],
                            allow_slow_non_contiguous=True).then_inc(sem("pos_in"), 16)
            a.dma_start(table2[:, :], row(dram["rel_bias_table_2"].rearrange("b h -> (b h)"), 256)).then_inc(
                sem("late_in"), 16)
            a.dma_start(inv_freq[:, :], dram["inv_freq"]).then_inc(sem("late_in"), 16)
            a.dma_start(pe_gain[:, 0, :], row(dram["mla_q_rope_norm_2"][0], 64)).then_inc(sem("late_in"), 16)
            a.dma_start(pe_gain[:, 1, :], row(dram["mla_k_rope_norm_2"][0], 64)).then_inc(sem("late_in"), 16)

            def square(src, dst, accum=None, signal=None):
                ins = a.activation(dst, src, ACT.Square, accum_out=accum) if accum is not None else \
                    a.activation(dst, src, ACT.Square)
                ins.then_inc(signal, 1)

            def x_squares(call, total=None, after=None):
                at = (call % 2) * 32
                for t in range(TT):
                    if total:
                        act.wait_ge(x_ready, total - 1 + t)
                    if after:
                        bank_emptied(act, after(t))
                    ins = a.activation(ps_s[:, :, :].rearrange("p a c -> p (a c)"), x_res[:, t, :], ACT.Square,
                                       accum_out=ss[:, at + t:at + t + 1])
                    if t == 0:
                        ins.then_inc(sem("first_squares"), 1)
                        n_squares[0] += 1
                        act.wait_ge(sem("first_squares"), n_squares[0])
                ins.then_inc(ss_ready, 1)

            def norm(name, outs, gains):
                if gains:
                    act.wait_ge(sem("gains_ready"), gains)
                for g in range(1, KT // 2, 2):
                    src = bank_full(act, (name, "turn", g))
                    b = uses[(name, "turn", g)][0]
                    for dst, gn, sh in outs:
                        for i in range(2):
                            j = 2 * g + i
                            part = src[:, i * T:(i + 1) * T]
                            if sh is None:
                                ins = a.activation(dst[:, j, :], part, ACT.Identity, scale=gn[:, j:j + 1])
                            else:
                                ins = a.activation(dst[:, j, :], part, ACT.Identity, scale=gn[:, j:j + 1],
                                                   bias=sh[:, j:j + 1])
                            ins.then_inc(drained[b], 1)

            def drain(key, dst, cols, scale=None, func=ACT.Copy):
                src = bank_full(act, key)
                ins = a.activation(dst, src[:, cols[0]:cols[1]], func) if scale is None else \
                    a.activation(dst, src[:, cols[0]:cols[1]], ACT.Identity, scale=scale)
                ins.then_inc(drained[uses[key][0]], 1)

            def attention(name, units, pairs):
                maxed, exped = sem(f"{name}_maxed"), sem(f"{name}_exped")
                turned_, copied = sem(f"{name}_turned"), sem(f"{name}_copied")
                outs = units // 2 if pairs else units

                def exps(u):
                    act.wait_ge(maxed, 2 * u + 2)
                    if u >= ATT:
                        act.wait_ge(turned_, (u - ATT) // 2 + 1 if pairs else u - ATT + 1)
                    for t in range(TT):
                        lo, hi = (0, P) if t == 0 else (P, STRIP)
                        a.activation(ex[:, u % ATT, lo:hi], sc[:, u % 2, lo:hi], ACT.Exp, bias=nmax[:, u, t:t + 1],
                                     accum_out=rsum[:, u, t:t + 1]).then_inc(exped, 1)

                def copy(v_):
                    act.wait_ge(turned_, v_ + 1)
                    if v_ >= 2:
                        bank_full(act, (name, "o", v_ - 2))
                    a.activation(pt[:, v_ % 2, :], ps_p[:, v_ % 2, 0:STRIP], ACT.Copy).then_inc(copied, 1)

                if pairs:
                    for h in range(outs + 1):
                        if h < outs:
                            exps(2 * h)
                            exps(2 * h + 1)
                        if h >= 1:
                            copy(h - 1)
                else:
                    for u in range(units + 1):
                        if u < units:
                            exps(u)
                        if u >= 1:
                            copy(u - 1)

            def turn_o(name, scale=None):
                for g in range(KT // 2):
                    drain((name, "turn_o", g), o_t[:, 2 * g:2 * g + 2, :].rearrange("p a t -> p (a t)"), (0, W),
                          scale)

            def hidden(tag):
                for c in range(FF // W):
                    for g in range(2):
                        f = 4 * c + 2 * g
                        drain((f"{tag}_w1", c, g), arena[:, f * T:(f + 2) * T], (0, W), func=ACT.Relu)

            for h in range(HEADS):
                drain(("bias", h), bias1_v[:, h, :], (0, STRIP))
            act.wait_ge(sem("x_in"), 32)
            x_squares(0)
            norm("a0", [(h_t, gs, mod[:, 0:8])], 1)
            for c in range(4):
                for g in range(2):
                    h = 4 * c + 2 * g
                    drain(("a_in", c, g), arena[:, h * T:(h + 2) * T], (0, W))
            for c in (4, 5):
                for t in range(TT):
                    drain(("a_in", c, "tok", t), v_tok[:, t, (c - 4) * W:(c - 3) * W], (0, W))
            attention("diff", 16, True)
            bank_emptied(act, ("diff", "o", 7))
            for t in range(TT):
                square(o_tok[:, t, :], xn[:, t, :], signal=sem("diff_squares"))
            a.activation(stat[:, 8:9], params[:, col["subln"]:col["subln"] + 1], ACT.Copy,
                         scale=1.0 - LAM_INIT).then_inc(sem("subln_ready"), 1)
            act.wait_ge(sem("subln_ready"), 1)
            turn_o("diff", stat[:, 8:9])
            x_squares(2, 4)
            norm("m0", [(h_t, gs, mod[:, 24:32])], 2)
            hidden("m0")
            x_squares(3, 8)
            norm("kv", [(h_t, gs, mod[:, 64:72]), (h_kv, gs2, mod[:, 48:56])], 4)
            for w_, name in enumerate(("k_slc", "k_win")):
                src = bank_full(act, (name, 0))
                for par in range(2):
                    for i in range(2):
                        for g in range(2):
                            ins = a.activation(k_nsa[64 * par:64 * par + 64, w_, 2 * i + g, :],
                                               src[64 * g:64 * g + 64, i * T:(i + 1) * T], ACT.Copy)
                ins.then_inc(drained[uses[(name, 0)][0]], 1)
                for t in range(TT):
                    drain(("w_kv", 1 + w_, "tok", t), v_nsa[:, w_, t, :], (0, 256))
            for s in range(2):
                act.wait_ge(sem("gelu_arg"), s + 1)
                a.activation(gel[:, 2, :, :], gel[:, 1, :, :], ACT.Exp, scale=-2.0 * GELU_C).then_inc(
                    sem("gelu_exp"), 1)
            for c in range(2):
                for g in range(2):
                    h = 4 * c + 2 * g
                    drain(("b_in", c, g), arena[:, h * T:(h + 2) * T], (0, W))
            for t in range(TT):
                src = bank_full(act, ("b_in", 2, "tok", t))
                a.activation(gates[:, t, :], src[:, 0:48], ACT.Exp, scale=-1.0).then_inc(
                    drained[uses[("b_in", 2, "tok", t)][0]], 1)
            act.wait_ge(sem("cmp_centred"), 1)
            a.activation(s_cmp2[:, :, :, 0:NCMP], s_cmp[:, :, :, 0:NCMP], ACT.Exp).then_inc(sem("cmp_exped"), 1)
            for t in range(TT):
                drain(("cmp_turn", t), extra[:, 1024 + t * W:1024 + (t + 1) * W], (0, W))
            attention("slc", HEADS, False)
            attention("win", HEADS, False)
            turn_o("nsa")
            x_squares(4, 12)
            norm("m1", [(h_t, gs, mod[:, 64 + 24:64 + 32])], 5)
            hidden("m1")
            act.wait_ge(sem("angles_ready"), 1)
            a.activation(ang[:, 1, :, :], ang[:, 0, :, :], ACT.Abs).then_inc(sem("abs_ready"), 1)
            a.activation(stat[:, 16:17], params[:, 0:1], ACT.Copy, scale=0.0).then_inc(sem("abs_ready"), 1)
            act.wait_ge(sem("abs_ready"), 2)
            a.activation(stat[:, 17:18], stat[:, 16:17], ACT.Copy, bias=math.pi / 2).then_inc(sem("abs_ready"), 1)
            a.activation(trig[:, 1, :, :], ang[:, 0, :, :], ACT.Sin).then_inc(sem("trig_ready"), 1)
            act.wait_ge(sem("abs_ready"), 3)
            a.activation(trig[:, 0, :, :], ang[:, 1, :, :], ACT.Sin, scale=-1.0, bias=stat[:, 17:18]).then_inc(
                sem("trig_ready"), 1)
            x_squares(5, 16)

            x_squares(6, 18)
            norm("l", [(h_t, params[:, col["an2_0"]:col["an2_0"] + KT], None)], 0)
            for c, n in ((0, W), (1, 192)):
                for t in range(TT):
                    drain(("l_in", c, "tok", t), lat[:, t, c * W:c * W + n], (0, n))
            for c in range(2):
                for t in range(TT):
                    bank_emptied(act, ("l_in", c, "tok", t))
            for t in range(TT):
                square(lat[:, t, :], arena[:, t * 704:(t + 1) * 704], signal=sem("lat_squares"))
            for g, (j0, n) in enumerate(((0, 2), (2, 2), (4, 1))):
                key = ("latent_turn", g)
                src = bank_full(act, key)
                for i in range(n):
                    j = j0 + i
                    ins = a.activation(lat_t[:, j, :], src[:, i * T:(i + 1) * T], ACT.Identity,
                                       scale=params[:, col["qan"] + j:col["qan"] + j + 1])
                ins.then_inc(drained[uses[key][0]], 1)
            src = bank_full(act, "kpe_turn")
            a.activation(kpe_t, src[0:64, 0:T], ACT.Copy).then_inc(drained[uses["kpe_turn"][0]], 1)
            for c in range(3):
                for t in range(TT):
                    drain(("l_uq", c, "tok", t), bias1[:, t * 1536 + c * W:t * 1536 + (c + 1) * W], (0, W))
            for c in range(3):
                for t in range(TT):
                    bank_emptied(act, ("l_uq", c, "tok", t))
            for t in range(TT):
                square(bias1[:, t * 1536:(t + 1) * 1536], arena[:, t * 1536:(t + 1) * 1536], signal=sem("lq_squares"))
            for c in range(4):
                for t in range(TT):
                    key = ("l_ukv", c, "tok", t)
                    src = bank_full(act, key).rearrange("p (h c) -> p h c", c=T)
                    b = uses[key][0]
                    a.activation(lk[:, t, 2 * c:2 * c + 2, :], src[:, :, 0:P], ACT.Copy).then_inc(drained[b], 1)
                    a.activation(v_tok[:, t, :].rearrange("p (h c) -> p h c", c=P)[:, 2 * c:2 * c + 2, :],
                                 src[:, :, P:2 * P], ACT.Copy).then_inc(drained[b], 1)
            for c in range(4):
                for t in range(TT):
                    bank_emptied(act, ("l_ukv", c, "tok", t))
            for t in range(TT):
                square(lk[:, t], extra[:, t * 1024:(t + 1) * 1024].rearrange("p (h c) -> p h c", c=P),
                       signal=sem("lk_squares"))
            act.wait_ge(sem("lk_normed"), 1)
            for what, dst, gname in (("q", 0, "qnn"), ("k", 2048, "knn")):
                for g in range(4):
                    drain(("l_turn", what, g), arena[:, dst + 2 * g * T:dst + (2 * g + 2) * T], (0, W),
                          params[:, col[gname]:col[gname] + 1])
            for g in range(4):
                key = ("qpe_turn", g)
                src = bank_full(act, key)
                a.activation(qpe_t[:, 2 * g:2 * g + 2, :].rearrange("p a t -> p (a t)"), src[0:64, :],
                             ACT.Copy).then_inc(drained[uses[key][0]], 1)
            attention("mla", 8, False)
            turn_o("mla")
            x_squares(13, after=lambda t: ("l_o", 1, "tok", t))
            norm("m2", [(h_t, params[:, col["mn2_0"]:col["mn2_0"] + KT], None)], 0)
            hidden("m2")
            x_squares(14, after=lambda t: ("m2", "y", 1, t))

            norm("o", [(h_t, params[:, col["an2_1"]:col["an2_1"] + KT], None)], 0)
            for c in range(4):
                to = xn if c < 2 else o_tok
                for t in range(TT):
                    key = ("o_qkv", c, "tok", t)
                    src = bank_full(act, key)
                    cc = c % 2
                    at = (0 if c < 2 else 2048) + t * D + cc * W
                    a.activation(to[:, t, cc * W:(cc + 1) * W], src, ACT.Copy).then_inc(drained[uses[key][0]], 1)
                    a.activation(extra[:, at:at + W], src, ACT.Square).then_inc(drained[uses[key][0]], 1)
            for c in (4, 5):
                for t in range(TT):
                    drain(("o_qkv", c, "tok", t), v_tok[:, t, (c - 4) * W:(c - 3) * W], (0, W))
            for what, dst, gname in (("q", 0, "mqn"), ("k", 2048, "mkn")):
                for g in range(4):
                    drain(("o_turn", what, g), arena[:, dst + 2 * g * T:dst + (2 * g + 2) * T], (0, W),
                          params[:, col[gname]:col[gname] + 1])
            attention("moba", 8, False)
            turn_o("moba")
            x_squares(17, after=lambda t: ("o_o", 1, "tok", t))
            norm("m3", [(h_t, params[:, col["mn2_1"]:col["mn2_1"] + KT], None)], 0)
            hidden("m3")

        @block.gpsimd
        def _(pool):
            g_ = nc.gpsimd
            g_.memset(mhalf[:, :], -0.5).then_inc(sem("mhalf_set"), 1)
            pool.wait_ge(sem("mhalf_set"), 1)
            done = [0]
            squared_before = {3: "m0", 5: "m1", 14: "m2"}

            def roots(k):
                width, n = rstd_calls[k]
                at = (k % 2) * 32
                pool.wait_ge(ss_ready, k + 1)
                g_.tensor_scalar(rs[:, at:at + width], ss[:, at:at + width], 1.0 / n, EPS, ALU.mult,
                                 ALU.add).then_inc(sem("mean_ready"), 1)
                pool.wait_ge(sem("mean_ready"), k + 1)
                g_.tensor_tensor(rs[:, at:at + width], rs[:, at:at + width], mhalf[:, 0:width],
                                 ALU.pow).then_inc(rstd_ready, 1)

            def squares(tag):
                for c in range(FF // W):
                    for g in range(2):
                        bank_emptied(pool, (f"{tag}_w1", c, g))
                        f = 4 * c + 2 * g
                        h = arena[:, f * T:(f + 2) * T]
                        g_.tensor_tensor(h, h, h, ALU.mult).then_inc(sem(f"{tag}_squared"), 1)

            for k in range(len(rstd_calls)):
                if k in squared_before:
                    squares(squared_before[k])
                roots(k)
            squares("m3")

        @block.sync
        def _(sp):
            for i, (key, kind, arg, kt, n) in enumerate(plan):
                if i >= SLOTS:
                    sem_, value = chunk_free[plan[i - SLOTS][0]]
                    sp.wait_ge(sem_, value)
                dst = chunk(key)
                if kind == "mat":
                    src = dram[arg[0]].rearrange("(k p) n -> p k n", p=P)[:, :, arg[1]:arg[1] + n]
                elif kind == "mlp2":
                    src = dram[arg[0]].rearrange("(k p) n -> p k n", p=P)[:, arg[2]:arg[2] + kt, arg[1]:arg[1] + n]
                else:
                    src = dram["cmp_w1"][arg[1]].rearrange("(k p) n -> p k n", p=P)
                sp.dma_start(dst, src).then_inc(chunk_in[i % SLOTS], 16)
            for n in range(2):
                for t in range(TT):
                    bank_emptied(sp, ("m3", "y", n, t))
                    sp.dma_start(out[0, t * P:(t + 1) * P, n * W:(n + 1) * W],
                                 x_res[:, t, n * W:(n + 1) * W]).then_inc(sem("out_done"), 16)
            sp.wait_ge(sem("out_done"), 64)


def shape_constants():
    p = np.arange(P)
    dist = 255 - np.arange(384)
    starts = list(range(17)) + [math.ceil(16 * 8.0 ** (i / 16) - 1e-6) for i in range(1, 16)]
    bucket = np.searchsorted(np.array(starts), np.maximum(dist, 0), side="right") - 1
    onehot = (np.arange(BUCKETS)[:, None] == bucket[None, :]).astype(np.float32)
    negrow = np.broadcast_to(np.where(dist < 0, NEG, 0.0), (HEADS, 384)).astype(np.float32)
    tri = np.where(p[:, None] >= p[None, :], 0.0, NEG).astype(np.float32)
    mask = np.concatenate([tri, np.zeros((P, P), np.float32), tri], axis=1)
    q = np.arange(T).reshape(TT, P).T
    valid = (np.arange(NCMP) * 16 + 31)[None, None, :] <= q[:, :, None]
    cmask = np.stack([np.where(valid, 0.0, NEG), valid.astype(np.float64)], axis=1).astype(np.float32)
    inv = (10000.0 ** (-np.arange(0, 64, 2) / 64)).astype(np.float32)
    return {"ident": np.eye(P, dtype=np.float32), "flip": np.eye(P, dtype=np.float32)[::-1].copy(), "mask": mask,
            "negrow": negrow, "cmask": cmask.reshape(P, -1), "onehot": onehot,
            "inv_freq": np.broadcast_to(inv, (P, 32)).copy()}


def kernel(**inputs):
    import concourse.bacc as bacc
    from concourse.bass_utils import run_bass_kernel_spmd

    nc = bacc.Bacc("TRN2", target_bir_lowering=False, num_devices=1)
    arrays = {name: np.ascontiguousarray(a) for name, a in inputs.items()}
    arrays.update(shape_constants())
    feed, dram = {}, {}
    for name, a in arrays.items():
        feed[f"in_{name}"] = a
        dram[name] = nc.dram_tensor(f"in_{name}", a.shape, mybir.dt.from_np(a.dtype), kind="ExternalInput").ap()
    stack_one = {"a_in": dram["a_w_in"][0], "a_out": dram["a_w_out"][0], "b_in": dram["b_w_in"][0],
                 "b_out": dram["b_w_out"][0], "ada0": dram["ada_w"][0], "ada1": dram["ada_w"][1],
                 "adakv": dram["kv_ada_w"]}
    stack_two = {"l_in": dram["mla_w_in_2"][0], "l_uq": dram["mla_w_uq_2"][0], "l_ukv": dram["mla_w_ukv_2"][0],
                 "l_o": dram["mla_w_o_2"][0], "o_qkv": dram["moba_w_qkv_2"][0], "o_o": dram["moba_w_o_2"][0]}
    for i, (w1, w2, layer) in enumerate((("mlp_w1", "mlp_w2", 0), ("mlp_w1", "mlp_w2", 1),
                                         ("mlp_w_in_2", "mlp_w_out_2", 0), ("mlp_w_in_2", "mlp_w_out_2", 1))):
        stack_two[f"m{i}_w1"] = dram[w1][layer]
        stack_two[f"m{i}_w2"] = dram[w2][layer]
    dram.update(stack_one)
    dram.update(stack_two)
    out = nc.dram_tensor("out", (1, T, D), F32, kind="ExternalOutput").ap()
    build(nc, dram, out)
    r = run_bass_kernel_spmd(nc, [feed], core_ids=[0])
    return r.results[0]["out"]
```

```python
from contextlib import ExitStack
import math

import numpy as np

import concourse.bass as bass
from concourse import mybir

F32 = mybir.dt.float32
F32R = mybir.dt.float32r
I32 = mybir.dt.int32
ALU = mybir.AluOpType
ACT = mybir.ActivationFunctionType
AX = mybir.AxisListType.X

P = 128
D = 1024
T = 256
TT = T // P
KT = D // P
FF = 4 * D
W = 512
SLOTS = 10
PIECES = 5
PIECE = 1024
EPS = 1e-6
NEG = -1e30
HEADS = 16
POOL_HEADS = 1
BUCKETS = 32
NCMP = (T - 32) // 16 + 1
LAM_INIT = 0.8 - 0.6 * math.exp(-0.3 * 0)
GELU_C = math.sqrt(2.0 / math.pi)
BANKS = 4
TWO_PI = 2.0 * math.pi
STRIP = 3 * P
ATT = 4

PARAM_ROWS = [("c", 8), ("ada_b0", 48), ("ada_b1", 48), ("kv_b", 16),
              ("an0", 8), ("an1", 8), ("mn0", 8), ("mn1", 8), ("kvn", 8),
              ("an2_0", 8), ("an2_1", 8), ("mn2_0", 8), ("mn2_1", 8),
              ("subln", 1), ("qan", 3), ("kvan", 2), ("qnn", 1), ("knn", 1), ("mqn", 1), ("mkn", 1)]


def param_columns():
    col, at = {}, 0
    for name, n in PARAM_ROWS:
        col[name] = at
        at += n
    return col, at


def pow2_split(value, bits, parts):
    out = []
    for _ in range(parts - 1):
        e = math.floor(math.log2(abs(value))) if value else 0
        q = 2.0 ** (e - bits + 1)
        head = math.floor(value / q) * q
        out.append(head)
        value -= head
    return out + [value]


def weight_plan():
    plan = []

    def feat(kt, lo, hi):
        return [((0, kt), (n, n + P)) for n in range(lo, hi, P)]

    def tok(kt, lo, hi):
        step = max(1, min(kt, PIECE // (hi - lo)))
        return [((k, min(k + step, kt)), (lo, hi)) for k in range(0, kt, step)]

    def mat(name, k, n, kinds):
        out = []
        for c in range(-(-n // W)):
            w, kt = min(W, n - c * W), k // P
            pieces = {"f": feat(kt, 0, w), "t": tok(kt, 0, w), "ft": feat(kt, 0, T) + tok(kt, T, W)}[kinds[c]]
            out.append(((name, c), (name, 0, c * W), kt, w, pieces))
        return out

    def ada(layer, cs):
        return [((f"ada{layer}", c), (f"ada{layer}", 0, c * W), KT, W, tok(KT, 0, W)) for c in cs]

    def mlp(tag):
        w1 = mat(f"{tag}_w1", D, FF, "f" * 8)
        w2 = [((f"{tag}_w2", c), (f"{tag}_w2", 4 * c, 0), 4, D, tok(4, 0, D)) for c in range(8)]
        out = w1[:1]
        for c in range(1, 8):
            out += [w1[c], w2[c - 1]]
        return out + w2[7:]

    def mix(a, b):
        out = []
        for i in range(max(len(a), len(b))):
            out += a[i:i + 1] + b[i:i + 1]
        return out

    plan += ada(0, range(4))
    plan += mix(mat("a_in", D, 3 * D, "fffftt"), ada(0, range(4, 10))) + ada(0, range(10, 12))
    plan += mat("a_out", D, D, "tt")
    plan += mix(mlp("m0"), ada("kv", range(4)) + ada(1, range(6)))
    w_kv, b_in = mat("w_kv", D, 1536, ["f", "ft", "ft"]), mat("b_in", D, 1072, "fft")
    cmp = [(("cmp_w1", s), ("cmp_w1", s, 0), 16, 256, tok(16, 0, 256)) for s in range(2)]
    late = ada(1, range(6, 12))
    plan += w_kv[:2] + late[:1] + w_kv[2:] + cmp + late[1:2] + b_in[:2] + late[2:3] + b_in[2:] + late[3:]
    plan += mat("b_out", D, D, "tt") + mlp("m1")
    plan += mat("l_in", D, 704, "tt") + mat("l_uq", 384, 1536, "ttt") + mat("l_ukv", 256, 2048, "tttt")
    plan += mat("l_o", D, D, "tt") + mlp("m2") + mat("o_qkv", D, 3 * D, "t" * 6) + mat("o_o", D, D, "tt") + mlp("m3")
    return plan


def build(nc, dram, out):
    col, n_cols = param_columns()
    plan = weight_plan()
    chunk_of = {c[0]: c for c in plan}
    loads = [(c[0], ks, ns) for c in plan for ks, ns in c[4]]
    first_load = {}
    for i, (key, _, _) in enumerate(loads):
        first_load.setdefault(key, i)
    piece_load = [i for i, (key, _, _) in enumerate(loads) if key[0] != "cmp_w1" and not key[0].startswith("ada")]
    pieces = [loads[i] for i in piece_load]
    first_piece = {}
    for i, (key, _, _) in enumerate(pieces):
        first_piece.setdefault(key, i)

    with ExitStack() as ctx:
        def sb(name, shape, dt=F32):
            return ctx.enter_context(nc.sbuf_tensor(name, shape, dt))

        sems = {}

        def sem(name):
            if name not in sems:
                sems[name] = ctx.enter_context(nc.semaphore(name))
            return sems[name]

        wring = sb("wring", [P, SLOTS, PIECE])
        x_res = sb("x_res", [P, TT, D])
        h_hi = sb("h_hi", [P, KT, T], F32R)
        h_lo = sb("h_lo", [P, KT, T], F32R)
        whi = sb("whi", [P, PIECES, PIECE], F32R)
        wlo = sb("wlo", [P, PIECES, PIECE], F32R)

        def in_turn(name, elements, others):
            with nc.sbuf_tensor(name, [P, elements], F32) as first:
                pass
            return first, [sb(n, shape, F32R) for n, shape in others]

        arena, (g_hi, g_lo, _) = in_turn("arena", 32 * T, [("g_hi", [P, 2, 4, T]), ("g_lo", [P, 2, 4, T]),
                                                            ("arena_rest", [P, 16 * T])])
        q_t = arena[:, 0:2048].rearrange("p (h t) -> p h t", t=T)
        k_t = arena[:, 2048:4096].rearrange("p (h t) -> p h t", t=T)
        v_tok = arena[:, 4096:6144].rearrange("p (t c) -> p t c", t=TT)
        o_tok = arena[:, 6144:8192].rearrange("p (t c) -> p t c", t=TT)
        bias1 = sb("bias1", [P, HEADS * T])
        bias1_v = bias1[:, :].rearrange("p (h c) -> p h c", c=T)
        xn = sb("xn", [P, TT, D])
        extra, (hk_hi, hk_lo) = in_turn("extra", 4096, [("hk_hi", [P, KT, T]), ("hk_lo", [P, KT, T])])
        gate_row = sb("gate_row", [P, D])
        att = sb("att", [P, 4 * STRIP])
        sc = att[:, 0:2 * STRIP].rearrange("p (b c) -> p b c", c=STRIP)
        ex = sb("ex", [P, ATT, STRIP])
        pt = att[:, 2 * STRIP:].rearrange("p (b c) -> p b c", c=STRIP)
        tmp = att[:, 0:2 * W].rearrange("p (b c) -> p b c", c=W)
        acc = sb("acc", [P, 3, W])
        prow = acc[:, 2, 0:2 * P].rearrange("p (i c) -> p i c", i=2)
        params = sb("params", [P, n_cols])
        mod = sb("mod", [P, 112])
        gs = sb("gs", [P, KT])
        gs2 = sb("gs2", [P, KT])
        c_col = sb("c_col", [P, KT])
        c_tmp = sb("c_tmp", [P, KT])
        c_raw = sb("c_raw", [P, KT])
        ident = sb("ident", [P, P])
        ones = sb("ones", [P, 1])
        mhalf = sb("mhalf", [P, 32])
        mask = sb("mask", [P, STRIP])
        stat = sb("stat", [P, 32])
        nmax = sb("nmax", [P, 16, 2])
        rsum = sb("rsum", [P, 16, 2])
        rinv = sb("rinv", [P, 16, 2])
        lam_in = pt[:, 0, 0:256].rearrange("p (a c) -> p a c", a=4)
        lam = sb("lam", [P, 8])
        ss = sb("ss", [P, 64])
        rs = sb("rs", [P, 64])
        fn_row = extra[:, 2048:3072]
        kv_raw = arena[:, 6144:8192].rearrange("p (s g t) -> p s g t", s=2, t=T)
        k_nsa = arena[:, 2048:4096].rearrange("p (w g t) -> p w g t", w=2, t=T)
        v_nsa = arena[:, 4096:5120].rearrange("p (w t c) -> p w t c", w=2, t=TT)
        blocks = arena[:, 5120:5120 + 16 * 4 * NCMP].rearrange("p (l c) -> p l c", l=16)
        p_cmp = extra[:, 0:1024].rearrange("p (t g c) -> p t g c", t=TT, c=P)
        pt_cmp = extra[:, 1024:2048].rearrange("p (t g c) -> p t g c", t=TT, c=P)
        v_cmp = extra[:, 2048:3072].rearrange("p (g c) -> p g c", g=4)
        s_cmp = extra[:, 3072:3584].rearrange("p (t h n) -> p t h n", t=TT, n=16)
        s_cmp2 = extra[:, 3584:4096].rearrange("p (t h n) -> p t h n", t=TT, n=16)
        cmp_hid = extra[:, 1024:1536].rearrange("p (s i c) -> p s i c", s=2, i=2)
        cmp_w2 = sb("cmp_w2", [P, 2, 2, 64])
        k_cmp = sb("k_cmp", [P, 4, 32])
        flip = k_cmp[:, :, :].rearrange("p g n -> p (g n)")
        pos_cmp = sb("pos_cmp", [P, 2, 16])
        cmask = sb("cmask", [P, 2, TT, NCMP])
        gates = sb("gates", [P, TT, 48])
        gel = att[:, 0:24 * NCMP].rearrange("p (a i c) -> p a i c", a=3, i=2)
        c_stat = sb("c_stat", [P, TT, HEADS])
        lat = extra[:, 0:TT * 704].rearrange("p (t c) -> p t c", t=TT)
        qpe_tok = extra[:, 2048:3072].rearrange("p (t h c) -> p t h c", t=TT, c=64)
        lq = bias1[:, 0:TT * 1536].rearrange("p (t h c) -> p t h c", t=TT, c=192)
        lk = xn[:, :, :].rearrange("p t (h c) -> p t h c", c=P)
        qpe_t = extra[:, 3072:4096].rearrange("p (h t) -> p h t", t=T)
        kpe_t = gate_row[:, 384:640]
        bias2 = bias1[:, 0:8 * STRIP].rearrange("p (h c) -> p h c", c=STRIP)
        dist = extra[:, 0:384]
        ge = extra[:, 384:1152].rearrange("p (i c) -> p i c", i=2)
        bias_term = extra[:, 3072:3072 + POOL_HEADS * STRIP].rearrange("p (i c) -> p i c", c=STRIP)
        onehot = extra[:, 1152:1920].rearrange("p (i c) -> p i c", i=2)
        pos_i = extra[:, 0:T + TT].bitcast(I32)
        pos_h = extra[:, 512:512 + 2 * (T + TT)].rearrange("p (i c) -> p i c", i=2).bitcast(I32)
        pos_f = sb("pos_f", [P, 2, T + TT])
        pos_q = sb("pos_q", [P, TT])
        table2 = cmp_w2[:, :, :, :].rearrange("p s i d -> p (s i d)")
        inv_freq = sb("inv_freq", [P, 32])
        trig = sb("trig", [P, 2, TT, 32])
        ang = att[:, 1408:1536].rearrange("p (i t c) -> p i t c", i=2, t=TT)
        pe_gain = k_cmp[:, :, :].rearrange("p g n -> p (g n)").rearrange("p (i c) -> p i c", i=2)
        kpe_n = gate_row[:, 0:128].rearrange("p (t c) -> p t c", t=TT)
        kpe_tok = gate_row[:, 128:384].rearrange("p (t i c) -> p t i c", t=TT, i=2)

        def lq_nope(t, h):
            return lq[:, t, h, 0:P]

        def lk_nope(t, h):
            return lk[:, t, h, :]

        bank = ctx.enter_context(nc.psum_tensor("bank", [P, BANKS, W], F32))
        ps_s = ctx.enter_context(nc.psum_tensor("ps_s", [P, 2, W], F32))
        ps_p = ctx.enter_context(nc.psum_tensor("ps_p", [P, 2, W], F32))

        bias_stash = nc.dram_tensor("bias_stash", [P, 4 * STRIP], F32, kind="Internal").ap()
        bias_scratch = nc.dram_tensor("bias_scratch", [HEADS, 384], F32, kind="Internal").ap()

        load_in = [sem(f"load_in{i}") for i in range(SLOTS)]
        filled = [sem(f"filled{i}") for i in range(BANKS)]
        drained = [sem(f"drained{i}") for i in range(BANKS)]
        matvec_done = sem("matvec_done")
        mod_drained = sem("mod_drained")
        hi_ready = sem("hi_ready")
        lo_ready = sem("lo_ready")
        pieces_read = sem("pieces_read")
        read_end = []
        x_ready = sem("x_ready")
        ss_ready = sem("ss_ready")
        rstd_ready = sem("rstd_ready")
        freed = {}

        def loaded(i):
            (k0, k1), (n0, n1) = loads[i][1:]
            return wring[:, i % SLOTS, 0:(k1 - k0) * (n1 - n0)].rearrange("p (k n) -> p k n", n=n1 - n0)

        def load_wait(eng, i):
            eng.wait_ge(load_in[i % SLOTS], 16 * (i // SLOTS + 1))

        NORMS = ["a0", "m0", "kv", "m1", "l", "m2", "o", "m3"]

        uses = {}
        piece_of = {}
        n_uses = [0]
        owed = [0] * BANKS

        def bank_take(pe, key, readers=1):
            b = n_uses[0] % BANKS
            if owed[b]:
                pe.wait_ge(drained[b], owed[b])
            owed[b] += readers
            uses[key] = (b, n_uses[0] // BANKS + 1, owed[b])
            piece_of[key] = len(read_end) - 1
            n_uses[0] += 1
            return b

        def piece_view(buf, p):
            _, (k0, k1), (n0, n1) = pieces[p]
            return buf[:, p % PIECES, 0:(k1 - k0) * (n1 - n0)].rearrange("p (k n) -> p k n", n=n1 - n0)

        def raw_view(p):
            return loaded(piece_load[p])

        next_split = {}
        split = {}
        held = dict.fromkeys(("act", "dve"), first_piece[("a_out", 0)])

        def keep_ahead(who, p, n=PIECES):
            while p >= 0 and next_split[who] < min(p + n, held.get(who, len(pieces))):
                split[who](next_split[who])
                next_split[who] += 1

        def last_of(key):
            return first_piece[key] + len(chunk_of[key][4]) - 1

        def bank_full(eng, key):
            if eng.engine in (mybir.EngineType.Activation, mybir.EngineType.DVE):
                keep_ahead("act" if eng.engine == mybir.EngineType.Activation else "dve", piece_of[key])
            b, n, _ = uses[key]
            eng.wait_ge(filled[b], n)
            return bank[:, b, :]

        def bank_emptied(eng, key):
            b, _, n = uses[key]
            eng.wait_ge(drained[b], n)

        ada_order = [k for k, *_ in plan if k[0].startswith("ada")]
        early = (ada_order[9:12], [extra[:, i * W:(i + 1) * W] for i in range(3)], extra[:, 4 * W:5 * W])
        late = (ada_order[22:28], [xn[:, i // 2, (i % 2) * W:(i % 2 + 1) * W] for i in range(4)]
                + [acc[:, 1, :], acc[:, 2, :]], acc[:, 0, :])

        LATE_UNITS = (3, 5, 7, 9, 11, 13)

        def ada_index(key):
            return ada_order.index(key)

        def matvec_index(key):
            return [k for k in ada_order if k not in early[0] + late[0]].index(key)


        block = ctx.enter_context(nc.Block())

        @block.tensor
        def _(pe):
            def mod_columns(key):
                i = matvec_index(key)
                b = bank_take(pe, ("mod", key))
                pe.wait_ge(matvec_done, i + 1)
                for j in range(4):
                    last = nc.tensor.matmul(bank[:, b, j:j + 1], acc[:, i % 3, j * P:(j + 1) * P], ones[:, 0:1],
                                            start=True, stop=True)
                last.then_inc(filled[b], 1)

            def pool_columns(all_sums, key, total):
                b = bank_take(pe, key)
                pe.wait_ge(sem("pool_matvec"), total)
                for c, sums in enumerate(all_sums):
                    for j in range(4):
                        last = nc.tensor.matmul(bank[:, b, 4 * c + j:4 * c + j + 1], sums[:, j * P:(j + 1) * P],
                                                ones[:, 0:1], start=True, stop=True)
                last.then_inc(filled[b], 1)

            def turn(name, t, src=xn, tiles=KT):
                for half in range(2):
                    key = (name, "turn", 2 * t + half)
                    b = bank_take(pe, key)
                    piece_of[key] = -1
                    for i in range(min(4, tiles - 4 * half)):
                        j = 4 * half + i
                        last = nc.tensor.transpose(bank[:, b, i * P:(i + 1) * P], src[:, t, j * P:(j + 1) * P],
                                                   ident[:, :])
                    last.then_inc(filled[b], 1)

            def turn_normed(name, t, outs=1):
                pe.wait_ge(sem("normed"), TT * NORMS.index(name) + t + 1)
                turn(name, t)
                turned(name, t, outs)

            def turn_both(name, outs=1):
                for t in range(TT):
                    pe.wait_ge(sem("normed"), TT * NORMS.index(name) + t + 1)
                    turn(name, t)
                turned(name, TT - 1, outs)

            def turned(name, t, outs=1):
                pe.wait_ge(sem(f"{name}_split"), 2 * (t + 1) * outs)

            def piece_wait(ahead=0):
                pe.wait_ge(lo_ready, len(read_end) + 1 + ahead)
                return len(read_end) + ahead

            def piece_over(ins, bank_use=None):
                if bank_use is None:
                    n_read[0] += 1
                    ins.then_inc(pieces_read, 1)
                    read_end.append((pieces_read, n_read[0]))
                else:
                    b, n, _ = uses[bank_use]
                    ins.then_inc(filled[b], 1)
                    read_end.append((filled[b], n))

            n_read = [0]

            def product(out, left, right, first, last):
                (lh, ll), (rh, rl) = left, right
                nc.tensor.matmul(out, lh, rh, start=first, stop=False)
                nc.tensor.matmul(out, lh, rl, start=False, stop=False)
                return nc.tensor.matmul(out, ll, rh, start=False, stop=last)

            def by_feature(key, src, n, name=None):
                for g in range(n // T):
                    use = (name or key, g) if name else key + (g,)
                    b = bank_take(pe, use)
                    for i in range(2):
                        p = piece_wait()
                        wh, wl = piece_view(whi, p), piece_view(wlo, p)
                        for k in range(KT):
                            last = product(bank[:, b, i * T:(i + 1) * T], (wh[:, k, :], wl[:, k, :]),
                                           (src[0][:, k, :], src[1][:, k, :]), k == 0, k == KT - 1)
                        piece_over(last, use if i else None)
                    piece_of[use] = p

            def by_token(key, src, kt, readers=1, first_k=0, between=None, apart=False):
                uses_ = [key + ("tok", t) for t in range(TT)]
                banks = [bank_take(pe, use, readers) for use in uses_]
                p0 = len(read_end)

                def part(t, p):
                    wh, wl = piece_view(whi, p), piece_view(wlo, p)
                    k0, k1 = pieces[p][1]
                    for k in range(k0, k1):
                        at = (slice(None), first_k + k, slice(t * P, (t + 1) * P))
                        last = product(bank[:, banks[t], 0:wh.shape[2]], (src[0][at], src[1][at]),
                                       (wh[:, k - k0, :], wl[:, k - k0, :]), k == 0, k == kt - 1)
                    return last, k1 == kt

                if apart or between:
                    for t in range(TT):
                        if t and between:
                            between()
                        piece_of[uses_[t]] = p0
                        end, j = False, 0
                        while not end:
                            p = piece_wait(0 if t else j)
                            last, end = part(t, p)
                            if t:
                                piece_over(last, uses_[t] if end else None)
                            elif end:
                                last.then_inc(filled[banks[t]], 1)
                            j += 1
                    return
                end = False
                while not end:
                    p = piece_wait()
                    for t in range(TT):
                        last, end = part(t, p)
                        if end:
                            piece_of[uses_[t]] = p
                            if t == 0:
                                last.then_inc(filled[banks[0]], 1)
                    piece_over(last, uses_[1] if end else None)

            def gate_rows(name, first):
                pe.wait_ge(mod_drained, first // 4 + 2)
                for g in range(2):
                    b = bank_take(pe, (name, "gate", g))
                    for j in range(4):
                        c = first + 4 * g + j
                        last = nc.tensor.matmul(bank[:, b, j * P:(j + 1) * P], mod[:, c:c + 1].to_broadcast([P, P]),
                                                ident[:, :], start=True, stop=True)
                    last.then_inc(filled[b], 1)

            def attention(name, units, q_parts, pairs, v, dv, beside=None):
                outs = units // 2 if pairs else units
                scored, biased = sem(f"{name}_scored"), sem(f"{name}_biased")
                weights, turned_, copied = sem(f"{name}_weights"), sem(f"{name}_turned"), sem(f"{name}_copied")

                def scores(u):
                    if u >= 2:
                        pe.wait_ge(biased, u - 1)
                    parts = q_parts(u)
                    for t in range(TT):
                        lo, n = (0, P) if t == 0 else (P, T)
                        for i, (q, k) in enumerate(parts):
                            last = nc.tensor.matmul(ps_s[:, u % 2, lo:lo + n], q[:, t * P:(t + 1) * P], k[:, 0:n],
                                                    start=(i == 0), stop=(i == len(parts) - 1))
                    last.then_inc(scored, 1)

                def turns(v_):
                    if pairs:
                        pe.wait_ge(weights, v_ + 1)
                    else:
                        pe.wait_ge(sem(f"{name}_exped"), 2 * v_ + 2)
                    if v_ >= 2:
                        pe.wait_ge(copied, v_ - 1)
                    e = (2 * v_ if pairs else v_) % ATT
                    for i in range(3):
                        last = nc.tensor.transpose(ps_p[:, v_ % 2, i * P:(i + 1) * P], ex[:, e, i * P:(i + 1) * P],
                                                   ident[:, :])
                    last.then_inc(turned_, 1)

                def mix(v_):
                    pe.wait_ge(copied, v_ + 1)
                    b = bank_take(pe, (name, "o", v_))
                    vv = v(v_)
                    p_ = pt[:, v_ % 2, :]
                    nc.tensor.matmul(bank[:, b, 0:dv], p_[:, 0:P], vv[:, 0, :], start=True, stop=True)
                    nc.tensor.matmul(bank[:, b, dv:2 * dv], p_[:, P:2 * P], vv[:, 0, :], start=True, stop=False)
                    nc.tensor.matmul(bank[:, b, dv:2 * dv], p_[:, 2 * P:3 * P], vv[:, 1, :], start=False,
                                     stop=True).then_inc(filled[b], 1)

                if pairs:
                    for h in range(outs + 2):
                        if h < outs:
                            scores(2 * h)
                            scores(2 * h + 1)
                        if 1 <= h <= outs:
                            turns(h - 1)
                        if h >= 2:
                            mix(h - 2)
                else:
                    for u in range(units + 2):
                        if u < units:
                            scores(u)
                        if 1 <= u <= units:
                            turns(u - 1)
                        if u >= 2:
                            mix(u - 2)
                        if beside:
                            beside(u)

            def out_product(name, key):
                if name == "diff":
                    pe.wait_ge(sem("diff_o_ready"), 1)
                else:
                    bank_emptied(pe, ("win", "o", HEADS - 1) if name == "nsa" else (name, "o", 7))
                turn(f"{name}_o", 0, o_tok)
                turned(f"{name}_o", 0)

                def second():
                    if name == "diff":
                        pe.wait_ge(sem("diff_o_ready"), 2)
                    turn(f"{name}_o", 1, o_tok)
                    turned(f"{name}_o", 1)

                by_token((key, 0), (h_hi, h_lo), KT, between=second)
                by_token((key, 1), (h_hi, h_lo), KT, apart=True)

            def mlp(tag, ada=(), before_last=None):
                ada = list(ada)
                y = [ps_s[:, 0, :], ps_s[:, 1, :], ps_p[:, 0, :], ps_p[:, 1, :]]

                def up(c):
                    by_feature((f"{tag}_w1", c), (h_hi, h_lo), W)

                def down_part(c, k, p, t, n):
                    wh, wl = piece_view(whi, p), piece_view(wlo, p)
                    g = (slice(None), c % 2, k, slice(t * P, (t + 1) * P))
                    cols = slice(n * W, (n + 1) * W)
                    return product(y[2 * t + n], (g_hi[g], g_lo[g]), (wh[:, 0, cols], wl[:, 0, cols]),
                                   c == 0 and k == 0, c == 7 and k == 3)

                def down(c):
                    pe.wait_ge(sem("mlp_glo"), 16 * int(tag[1]) + 2 * c + 2)
                    if c < 7:
                        for k in range(4):
                            p = piece_wait()
                            for t in range(TT):
                                for n in range(2):
                                    last = down_part(c, k, p, t, n)
                            piece_over(last)
                        return
                    for t in range(TT):
                        for k in range(4):
                            p = piece_wait(0 if t else k)
                            for n in range(2):
                                last = down_part(c, k, p, t, n)
                                if k == 3:
                                    last.then_inc(sem("mlp_y"), 1)
                            if t and k < 3:
                                piece_over(last)
                    read_end.append((sem("mlp_y"), 4 * int(tag[1]) + 4))

                def ride():
                    if ada:
                        mod_columns(ada.pop(0))

                turn_both(tag)
                up(0)
                for c in range(1, 8):
                    up(c)
                    ride()
                    down(c - 1)
                    ride()
                assert not ada
                if before_last:
                    before_last()
                down(7)

            pe.wait_ge(sem("const_in"), 16 * 5)
            pe.wait_ge(sem("param_in"), 16 * 2)
            b = bank_take(pe, "params")
            nc.tensor.transpose(bank[:, b, 0:P], prow[:, 0, :], ident[:, :])
            nc.tensor.transpose(bank[:, b, P:n_cols], prow[0:n_cols - P, 1, :],
                                ident[0:n_cols - P, 0:n_cols - P]).then_inc(filled[b], 1)
            pe.wait_ge(sem("table_in"), 32)
            b = bank_take(pe, "bias_rows")
            nc.tensor.matmul(bank[0:HEADS, b, 0:384], sc[0:BUCKETS, 0, 0:HEADS], sc[0:BUCKETS, 1, :], start=True,
                             stop=True).then_inc(filled[b], 1)
            for c in range(4):
                mod_columns(("ada0", c))
            h = (h_hi, h_lo)
            turn_both("a0")
            for c in range(6):
                if c < 4:
                    by_feature(("a_in", c), h, W)
                else:
                    by_token(("a_in", c), h, KT)
                if c:
                    mod_columns(("ada0", 3 + c))
                if c < 4:
                    pe.wait_ge(sem("bias_back"), 16)
                    if c >= 2:
                        pe.wait_ge(sem("bias_copied"), 2 * c - 2)
                    for j in range(4):
                        last = nc.tensor.matmul((ps_s, ps_p)[c % 2][:, j // 2, (j % 2) * T:(j % 2 + 1) * T], flip,
                                                bias1_v[:, 4 * c + j, :], start=True, stop=True)
                    last.then_inc(sem("bias_turned"), 1)
            gate_rows("a0", 16)
            for t in range(TT):
                for c in (4, 5):
                    bank_emptied(pe, ("a_in", c, "tok", t))

            def diff_q(u):
                h, m = u // 2, u % 2
                return [(q_t[64 * m:64 * m + 64, h, :], k_t[64 * m:64 * m + 64, h, :])]

            attention("diff", 16, diff_q, True, lambda v_: v_tok[:, :, v_ * P:(v_ + 1) * P], P)
            pool_columns(early[1], "early_mod", 3)
            out_product("diff", "a_out")

            mlp("m0", ada_order[12:22], lambda: gate_rows("m0", 40))

            turn_both("kv", 2)
            h_kv = (hk_hi, hk_lo)
            by_feature(("w_kv", 0), h_kv, W)
            by_feature(("w_kv", 1), h_kv, T, name="k_slc")
            by_token(("w_kv", 1), h_kv, KT)
            by_feature(("w_kv", 2), h_kv, T, name="k_win")
            by_token(("w_kv", 2), h_kv, KT)
            for s in range(2):
                first = first_load[("cmp_w1", s)]
                for i in range(4):
                    load_wait(pe, first + i)
                pe.wait_ge(sem("blocks_ready"), s + 1)
                b = bank_take(pe, ("cmp_hidden", s))
                for ht in range(2):
                    for l in range(16):
                        last = nc.tensor.matmul(bank[:, b, ht * 64:ht * 64 + 4 * NCMP],
                                                loaded(first + l // 4)[:, l % 4, ht * P:(ht + 1) * P],
                                                blocks[:, l, :], start=(l == 0), stop=(l == 15))
                last.then_inc(filled[b], 1)
                for i in range(4):
                    freed[first + i] = (filled[b], uses[("cmp_hidden", s)][1])
            pe.wait_ge(sem("cmp_act"), 2)
            pe.wait_ge(sem("cmp_w2_in"), 16)
            b = bank_take(pe, "k_cmp")
            for ht in range(2):
                for rep in range(2):
                    last = nc.tensor.matmul(bank[64 * rep:64 * rep + 64, b, 0:P], cmp_w2[:, 0, ht, :],
                                            cmp_hid[:, 0, ht, :], start=(ht == 0), stop=(ht == 1),
                                            skip_group_check=True)
            last.then_inc(filled[b], 1)
            b = bank_take(pe, "v_cmp")
            for g in range(4):
                for ht in range(2):
                    hid = cmp_hid[:, 1, ht, g * 32:(g + 1) * 32]
                    for r in range(4):
                        last = nc.tensor.matmul(bank[32 * r:32 * r + 32, b, g * 64:(g + 1) * 64], hid,
                                                cmp_w2[:, 1, ht, :], start=(ht == 0), stop=(ht == 1),
                                                skip_group_check=True)
            last.then_inc(filled[b], 1)

            for c in range(2):
                by_feature(("b_in", c), h, W)
            by_token(("b_in", 2), h, KT)
            gate_rows("n1", 64 + 16)
            for c in range(2):
                for g in range(2):
                    bank_emptied(pe, ("b_in", c, g))
            bank_emptied(pe, "k_cmp")
            for m in range(2):
                b = bank_take(pe, ("cmp_scores", m), TT)
                for t in range(TT):
                    for j in range(HEADS // 2):
                        at = (t * (HEADS // 2) + j) * 16
                        last = nc.tensor.matmul(bank[:, b, at:at + NCMP],
                                                q_t[64 * m:64 * m + 64, j, t * P:(t + 1) * P],
                                                k_cmp[64 * m:64 * m + 64, j // 2, 0:NCMP], start=True, stop=True)
                last.then_inc(filled[b], 1)
            pe.wait_ge(sem("cmp_weights"), 1)
            for t in range(TT):
                b = bank_take(pe, ("cmp_turn", t))
                for g in range(4):
                    last = nc.tensor.transpose(bank[:, b, g * P:(g + 1) * P], p_cmp[:, t, g, :], ident[:, :])
                last.then_inc(filled[b], 1)
            bank_emptied(pe, "v_cmp")
            pe.wait_ge(sem("v_cmp_ready"), 1)
            for t in range(TT):
                bank_emptied(pe, ("cmp_turn", t))
                for half in range(2):
                    b = bank_take(pe, ("cmp_o", t, half))
                    for g in range(2):
                        last = nc.tensor.matmul(bank[:, b, g * T:(g + 1) * T], pt_cmp[:, t, 2 * half + g, :],
                                                v_cmp[:, 2 * half + g, :], start=True, stop=True)
                    last.then_inc(filled[b], 1)

            def nsa_q(which):
                def parts(u):
                    lo = 64 * (u % 2)
                    return [(q_t[lo:lo + 64, u // 2, :], k_nsa[lo:lo + 64, which, u // 4, :])]
                return parts

            def late_columns(u):
                if u in LATE_UNITS:
                    c = LATE_UNITS.index(u)
                    pool_columns(late[1][c:c + 1], ("late_mod", c), 4 + c)

            for which, name in enumerate(("slc", "win")):
                attention(name, HEADS, nsa_q(which), False,
                          lambda v_, w_=which: v_nsa[:, w_, :, (v_ // 4) * 64:(v_ // 4) * 64 + 64], 64,
                          late_columns if name == "win" else None)
            out_product("nsa", "b_out")
            mlp("m1", before_last=lambda: gate_rows("m1", 64 + 40))

            turn_normed("l", 0)
            for c in range(2):
                by_token(("l_in", c), h, KT, between=None if c else lambda: turn_normed("l", 1))
            pe.wait_ge(sem("latent_normed"), 1)
            for t in range(TT):
                turn("latent", t, lat, 5)
                turned("latent", t)
            for c in range(3):
                by_token(("l_uq", c), h, 3)
            for c in range(4):
                by_token(("l_ukv", c), h, 2, readers=2, first_k=3)
            b = bank_take(pe, "kpe_turn")
            pe.wait_ge(sem("kpe_ready"), 1)
            for t in range(TT):
                last = nc.tensor.transpose(bank[:, b, t * P:(t + 1) * P],
                                           kpe_tok[:, t, :, :].rearrange("p i c -> p (i c)"), ident[:, :])
            last.then_inc(filled[b], 1)
            for what, n_h, ready in (("q", 8, "lq_normed"), ("k", 8, "lk_normed")):
                pe.wait_ge(sem(ready), 1)
                src = lq_nope if what == "q" else lk_nope
                for g in range(4):
                    b = bank_take(pe, ("l_turn", what, g))
                    for i in range(2):
                        for t in range(TT):
                            last = nc.tensor.transpose(bank[:, b, i * T + t * P:i * T + t * P + P],
                                                       src(t, 2 * g + i), ident[:, :])
                    last.then_inc(filled[b], 1)
            pe.wait_ge(sem("qpe_ready"), 1)
            for g in range(2):
                b = bank_take(pe, ("qpe_turn", g))
                for i in range(2):
                    for t in range(TT):
                        j = 2 * g + i
                        last = nc.tensor.transpose(bank[:, b, i * T + t * P:i * T + t * P + P],
                                                   qpe_tok[:, t, 2 * j:2 * j + 2, :].rearrange("p h c -> p (h c)"),
                                                   ident[:, :])
                last.then_inc(filled[b], 1)
            for what in "qk":
                for g in range(4):
                    bank_emptied(pe, ("l_turn", what, g))
            for g in range(2):
                bank_emptied(pe, ("qpe_turn", g))
            bank_emptied(pe, "kpe_turn")
            for c in range(4):
                for t in range(TT):
                    bank_emptied(pe, ("l_ukv", c, "tok", t))
            attention("mla", 8, lambda u: [(q_t[:, u, :], k_t[:, u, :]),
                                           (qpe_t[64 * (u % 2):64 * (u % 2) + 64, u // 2, :],
                                            kpe_t[64 * (u % 2):64 * (u % 2) + 64, :])], False,
                      lambda v_: v_tok[:, :, v_ * P:(v_ + 1) * P], P)
            out_product("mla", "l_o")
            mlp("m2")

            turn_normed("o", 0)
            for c in range(4):
                by_token(("o_qkv", c), h, KT, readers=2, between=None if c else lambda: turn_normed("o", 1))
            for c in range(4, 6):
                by_token(("o_qkv", c), h, KT)
            for what in "qk":
                pe.wait_ge(sem(f"o{what}_normed"), 1)
                src = xn if what == "q" else o_tok
                for g in range(4):
                    b = bank_take(pe, ("o_turn", what, g))
                    for i in range(2):
                        for t in range(TT):
                            j = 2 * g + i
                            last = nc.tensor.transpose(bank[:, b, i * T + t * P:i * T + t * P + P],
                                                       src[:, t, j * P:(j + 1) * P], ident[:, :])
                    last.then_inc(filled[b], 1)
            for what in "qk":
                for g in range(4):
                    bank_emptied(pe, ("o_turn", what, g))
            for c in (4, 5):
                for t in range(TT):
                    bank_emptied(pe, ("o_qkv", c, "tok", t))
            attention("moba", 8, lambda u: [(q_t[:, u, :], k_t[:, u, :])], False,
                      lambda v_: v_tok[:, :, v_ * P:(v_ + 1) * P], P)
            out_product("moba", "o_o")
            mlp("m3")

        rstd_calls = []
        hidden = ex[:, :, :].rearrange("p a c -> p (a c)").rearrange("p (b c) -> p b c", c=W)

        def whole(g, o):
            if o:
                return arena[:, g * W:(g + 1) * W].rearrange("p (i t) -> p i t", t=P)
            return xn[:, g // 2, (g % 2) * W:(g % 2 + 1) * W].rearrange("p (i t) -> p i t", t=P)

        def tile_part(g, n):
            return slice(None), slice(4 * (g % 2), 4 * (g % 2) + n), slice((g // 2) * P, (g // 2 + 1) * P)

        rstd_at = {}

        @block.vector
        def _(dve):
            done = sem("dve_done")
            n_done = [0]

            def link(ins):
                ins.then_inc(done, 1)
                n_done[0] += 1

            def settle():
                dve.wait_ge(done, n_done[0])

            v = nc.vector

            def signal(name):
                settle()
                v.memset(stat[:, 0:1], 0.0).then_inc(sem(name), 1)

            def split_low(p):
                if p >= PIECES:
                    dve.wait_ge(*read_end[p - PIECES])
                dve.wait_ge(hi_ready, p + 1)
                v.tensor_tensor(piece_view(wlo, p), raw_view(p), piece_view(whi, p).bitcast(F32),
                                ALU.subtract).then_inc(lo_ready, 1)
                freed[piece_load[p]] = (lo_ready, p + 1)

            next_split["dve"], split["dve"] = 0, split_low

            def matvec(key, k0=0, k1=KT):
                i = matvec_index(key)
                first = first_load[key]
                a = acc[:, i % 3, :]
                for k in range(k0, k1):
                    w = loaded(first + k // 2)[:, k % 2, :]
                    if k % 2 == 0:
                        load_wait(dve, first + k // 2)
                    settle()
                    if k == 0:
                        ins = v.tensor_scalar(a, w, c_col[:, 0:1], None, ALU.mult)
                    else:
                        ins = v.scalar_tensor_tensor(a, w, c_col[:, k:k + 1], a, ALU.mult, ALU.add)
                    if k < KT - 1:
                        link(ins)
                        if k % 2:
                            freed[first + k // 2] = (done, n_done[0])
                if k1 == KT:
                    ins.then_inc(matvec_done, 1)
                    freed[first + KT // 2 - 1] = (matvec_done, i + 1)

            def mod_drain(key):
                i = ada_index(key)
                name, c = key
                first = col[{"ada0": "ada_b0", "ada1": "ada_b1", "adakv": "kv_b"}[name]]
                src = bank_full(dve, ("mod", key))
                v.tensor_tensor(mod[:, 4 * i:4 * i + 4], src[:, 0:4], params[:, first + 4 * c:first + 4 * c + 4],
                                ALU.add).then_inc(drained[uses[("mod", key)][0]], 1)
                bank_emptied(dve, ("mod", key))
                v.memset(stat[:, 1:2], 0.0).then_inc(mod_drained, 1)

            def pool_drain(key, first, n, bias, bias_col):
                src = bank_full(dve, key)
                at = col[bias] + bias_col
                v.tensor_tensor(mod[:, 4 * first:4 * (first + n)], src[:, 0:4 * n], params[:, at:at + 4 * n],
                                ALU.add).then_inc(drained[uses[key][0]], 1)
                bank_emptied(dve, key)
                v.memset(stat[:, 1:2], 0.0).then_inc(mod_drained, n)

            def rstd(width, n, tag=None):
                k = len(rstd_calls)
                rstd_calls.append((width, n))
                if tag:
                    rstd_at[tag] = k
                return (k % 4) * 16

            def rstd_wait():
                dve.wait_ge(rstd_ready, len(rstd_calls))

            def gain(dst, name, scale_col):
                dve.wait_ge(mod_drained, scale_col // 4 + 2)
                link(v.tensor_scalar(dst[:, :], mod[:, scale_col:scale_col + KT], 1.0, None, ALU.add))
                settle()
                v.tensor_tensor(dst[:, :], dst[:, :], params[:, col[name]:col[name] + KT],
                                ALU.mult).then_inc(sem("gains_ready"), 1)

            def split_turned(name, t, outs, tiles=KT):
                for g in (2 * t, 2 * t + 1):
                    n = min(4, tiles - 4 * (g % 2))
                    for o, (hi, lo, gn, sh) in enumerate(outs):
                        f = whole(g, o)[:, 0:n, :]
                        part = tile_part(g, n)
                        if g % 2 == 0:
                            src = bank_full(dve, (name, "turn", g))
                            if gn is None:
                                ins = [v.tensor_copy(f, src[:, 0:n * P].rearrange("p (i t) -> p i t", t=P))]
                            else:
                                ins = [v.tensor_scalar(f[:, i, :], src[:, i * P:(i + 1) * P], gn[:, i:i + 1],
                                                       sh[:, i:i + 1] if sh is not None else None, ALU.mult,
                                                       *([ALU.add] if sh is not None else []))
                                       for i in range(n)]
                            for i in ins[:-1]:
                                link(i)
                            if o == len(outs) - 1:
                                ins[-1].then_inc(drained[uses[(name, "turn", g)][0]], 1)
                                bank_emptied(dve, (name, "turn", g))
                            else:
                                link(ins[-1])
                            settle()
                            link(v.tensor_copy(hi[part], f))
                            settle()
                        else:
                            dve.wait_ge(sem(f"{name}_high"), t * len(outs) + o + 1)
                        v.tensor_tensor(lo[part], f, hi[part].bitcast(F32), ALU.subtract).then_inc(
                            sem(f"{name}_split"), 1)

            def norm(name, outs, gains, done_with=None, last=None):
                def scale(t):
                    at = rstd(1, D, (name, t))
                    rstd_wait()
                    v.tensor_scalar(xn[:, t, :], x_res[:, t, :], rs[:, at:at + 1], None,
                                    ALU.mult).then_inc(sem("normed"), 1)

                if done_with:
                    done_with(0)
                if last is not None:
                    keep_ahead("dve", last - 2)
                if name == "l":
                    final(0)
                scale(0)
                if done_with:
                    done_with(1)
                if gains:
                    dve.wait_ge(sem("gains_ready"), gains)
                if name == "l":
                    final(1)
                split_turned(name, 0, outs)
                if last is not None and name in ("l", "o"):
                    keep_ahead("dve", last - 1)
                scale(1)
                if last is not None and name in ("l", "o"):
                    keep_ahead("dve", last + 1)
                split_turned(name, 1, outs)
                if last is not None:
                    keep_ahead("dve", last + 1)

            def final(t):
                at = rstd(1, D, ("final", t))
                rstd_wait()
                v.scalar_tensor_tensor(x_res[:, t, :], x_res[:, t, :], rs[:, at:at + 1], fn_row[:, :], ALU.mult,
                                       ALU.mult).then_inc(x_ready, 1)
                x_count[0] += 1

            def ahead(*keys):
                for key in keys:
                    for p in range(first_piece[key], first_piece[key] + len(chunk_of[key][4])):
                        keep_ahead("dve", p)

            def mlp(tag, ada=(), other=None, last=None):
                ada = list(ada)
                base = first_piece[(f"{tag}_w1", 0)]
                late = None

                def g_low(b):
                    dve.wait_ge(sem("mlp_sq"), 16 * int(tag[1]) + b + 1)
                    c, half = b // 2, b % 2
                    at = (slice(None), c % 2, slice(2 * half, 2 * half + 2))
                    v.tensor_tensor(g_lo[at], hidden[:, b % 3, :].rearrange("p (i t) -> p i t", t=T),
                                    g_hi[at].bitcast(F32), ALU.subtract).then_inc(sem("mlp_glo"), 1)

                for j in range(64):
                    p = base + j
                    if late is not None:
                        g_low(late)
                        late = None
                    key = pieces[p][0]
                    local = p - first_piece[key]
                    if key[0].endswith("w1") and local % 2:
                        late = 2 * key[1] + local // 2
                    if j < 4 * len(ada):
                        matvec(ada[j // 4], 2 * (j % 4), 2 * (j % 4) + 2)
                    keep_ahead("dve", min(p, base + 60))
                    if j < 4 * len(ada):
                        if j % 4 == 3 and j // 4 >= 2:
                            mod_drain(ada[j // 4 - 2])
                    if ada and j in (4 * len(ada) + 3, 4 * len(ada) + 7):
                        mod_drain(ada[j // 4 - 2])
                    if other:
                        other(j)
                if last:
                    last()

            x_count = [0]

            def y_residual(tag, gated, t):
                y = [ps_s[:, 0, :], ps_s[:, 1, :], ps_p[:, 0, :], ps_p[:, 1, :]]
                for n in range(2):
                    dve.wait_ge(sem("mlp_y"), 4 * int(tag[1]) + 2 * t + n + 1)
                    x_ = x_res[:, t, n * W:(n + 1) * W]
                    if gated:
                        link(v.tensor_tensor(tmp[:, n, :], y[2 * t + n], gate_row[:, n * W:(n + 1) * W], ALU.mult))
                        settle()
                        v.tensor_tensor(x_, tmp[:, n, :], x_, ALU.add).then_inc(x_ready, 1)
                    else:
                        v.tensor_tensor(x_, y[2 * t + n], x_, ALU.add).then_inc(x_ready, 1)
                    x_count[0] += 1
                    if gated:
                        dve.wait_ge(x_ready, x_count[0])

            def residual(key, t, n, gated):
                src = bank_full(dve, key)
                b = uses[key][0]
                x_ = x_res[:, t, n * W:(n + 1) * W]
                if gated:
                    v.tensor_tensor(tmp[:, t, :], src, gate_row[:, n * W:(n + 1) * W], ALU.mult).then_inc(drained[b], 1)
                    bank_emptied(dve, key)
                    v.tensor_tensor(x_, tmp[:, t, :], x_, ALU.add).then_inc(x_ready, 1)
                    x_count[0] += 1
                else:
                    v.tensor_tensor(x_, src, x_, ALU.add).then_inc(drained[b], 1)

            def gate(name):
                for g in range(2):
                    src = bank_full(dve, (name, "gate", g))
                    v.tensor_copy(gate_row[:, g * W:(g + 1) * W], src).then_inc(drained[uses[(name, "gate", g)][0]], 1)

            def gate_use(name):
                for g in range(2):
                    bank_emptied(dve, (name, "gate", g))

            def attention(name, units, bias, scale, pairs, output, beside=None):
                scored, biased, maxed = sem(f"{name}_scored"), sem(f"{name}_biased"), sem(f"{name}_maxed")
                exped, weights = sem(f"{name}_exped"), sem(f"{name}_weights")
                outs = units // 2 if pairs else units

                def scores(u):
                    dve.wait_ge(scored, u + 1)
                    if u >= 2:
                        dve.wait_ge(exped, 2 * u - 2)
                    s = sc[:, u % 2, :]
                    for lo, hi, b_ in bias(u):
                        ins = v.scalar_tensor_tensor(s[:, lo:hi], ps_s[:, u % 2, lo:hi], scale, b_, ALU.mult, ALU.add)
                    ins.then_inc(biased, 1)
                    dve.wait_ge(biased, u + 1)
                    v.tensor_reduce(nmax[:, u, 0:1], s[:, 0:P], AX, ALU.max, negate=True).then_inc(maxed, 1)
                    v.tensor_reduce(nmax[:, u, 1:2], s[:, P:STRIP], AX, ALU.max, negate=True).then_inc(maxed, 1)

                def combine(h):
                    dve.wait_ge(exped, 4 * h + 4)
                    link(v.reciprocal(rinv[:, 2 * h:2 * h + 2, :], rsum[:, 2 * h:2 * h + 2, :]))
                    settle()
                    link(v.scalar_tensor_tensor(rinv[:, 2 * h + 1, :], rinv[:, 2 * h + 1, :], lam[:, 3:4],
                                                rsum[:, 2 * h, :], ALU.mult, ALU.mult))
                    settle()
                    a, b_ = ex[:, (2 * h) % ATT, :], ex[:, (2 * h + 1) % ATT, :]
                    v.scalar_tensor_tensor(a[:, 0:P], b_[:, 0:P], rinv[:, 2 * h + 1, 0:1], a[:, 0:P], ALU.mult, ALU.add)
                    v.scalar_tensor_tensor(a[:, P:STRIP], b_[:, P:STRIP], rinv[:, 2 * h + 1, 1:2], a[:, P:STRIP],
                                           ALU.mult, ALU.add).then_inc(weights, 1)

                if pairs:
                    for h in range(outs + 2):
                        if h < outs:
                            scores(2 * h)
                            scores(2 * h + 1)
                        if 1 <= h <= outs:
                            combine(h - 1)
                        if h >= 2:
                            output(h - 2)
                else:
                    for u in range(units + 2):
                        if u < units:
                            scores(u)
                        if u >= 2:
                            output(u - 2)
                        if beside:
                            beside(u)

            def plain_output(name, outs, pairs):
                def output(h):
                    src = bank_full(dve, (name, "o", h))
                    b = uses[(name, "o", h)][0]
                    r = 2 * h if pairs else h
                    if not pairs:
                        link(v.reciprocal(rinv[:, r, :], rsum[:, r, :]))
                        settle()
                    for t in range(TT):
                        ins = v.tensor_scalar(o_tok[:, t, h * P:(h + 1) * P], src[:, t * P:(t + 1) * P],
                                              rinv[:, r, t:t + 1], None, ALU.mult)
                        if t == 0:
                            link(ins)
                    ins.then_inc(drained[b], 1)
                return output

            def head_scale(dst, src, at, t, heads, width):
                return v.tensor_tensor(dst, src, rs[:, at + t * heads:at + (t + 1) * heads]
                                       .unsqueeze(2).to_broadcast([P, heads, width]), ALU.mult)

            def bias_one(u):
                return [(0, P, bias1_v[:, u, P:T]), (P, STRIP, bias1_v[:, u, :])]

            v.memset(ones[:, :], 1.0).then_inc(sem("ones_set"), 1)
            dve.wait_ge(sem("silu_exp"), 1)
            link(v.tensor_scalar(c_tmp[:, :], c_tmp[:, :], 1.0, None, ALU.add))
            settle()
            link(v.reciprocal(c_tmp[:, :], c_tmp[:, :]))
            settle()
            link(v.tensor_tensor(c_col[:, :], c_tmp[:, :], c_raw[:, :], ALU.mult))
            settle()
            matvec(("ada0", 0))
            matvec(("ada0", 1))
            src = bank_full(dve, "params")
            v.tensor_copy(params[:, :], src[:, 0:n_cols]).then_inc(drained[uses["params"][0]], 1)
            bank_emptied(dve, "params")
            src = bank_full(dve, "bias_rows")
            dve.wait_ge(sem("const_in"), 16 * 5)
            v.tensor_tensor(ex[0:HEADS, 1, :], src[0:HEADS, 0:384], ex[0:HEADS, 0, :],
                            ALU.add).then_inc(drained[uses["bias_rows"][0]], 1)
            dve.wait_ge(sem("lam_in"), 16)
            link(v.tensor_tensor(lam_in[:, 0, :], lam_in[:, 0, :], lam_in[:, 1, :], ALU.mult))
            link(v.tensor_tensor(lam_in[:, 2, :], lam_in[:, 2, :], lam_in[:, 3, :], ALU.mult))
            settle()
            v.tensor_reduce(lam[:, 0:1], lam_in[:, 0, :], AX, ALU.add)
            v.tensor_reduce(lam[:, 1:2], lam_in[:, 2, :], AX, ALU.add).then_inc(sem("lam_dots"), 1)
            for c in range(1, 4):
                if c > 1:
                    matvec(("ada0", c))
                mod_drain(("ada0", c - 1))
            mod_drain(("ada0", 3))
            keep_ahead("dve", 0, 4)
            dve.wait_ge(sem("lam_exp"), 1)
            link(v.tensor_tensor(lam[:, 2:3], lam[:, 5:6], lam[:, 4:5], ALU.subtract))
            settle()
            link(v.tensor_scalar(lam[:, 3:4], lam[:, 2:3], LAM_INIT, None, ALU.subtract))
            gain(gs, "an0", 8)
            norm("a0", [(h_hi, h_lo, gs, mod[:, 0:8])], 1)
            for c in range(6):
                for i in range(4):
                    if c < 5:
                        matvec(("ada0", 4 + c), 2 * i, 2 * i + 2)
                    keep_ahead("dve", first_piece[("a_in", c)] + i)
                if c >= 2:
                    mod_drain(("ada0", 2 + c))
            mod_drain(("ada0", 8))
            gate("a0")
            dve.wait_ge(sem("bias_copied"), 8)
            attention("diff", 16, bias_one, 0.125, True, plain_output("diff", 8, True))
            held["dve"] = first_piece[("b_in", 0)]
            at = rstd(16, P)
            for t in range(TT):
                dve.wait_ge(sem("diff_squares"), t + 1)
                ins = v.tensor_reduce(ss[:, at + 8 * t:at + 8 * t + 8],
                                      xn[:, t, :].rearrange("p (h c) -> p h c", c=P), AX, ALU.add)
            ins.then_inc(ss_ready, 1)
            rstd_wait()
            for t in range(TT):
                o_ = o_tok[:, t, :].rearrange("p (h c) -> p h c", c=P)
                head_scale(o_, o_, at, t, 8, P).then_inc(sem("diff_o_ready"), 1)
            dve.wait_ge(sem("subln_ready"), 1)
            for t in range(TT):
                split_turned("diff_o", t, [(h_hi, h_lo, stat[:, 8:16], None)])
                if t == 0:
                    pool_drain("early_mod", 9, 3, "ada_b0", 36)
                keep_ahead("dve", first_piece[("a_out", 0)])
            gate_use("a0")
            keep_ahead("dve", first_piece[("a_out", 1)])
            gain(gs, "mn0", 32)
            for t in range(TT):
                residual(("a_out", 0, "tok", t), t, 0, True)
            norm("m0", [(h_hi, h_lo, gs, mod[:, 24:32])], 2,
                 lambda t: residual(("a_out", 1, "tok", t), t, 1, True), last_of(("a_out", 1)))
            mlp("m0", ada_order[12:22], last=lambda: (gate("m0"), gate_use("m0")))

            gain(gs, "an1", 64 + 8)
            gain(gs2, "kvn", 48 + 8)
            norm("kv", [(h_hi, h_lo, gs, mod[:, 64:72]), (hk_hi, hk_lo, gs2, mod[:, 48:56])], 4,
                 lambda t: y_residual("m0", True, t), last_of(("m0_w2", 7)))
            for s in range(2):
                src = bank_full(dve, ("w_kv", 0, s))
                for par in range(2):
                    for i in range(2):
                        for g in range(2):
                            d_ = kv_raw[64 * par:64 * par + 64, s, 2 * i + g, 0:T - par]
                            ins = v.tensor_copy(d_, src[64 * g:64 * g + 64, i * T + par:(i + 1) * T])
                            if (par, i, g) != (1, 1, 1):
                                link(ins)
                ins.then_inc(drained[uses[("w_kv", 0, s)][0]], 1)
                settle()
                bank_emptied(dve, ("w_kv", 0, s))
                dve.wait_ge(sem("pos_in"), 32)
                if s:
                    bank_full(dve, ("cmp_hidden", 0))
                for l in range(16):
                    b_ = blocks[:, l, :].rearrange("p (g n) -> p g n", g=4)
                    ins = v.tensor_scalar(b_, kv_raw[:, s, :, 2 * l:2 * l + 16 * (NCMP - 1) + 1:16],
                                          pos_cmp[:, s, l:l + 1], None, ALU.add)
                ins.then_inc(sem("blocks_ready"), 1)
            ahead(("w_kv", 1), ("w_kv", 2))
            for s in range(2):
                src = bank_full(dve, ("cmp_hidden", s))
                if s:
                    settle()
                else:
                    link(v.memset(cmp_hid[:, :, :, :], 0.0))
                    settle()
                x0 = gel[:, 0, :, :]
                v.tensor_copy(x0, src[:, 0:128].rearrange("p (i c) -> p i c", i=2)[:, :, 0:4 * NCMP]).then_inc(
                    drained[uses[("cmp_hidden", s)][0]], 1)
                bank_emptied(dve, ("cmp_hidden", s))
                link(v.tensor_scalar(gel[:, 2, :, :], x0, -9.0, None, ALU.max))
                settle()
                link(v.tensor_tensor(gel[:, 1, :, :], gel[:, 2, :, :], gel[:, 2, :, :], ALU.mult))
                settle()
                link(v.tensor_scalar(gel[:, 1, :, :], gel[:, 1, :, :], 0.044715, 1.0, ALU.mult, ALU.add))
                settle()
                v.tensor_tensor(gel[:, 1, :, :], gel[:, 1, :, :], gel[:, 2, :, :], ALU.mult).then_inc(sem("gelu_arg"), 1)
                dve.wait_ge(sem("gelu_exp"), s + 1)
                link(v.tensor_scalar(gel[:, 2, :, :], gel[:, 2, :, :], 1.0, None, ALU.add))
                settle()
                link(v.reciprocal(gel[:, 2, :, :], gel[:, 2, :, :]))
                settle()
                link(v.tensor_tensor(cmp_hid[:, s, :, :].rearrange("p i (g n) -> p i g n", g=4)[:, :, :, 0:NCMP],
                                     x0.rearrange("p i (g n) -> p i g n", g=4),
                                     gel[:, 2, :, :].rearrange("p i (g n) -> p i g n", g=4), ALU.mult))
                settle()
                signal("cmp_act")
            held["dve"] = first_piece[("b_out", 0)]
            link(v.memset(v_cmp[:, :, :], 0.0))
            link(v.memset(p_cmp[:, :, :, :], 0.0))
            src = bank_full(dve, "k_cmp")
            v.tensor_copy(k_cmp[:, :, :].rearrange("p g n -> p (g n)"), src[:, 0:P]).then_inc(
                drained[uses["k_cmp"][0]], 1)
            src = bank_full(dve, "v_cmp")
            settle()
            for r in range(4):
                rows = slice(32 * r, 32 * r + 32)
                ins = v.tensor_copy(v_cmp[rows, :, 64 * r:64 * r + 64], src[rows, 0:T].rearrange("p (g c) -> p g c", g=4))
                if r < 3:
                    link(ins)
            ins.then_inc(drained[uses["v_cmp"][0]], 1)
            bank_emptied(dve, "v_cmp")
            settle()
            signal("v_cmp_ready")
            dve.wait_ge(mod_drained, 22)
            ahead(("b_in", 0), ("b_in", 1), ("b_in", 2))
            for t in range(TT):
                bank_emptied(dve, ("b_in", 2, "tok", t))
            link(v.tensor_scalar(gates[:, :, :], gates[:, :, :], 1.0, None, ALU.add))
            settle()
            link(v.reciprocal(gates[:, :, :], gates[:, :, :]))
            gate("n1")
            gates_v = gates[:, :, :].rearrange("p t (h c) -> p t h c", c=3)
            for m in range(2):
                src = bank_full(dve, ("cmp_scores", m))[:, 0:256].rearrange("p (t j n) -> p t j n", t=TT, n=16)
                for t in range(TT):
                    v.scalar_tensor_tensor(s_cmp[:, t, m:HEADS:2, 0:NCMP], src[:, t, :, 0:NCMP], 0.125,
                                           cmask[:, 0, t, :].unsqueeze(1).to_broadcast([P, HEADS // 2, NCMP]),
                                           ALU.mult, ALU.add).then_inc(drained[uses[("cmp_scores", m)][0]], 1)
            for m in range(2):
                bank_emptied(dve, ("cmp_scores", m))
            s_ = s_cmp[:, :, :, 0:NCMP]
            e_ = s_cmp2[:, :, :, 0:NCMP]
            wide = [P, TT, HEADS, NCMP]
            link(v.tensor_reduce(c_stat[:, :, :], s_, AX, ALU.max))
            settle()
            v.tensor_tensor(s_, s_, c_stat[:, :, :].unsqueeze(3).to_broadcast(wide), ALU.subtract).then_inc(
                sem("cmp_centred"), 1)
            dve.wait_ge(sem("cmp_exped"), 1)
            link(v.tensor_reduce(c_stat[:, :, :], e_, AX, ALU.add))
            settle()
            link(v.reciprocal(c_stat[:, :, :], c_stat[:, :, :]))
            settle()
            for t in range(TT):
                link(v.tensor_tensor(e_[:, t], e_[:, t], cmask[:, 1, t, :].unsqueeze(1).to_broadcast(
                    [P, HEADS, NCMP]), ALU.mult))
            link(v.tensor_tensor(c_stat[:, :, :], c_stat[:, :, :], gates_v[:, :, :, 0], ALU.mult))
            settle()
            for t in range(TT):
                link(v.tensor_tensor(p_cmp[:, t, :, :].rearrange("p g (r n) -> p (g r) n", n=32)[:, :, 0:NCMP],
                                     e_[:, t], c_stat[:, t, :].unsqueeze(2).to_broadcast([P, HEADS, NCMP]), ALU.mult))
            settle()
            signal("cmp_weights")
            for t in range(TT):
                for half in range(2):
                    src = bank_full(dve, ("cmp_o", t, half))
                    v.tensor_copy(o_tok[:, t, half * W:(half + 1) * W], src).then_inc(
                        drained[uses[("cmp_o", t, half)][0]], 1)
            for t in range(TT):
                for half in range(2):
                    bank_emptied(dve, ("cmp_o", t, half))

            def nsa_output(name, c):
                def output(h):
                    src = bank_full(dve, (name, "o", h))
                    b = uses[(name, "o", h)][0]
                    link(v.reciprocal(rinv[:, h, :], rsum[:, h, :]))
                    settle()
                    link(v.tensor_tensor(rinv[:, h, :], rinv[:, h, :], gates_v[:, :, h, c], ALU.mult))
                    settle()
                    for t in range(TT):
                        o_ = o_tok[:, t, h * 64:(h + 1) * 64]
                        ins = v.scalar_tensor_tensor(o_, src[:, t * 64:(t + 1) * 64], rinv[:, h, t:t + 1], o_, ALU.mult,
                                                     ALU.add)
                        if t == 0:
                            link(ins)
                    ins.then_inc(drained[b], 1)
                return output

            def late_drain(u):
                if u in LATE_UNITS:
                    c = LATE_UNITS.index(u)
                    pool_drain(("late_mod", c), 22 + c, 1, "ada_b1", 24 + 4 * c)

            for c, name in ((1, "slc"), (2, "win")):
                attention(name, HEADS, bias_one, 0.125, False, nsa_output(name, c), late_drain if c == 2 else None)
                bank_emptied(dve, (name, "o", HEADS - 1))
                settle()
            del held["dve"]
            for t in range(TT):
                split_turned("nsa_o", t, [(h_hi, h_lo, None, None)])
                keep_ahead("dve", first_piece[("b_out", 0)])
            gate_use("n1")
            gain(gs, "mn1", 64 + 32)
            keep_ahead("dve", first_piece[("b_out", 1)])
            for t in range(TT):
                residual(("b_out", 0, "tok", t), t, 0, True)
            norm("m1", [(h_hi, h_lo, gs, mod[:, 64 + 24:64 + 32])], 5,
                 lambda t: residual(("b_out", 1, "tok", t), t, 1, True), last_of(("b_out", 1)))
            dve.wait_ge(sem("late_in"), 96)
            link(v.tensor_scalar(pos_h[:, 0, :], pos_i[:, :], 12, None, ALU.arith_shift_right))
            link(v.tensor_scalar(pos_h[:, 1, :], pos_i[:, :], 4095, None, ALU.bitwise_and))
            link(v.tensor_copy(pos_q[:, :], pos_i[:, T:T + TT]))
            settle()
            link(v.tensor_copy(pos_f[:, :, :], pos_h[:, :, :]))
            a_, n_ = ang[:, 0, :, :], ang[:, 1, :, :]
            for t in range(TT):
                link(v.tensor_scalar(a_[:, t, :], inv_freq[:, :], pos_q[:, t:t + 1], None, ALU.mult))
            magic = 1.5 * 2.0 ** 23
            for period in (TWO_PI * 4096, TWO_PI):
                settle()
                link(v.tensor_scalar(n_, a_, 1.0 / period, magic, ALU.mult, ALU.add))
                settle()
                link(v.tensor_scalar(n_, n_, magic, None, ALU.subtract))
                for part in pow2_split(period, 11, 4):
                    settle()
                    link(v.scalar_tensor_tensor(a_, n_, -part, a_, ALU.mult, ALU.add))
            settle()
            v.tensor_scalar(a_, a_, 3.1415925, -3.1415925, ALU.min, ALU.max).then_inc(sem("angles_ready"), 1)
            settle()
            def distances():
                for t in range(TT):
                    lo, n = (0, P) if t == 0 else (P, T)
                    link(v.tensor_scalar(dist[:, lo:lo + n], pos_f[:, 0, 0:n], pos_f[:, 0, T + t:T + t + 1], -4096.0,
                                         ALU.subtract, ALU.mult))
                    link(v.tensor_scalar(ge[:, 0, lo:lo + n], pos_f[:, 1, 0:n], pos_f[:, 1, T + t:T + t + 1], -1.0,
                                         ALU.subtract, ALU.mult))
                settle()
                link(v.tensor_tensor(dist, dist, ge[:, 0, :], ALU.add))
                settle()

            distances()
            starts = list(range(17)) + [math.ceil(16 * 64.0 ** (i / 16) - 1e-6) for i in range(1, 16)]

            def bucket(half, j):
                if j % 2:
                    return
                b_ = j // 2
                n = half * BUCKETS + b_
                oh = onehot[:, b_ % 2, :]
                if n >= 2:
                    dve.wait_ge(sem("bucket_used"), n - 1)
                if b_ == 0:
                    ins = v.tensor_scalar(oh, dist, float(starts[1]), None, ALU.is_lt)
                elif b_ < BUCKETS - 1:
                    link(v.tensor_scalar(ge[:, b_ % 2, :], dist, float(starts[b_ + 1]), None, ALU.is_lt))
                    settle()
                    ins = v.scalar_tensor_tensor(oh, dist, float(starts[b_]), ge[:, b_ % 2, :], ALU.is_ge, ALU.mult)
                else:
                    ins = v.tensor_scalar(oh, dist, float(starts[b_]), None, ALU.is_ge)
                ins.then_inc(sem("bucket_ready"), 1)
                dve.wait_ge(sem("bucket_ready"), n + 1)
                for h in range(4 * half + POOL_HEADS, 4 * half + 4):
                    link(v.scalar_tensor_tensor(bias2[:, h, :], oh, table2[:, b_ * 8 + h:b_ * 8 + h + 1],
                                                mask[:, :] if b_ == 0 else bias2[:, h, :], ALU.mult, ALU.add))
                settle()
            mlp("m1", other=lambda j: bucket(0, j), last=lambda: (gate("m1"), gate_use("m1")))
            dve.wait_ge(sem("bucket_used"), BUCKETS)
            signal("bias_half")

            dve.wait_ge(sem("final_in"), 16)
            norm("l", [(h_hi, h_lo, params[:, col["an2_0"]:col["an2_0"] + KT], None)], 0,
                 lambda t: y_residual("m1", True, t), last_of(("m1_w2", 7)))
            ahead(("l_in", 0), ("l_in", 1))
            segs = ((0, 384), (384, 640), (640, 704))
            ats = []
            for i, (a, b_) in enumerate(segs):
                ats.append(rstd(TT, b_ - a))
                if i == 2:
                    dve.wait_ge(rstd_ready, len(rstd_calls) - 2)
                sq = arena[:, 0:TT * 704].rearrange("p (t c) -> p t c", t=TT)
                if i == 0:
                    dve.wait_ge(sem("lat_squares"), TT)
                if i == 2:
                    for t in range(TT):
                        link(v.tensor_scalar(lat[:, t, 0:384], lat[:, t, 0:384], rs[:, ats[0] + t:ats[0] + t + 1], None,
                                             ALU.mult))
                    settle()
                v.tensor_reduce(ss[:, ats[i]:ats[i] + TT], sq[:, :, a:b_], AX, ALU.add).then_inc(ss_ready, 1)
            rstd_wait()
            for t in range(TT):
                link(v.tensor_scalar(lat[:, t, 384:640], lat[:, t, 384:640], rs[:, ats[1] + t:ats[1] + t + 1], None,
                                     ALU.mult))
                link(v.scalar_tensor_tensor(kpe_n[:, t, :], lat[:, t, 640:704], rs[:, ats[2] + t:ats[2] + t + 1],
                                            pe_gain[:, 1, :], ALU.mult, ALU.mult))
            settle()
            signal("latent_normed")
            for t in range(TT):
                split_turned("latent", t, [(h_hi, h_lo, params[:, col["qan"]:col["qan"] + 5], None)], 5)
            dve.wait_ge(sem("trig_ready"), 2)
            cos, sin = trig[:, 0, :, :], trig[:, 1, :, :]

            def rope(dst, src, shape, c_, s_, scratch):
                x1, x2 = src[..., 0:32], src[..., 32:64]
                for a, b_, op, to in ((x1, x2, ALU.subtract, 0), (x2, x1, ALU.add, 32)):
                    settle()
                    link(v.tensor_tensor(dst[..., to:to + 32], a, c_, ALU.mult))
                    link(v.tensor_tensor(scratch, b_, s_, ALU.mult))
                    settle()
                    link(v.tensor_tensor(dst[..., to:to + 32], dst[..., to:to + 32], scratch, op))
                settle()

            rope(kpe_tok[:, :, 0, :], kpe_n[:, :, :], None, cos, sin, ang[:, 1, :, :])
            link(v.tensor_copy(kpe_tok[:, :, 1, :], kpe_tok[:, :, 0, :]))
            signal("kpe_ready")
            ahead(("l_uq", 0), ("l_uq", 1), ("l_uq", 2))
            sq = arena[:, 0:3072].rearrange("p (t h c) -> p t h c", t=TT, c=192)
            dve.wait_ge(sem("lq_squares"), TT)
            at_n = rstd(16, P)
            v.tensor_reduce(ss[:, at_n:at_n + 16].rearrange("p (t h) -> p t h", t=TT), sq[:, :, :, 0:P], AX,
                            ALU.add).then_inc(ss_ready, 1)
            at_p = rstd(16, 64)
            v.tensor_reduce(ss[:, at_p:at_p + 16].rearrange("p (t h) -> p t h", t=TT), sq[:, :, :, P:192], AX,
                            ALU.add).then_inc(ss_ready, 1)
            rstd_wait()
            for t in range(TT):
                link(head_scale(lq[:, t, :, 0:P], lq[:, t, :, 0:P], at_n, t, 8, P))
            settle()
            signal("lq_normed")
            for t in range(TT):
                link(head_scale(lq[:, t, :, P:192], lq[:, t, :, P:192], at_p, t, 8, 64))
            settle()
            for t in range(TT):
                q_ = lq[:, t, :, P:192]
                link(v.tensor_tensor(q_, q_, pe_gain[:, 0, :].unsqueeze(1).to_broadcast([P, 8, 64]), ALU.mult))
            for t in range(TT):
                rope(qpe_tok[:, t], lq[:, t, :, P:192], None, cos[:, t, :].unsqueeze(1).to_broadcast([P, 8, 32]),
                     sin[:, t, :].unsqueeze(1).to_broadcast([P, 8, 32]),
                     tmp[:, 0, 0:256].rearrange("p (h c) -> p h c", c=32))
            signal("qpe_ready")
            ahead(*[("l_ukv", c) for c in range(4)])
            dve.wait_ge(sem("lk_squares"), TT)
            sq = extra[:, 0:2048].rearrange("p (t h c) -> p t h c", t=TT, c=P)
            at = rstd(16, P)
            v.tensor_reduce(ss[:, at:at + 16].rearrange("p (t h) -> p t h", t=TT), sq, AX, ALU.add).then_inc(ss_ready, 1)
            rstd_wait()
            for t in range(TT):
                link(head_scale(lk[:, t], lk[:, t], at, t, 8, P))
            settle()
            signal("lk_normed")
            attention("mla", 8, lambda u: [(0, STRIP, mask[:, :])], (P + 64) ** -0.5, False,
                      plain_output("mla", 8, False))
            for t in range(TT):
                split_turned("mla_o", t, [(h_hi, h_lo, None, None)])
                keep_ahead("dve", first_piece[("l_o", 0)])
            keep_ahead("dve", first_piece[("l_o", 1)])
            for t in range(TT):
                residual(("l_o", 0, "tok", t), t, 0, False)
            norm("m2", [(h_hi, h_lo, params[:, col["mn2_0"]:col["mn2_0"] + KT], None)], 0,
                 lambda t: residual(("l_o", 1, "tok", t), t, 1, False), last_of(("l_o", 1)))
            distances()
            mlp("m2", other=lambda j: bucket(1, j))
            dve.wait_ge(sem("bucket_used"), 2 * BUCKETS)

            norm("o", [(h_hi, h_lo, params[:, col["an2_1"]:col["an2_1"] + KT], None)], 0,
                 lambda t: y_residual("m2", False, t), last_of(("m2_w2", 7)))
            for what, src in (("q", xn), ("k", o_tok)):
                ahead(*[("o_qkv", c) for c in ((0, 1) if what == "q" else (2, 3))])
                sq = extra[:, 0:2048] if what == "q" else extra[:, 2048:4096]
                for c in range(2):
                    for t in range(TT):
                        bank_emptied(dve, ("o_qkv", c if what == "q" else 2 + c, "tok", t))
                at = rstd(16, P)
                v.tensor_reduce(ss[:, at:at + 16].rearrange("p (t h) -> p t h", t=TT),
                                sq.rearrange("p (t h c) -> p t h c", t=TT, c=P), AX, ALU.add).then_inc(ss_ready, 1)
                rstd_wait()
                for t in range(TT):
                    s_ = src[:, t, :].rearrange("p (h c) -> p h c", c=P)
                    link(head_scale(s_, s_, at, t, 8, P))
                settle()
                signal(f"o{what}_normed")
            ahead(("o_qkv", 4), ("o_qkv", 5))
            dve.wait_ge(sem("stash_back"), 16)
            attention("moba", 8, lambda u: [(0, STRIP, bias2[:, u, :])], P ** -0.5, False,
                      plain_output("moba", 8, False))
            for t in range(TT):
                split_turned("moba_o", t, [(h_hi, h_lo, None, None)])
                keep_ahead("dve", first_piece[("o_o", 0)])
            keep_ahead("dve", first_piece[("o_o", 1)])
            for t in range(TT):
                residual(("o_o", 0, "tok", t), t, 0, False)
            norm("m3", [(h_hi, h_lo, params[:, col["mn2_1"]:col["mn2_1"] + KT], None)], 0,
                 lambda t: residual(("o_o", 1, "tok", t), t, 1, False), last_of(("o_o", 1)))
            mlp("m3")
            for t in range(TT):
                y_residual("m3", False, t)

        @block.scalar
        def _(act):
            a = nc.scalar

            def row(v_, n):
                return v_.rearrange("(a n) -> a n", a=1)[0:1, 0:n].to_broadcast([P, n])

            act.wait_ge(sem("c_in"), 16)
            a.activation(c_tmp[:, :], c_raw[:, :], ACT.Exp, scale=-1.0).then_inc(sem("silu_exp"), 1)
            a.dma_start(prow[:, 0, :], dram["param_rows"][0:P]).then_inc(sem("param_in"), 16)
            a.dma_start(ident[:, :], dram["ident"]).then_inc(sem("const_in"), 16)
            a.dma_start(prow[0:n_cols - P, 1, :], dram["param_rows"][P:n_cols]).then_inc(sem("param_in"), 16)
            a.dma_start(flip, dram["flip"]).then_inc(sem("const_in"), 16)
            a.dma_start(mask[:, :], dram["mask"]).then_inc(sem("const_in"), 16)
            a.dma_start(ex[0:HEADS, 0, :], dram["negrow"]).then_inc(sem("const_in"), 16)
            a.dma_start(cmask[:, :, :, :], dram["cmask"].rearrange("p (a t n) -> p a t n", a=2, t=TT)).then_inc(
                sem("const_in"), 16)
            a.dma_start(sc[0:BUCKETS, 0, 0:HEADS], dram["rel_bias"]).then_inc(sem("table_in"), 16)
            a.dma_start(sc[0:BUCKETS, 1, :], dram["onehot"]).then_inc(sem("table_in"), 16)
            a.dma_start(lam_in[:, :, :].rearrange("p a b -> p (a b)"),
                        row(dram["a_lambda"].rearrange("l a b -> (l a b)"), 256)).then_inc(sem("lam_in"), 16)
            for t in range(TT):
                a.dma_start(x_res[:, t, :], dram["x"][0, t * P:(t + 1) * P, :]).then_inc(sem("x_in"), 16)
            act.wait_ge(sem("lam_dots"), 1)
            a.activation(lam[:, 4:6], lam[:, 0:2], ACT.Exp).then_inc(sem("lam_exp"), 1)
            bank_emptied(act, "bias_rows")
            a.dma_start(bias_scratch[:, :], ex[0:HEADS, 1, :]).then_inc(sem("bias_out"), 16)
            act.wait_ge(sem("bias_out"), 16)
            a.dma_start(bias1_v[:, :, :], bass.AP(tensor=bias_scratch.tensor, offset=0,
                                                       ap=[[1, P], [384, HEADS], [1, T]])).then_inc(sem("bias_back"), 16)
            a.dma_start(cmp_w2[:, :, :, :], dram["cmp_w2"].rearrange("s (i p) d -> p s i d", p=P)).then_inc(
                sem("cmp_w2_in"), 16)
            for par in range(2):
                a.dma_start(pos_cmp[64 * par:64 * par + 64, :, :],
                            dram["cmp_pos"].rearrange("s (l par) d -> par d s l", par=2)[par],
                            allow_slow_non_contiguous=True).then_inc(sem("pos_in"), 16)

            def square(src, dst, signal):
                a.activation(dst, src, ACT.Square).then_inc(signal, 1)

            def x_squares(name, t, ready=None, after=None):
                k = rstd_at[(name, t)]
                if ready:
                    act.wait_ge(x_ready, ready)
                if after:
                    bank_emptied(act, after)
                if k:
                    act.wait_ge(ss_ready, k)
                at = (k % 4) * 16
                a.activation(ps_s[:, :, :].rearrange("p a c -> p (a c)"), x_res[:, t, :], ACT.Square,
                             accum_out=ss[:, at:at + 1]).then_inc(ss_ready, 1)

            def split_high(p):
                load_wait(act, piece_load[p])
                if p >= PIECES:
                    act.wait_ge(*read_end[p - PIECES])
                a.activation(piece_view(whi, p), raw_view(p), ACT.Copy).then_inc(hi_ready, 1)

            next_split["act"], split["act"] = 0, split_high

            def ahead(*keys):
                for key in keys:
                    for p in range(first_piece[key], first_piece[key] + len(chunk_of[key][4])):
                        keep_ahead("act", p)

            def split_turned(name, t, outs, tiles=KT):
                g = 2 * t + 1
                n = tiles - 4
                for o, (hi, lo, gn, sh) in enumerate(outs):
                    f = whole(g, o)[:, 0:n, :]
                    src = bank_full(act, (name, "turn", g))
                    if gn is None:
                        ins = [a.activation(f, src[:, 0:n * P].rearrange("p (i t) -> p i t", t=P), ACT.Copy)]
                    elif sh is None:
                        ins = [a.activation(f[:, i, :], src[:, i * P:(i + 1) * P], ACT.Identity,
                                            scale=gn[:, 4 + i:5 + i]) for i in range(n)]
                    else:
                        ins = [a.activation(f[:, i, :], src[:, i * P:(i + 1) * P], ACT.Identity,
                                            scale=gn[:, 4 + i:5 + i], bias=sh[:, 4 + i:5 + i]) for i in range(n)]
                    if o == len(outs) - 1:
                        ins[-1].then_inc(drained[uses[(name, "turn", g)][0]], 1)
                        bank_emptied(act, (name, "turn", g))
                    else:
                        ins[-1].then_inc(sem("act_done"), 1)
                        n_act[0] += 1
                        act.wait_ge(sem("act_done"), n_act[0])
                    a.activation(hi[tile_part(g, n)], f, ACT.Copy).then_inc(sem(f"{name}_high"), 1)

            n_act = [0]

            def norm(name, outs, gains, ready=None, after=None, last=None):
                for t in range(TT):
                    x_squares(name, t, ready and ready[t], after and after(t))
                    if last is not None and (t == 0 or name == "o"):
                        keep_ahead("act", last - 2 + t)
                if gains:
                    act.wait_ge(sem("gains_ready"), gains)
                split_turned(name, 0, outs)
                if last is not None and name == "o":
                    keep_ahead("act", last + 1)
                split_turned(name, 1, outs)
                if last is not None:
                    keep_ahead("act", last + 1)

            def drain(key, dst, cols, scale=None, func=ACT.Copy):
                src = bank_full(act, key)
                ins = a.activation(dst, src[:, cols[0]:cols[1]], func) if scale is None else \
                    a.activation(dst, src[:, cols[0]:cols[1]], ACT.Identity, scale=scale)
                ins.then_inc(drained[uses[key][0]], 1)

            def attention(name, units, pairs):
                maxed, exped = sem(f"{name}_maxed"), sem(f"{name}_exped")
                turned_, copied = sem(f"{name}_turned"), sem(f"{name}_copied")
                outs = units // 2 if pairs else units

                def exps(u):
                    act.wait_ge(maxed, 2 * u + 2)
                    if u >= ATT:
                        act.wait_ge(turned_, (u - ATT) // 2 + 1 if pairs else u - ATT + 1)
                    for t in range(TT):
                        lo, hi = (0, P) if t == 0 else (P, STRIP)
                        a.activation(ex[:, u % ATT, lo:hi], sc[:, u % 2, lo:hi], ACT.Exp, bias=nmax[:, u, t:t + 1],
                                     accum_out=rsum[:, u, t:t + 1]).then_inc(exped, 1)

                def copy(v_):
                    act.wait_ge(turned_, v_ + 1)
                    if v_ >= 2:
                        bank_full(act, (name, "o", v_ - 2))
                    a.activation(pt[:, v_ % 2, :], ps_p[:, v_ % 2, 0:STRIP], ACT.Copy).then_inc(copied, 1)

                if pairs:
                    for h in range(outs + 1):
                        if h < outs:
                            exps(2 * h)
                            exps(2 * h + 1)
                        if h >= 1:
                            copy(h - 1)
                else:
                    for u in range(units + 1):
                        if u < units:
                            exps(u)
                        if u >= 1:
                            copy(u - 1)

            def mlp(tag):
                for b in range(2 * FF // W):
                    key = (f"{tag}_w1", b // 2, b % 2)
                    src = bank_full(act, key)
                    if b >= 3:
                        act.wait_ge(sem("mlp_glo"), 16 * int(tag[1]) + b - 2)
                    a.activation(hidden[:, b % 3, :], src, ACT.Relu).then_inc(drained[uses[key][0]], 1)
                    bank_emptied(act, key)
                    c, half = b // 2, b % 2
                    if c >= 2:
                        act.wait_ge(*read_end[first_piece[(f"{tag}_w2", c - 2)] + 3])
                    a.activation(g_hi[:, c % 2, 2 * half:2 * half + 2, :],
                                 hidden[:, b % 3, :].rearrange("p (i t) -> p i t", t=T),
                                 ACT.Square).then_inc(sem("mlp_ghi"), 1)
                keep_ahead("act", first_piece[(f"{tag}_w2", 7)])

            act.wait_ge(sem("x_in"), 32)
            for t in range(TT):
                x_squares("a0", t)
            keep_ahead("act", 0, 4)
            act.wait_ge(sem("gains_ready"), 1)
            for t in range(TT):
                split_turned("a0", t, [(h_hi, h_lo, gs, mod[:, 0:8])])
            for c in range(4):
                for g in range(2):
                    h = 4 * c + 2 * g
                    drain(("a_in", c, g), arena[:, h * T:(h + 2) * T], (0, W))
                act.wait_ge(sem("bias_turned"), c + 1)
                for i in range(2):
                    h = 4 * c + 2 * i
                    a.activation(bias1[:, h * T:(h + 2) * T], (ps_s, ps_p)[c % 2][:, i, :], ACT.Copy).then_inc(
                        sem("bias_copied"), 1)
            for c in (4, 5):
                for t in range(TT):
                    drain(("a_in", c, "tok", t), v_tok[:, t, (c - 4) * W:(c - 3) * W], (0, W))
            attention("diff", 16, True)
            held["act"] = first_piece[("b_in", 0)]
            bank_emptied(act, ("diff", "o", 7))
            for t in range(TT):
                square(o_tok[:, t, :], xn[:, t, :], signal=sem("diff_squares"))
            a.activation(stat[:, 8:16], params[:, col["subln"]:col["subln"] + 1].to_broadcast([P, KT]), ACT.Copy,
                         scale=1.0 - LAM_INIT).then_inc(sem("subln_ready"), 1)
            act.wait_ge(sem("subln_ready"), 1)
            for t in range(TT):
                split_turned("diff_o", t, [(h_hi, h_lo, stat[:, 8:16], None)])
                keep_ahead("act", first_piece[("a_out", 0)])
            keep_ahead("act", first_piece[("a_out", 1)])
            norm("m0", [(h_hi, h_lo, gs, mod[:, 24:32])], 2, ready=(3, 4), last=last_of(("a_out", 1)))
            mlp("m0")
            norm("kv", [(h_hi, h_lo, gs, mod[:, 64:72]), (hk_hi, hk_lo, gs2, mod[:, 48:56])], 4, ready=(6, 8),
                 last=last_of(("m0_w2", 7)))
            for w_, name in enumerate(("k_slc", "k_win")):
                src = bank_full(act, (name, 0))
                for par in range(2):
                    for i in range(2):
                        for g in range(2):
                            ins = a.activation(k_nsa[64 * par:64 * par + 64, w_, 2 * i + g, :],
                                               src[64 * g:64 * g + 64, i * T:(i + 1) * T], ACT.Copy)
                ins.then_inc(drained[uses[(name, 0)][0]], 1)
                for t in range(TT):
                    drain(("w_kv", 1 + w_, "tok", t), v_nsa[:, w_, t, :], (0, 256))
            held["act"] = first_piece[("b_out", 0)]
            for s in range(2):
                act.wait_ge(sem("gelu_arg"), s + 1)
                a.activation(gel[:, 2, :, :], gel[:, 1, :, :], ACT.Exp, scale=-2.0 * GELU_C).then_inc(
                    sem("gelu_exp"), 1)
            for c in range(2):
                for g in range(2):
                    h = 4 * c + 2 * g
                    drain(("b_in", c, g), arena[:, h * T:(h + 2) * T], (0, W))
            for t in range(TT):
                src = bank_full(act, ("b_in", 2, "tok", t))
                a.activation(gates[:, t, :], src[:, 0:48], ACT.Exp, scale=-1.0).then_inc(
                    drained[uses[("b_in", 2, "tok", t)][0]], 1)
            act.wait_ge(sem("cmp_centred"), 1)
            a.activation(s_cmp2[:, :, :, 0:NCMP], s_cmp[:, :, :, 0:NCMP], ACT.Exp).then_inc(sem("cmp_exped"), 1)
            for t in range(TT):
                drain(("cmp_turn", t), extra[:, 1024 + t * W:1024 + (t + 1) * W], (0, W))
            attention("slc", HEADS, False)
            attention("win", HEADS, False)
            del held["act"]
            for t in range(TT):
                split_turned("nsa_o", t, [(h_hi, h_lo, None, None)])
                keep_ahead("act", first_piece[("b_out", 0)])
            a.dma_start(pos_i[:, 0:T], dram["positions_2"][0:1, :].to_broadcast([P, T])).then_inc(sem("late_in"), 16)
            a.dma_start(pos_i[:, T:T + TT], dram["positions_2"].rearrange("a (t p) -> p (a t)", p=P),
                        allow_slow_non_contiguous=True).then_inc(sem("late_in"), 16)
            a.dma_start(table2[:, :], row(dram["rel_bias_table_2"].rearrange("b h -> (b h)"), 256)).then_inc(
                sem("late_in"), 16)
            a.dma_start(inv_freq[:, :], dram["inv_freq"]).then_inc(sem("late_in"), 16)
            a.dma_start(pe_gain[:, 0, :], row(dram["mla_q_rope_norm_2"][0], 64)).then_inc(sem("late_in"), 16)
            a.dma_start(pe_gain[:, 1, :], row(dram["mla_k_rope_norm_2"][0], 64)).then_inc(sem("late_in"), 16)
            a.dma_start(fn_row[:, :], row(dram["final_norm"], D)).then_inc(sem("final_in"), 16)
            keep_ahead("act", first_piece[("b_out", 1)])
            norm("m1", [(h_hi, h_lo, gs, mod[:, 64 + 24:64 + 32])], 5, ready=(11, 12),
                 last=last_of(("b_out", 1)))
            mlp("m1")
            act.wait_ge(sem("angles_ready"), 1)
            a.activation(ang[:, 1, :, :], ang[:, 0, :, :], ACT.Abs).then_inc(sem("abs_ready"), 1)
            a.activation(stat[:, 16:17], params[:, 0:1], ACT.Copy, scale=0.0).then_inc(sem("abs_ready"), 1)
            act.wait_ge(sem("abs_ready"), 2)
            a.activation(stat[:, 17:18], stat[:, 16:17], ACT.Copy, bias=math.pi / 2).then_inc(sem("abs_ready"), 1)
            a.activation(trig[:, 1, :, :], ang[:, 0, :, :], ACT.Sin).then_inc(sem("trig_ready"), 1)
            act.wait_ge(sem("abs_ready"), 3)
            a.activation(trig[:, 0, :, :], ang[:, 1, :, :], ACT.Sin, scale=-1.0, bias=stat[:, 17:18]).then_inc(
                sem("trig_ready"), 1)

            last = last_of(("m1_w2", 7))
            x_squares("final", 0, 14)
            act.wait_ge(sem("bias_half"), 1)
            a.dma_start(bias_stash[:, :], bias1[:, 0:4 * STRIP]).then_inc(sem("stashed"), 16)
            keep_ahead("act", last - 2)
            x_squares("l", 0, 15)
            keep_ahead("act", last - 1)
            x_squares("final", 1, 17)
            outs = [(h_hi, h_lo, params[:, col["an2_0"]:col["an2_0"] + KT], None)]
            split_turned("l", 0, outs)
            keep_ahead("act", last + 1)
            x_squares("l", 1, 18)
            split_turned("l", 1, outs)
            for c, n in ((0, W), (1, 192)):
                for t in range(TT):
                    drain(("l_in", c, "tok", t), lat[:, t, c * W:c * W + n], (0, n))
            for c in range(2):
                for t in range(TT):
                    bank_emptied(act, ("l_in", c, "tok", t))
            for t in range(TT):
                square(lat[:, t, :], arena[:, t * 704:(t + 1) * 704], signal=sem("lat_squares"))
            for t in range(TT):
                split_turned("latent", t, [(h_hi, h_lo, params[:, col["qan"]:col["qan"] + 5], None)], 5)
            act.wait_ge(sem("stashed"), 16)
            for c in range(3):
                for t in range(TT):
                    drain(("l_uq", c, "tok", t), bias1[:, t * 1536 + c * W:t * 1536 + (c + 1) * W], (0, W))
            for c in range(3):
                for t in range(TT):
                    bank_emptied(act, ("l_uq", c, "tok", t))
            for t in range(TT):
                square(bias1[:, t * 1536:(t + 1) * 1536], arena[:, t * 1536:(t + 1) * 1536], signal=sem("lq_squares"))
            for c in range(4):
                for t in range(TT):
                    key = ("l_ukv", c, "tok", t)
                    src = bank_full(act, key).rearrange("p (h c) -> p h c", c=T)
                    b = uses[key][0]
                    a.activation(lk[:, t, 2 * c:2 * c + 2, :], src[:, :, 0:P], ACT.Copy).then_inc(drained[b], 1)
                    a.activation(v_tok[:, t, :].rearrange("p (h c) -> p h c", c=P)[:, 2 * c:2 * c + 2, :],
                                 src[:, :, P:2 * P], ACT.Copy).then_inc(drained[b], 1)
            drain("kpe_turn", kpe_t, (0, T))
            for c in range(4):
                for t in range(TT):
                    bank_emptied(act, ("l_ukv", c, "tok", t))
            for t in range(TT):
                square(lk[:, t], extra[:, t * 1024:(t + 1) * 1024].rearrange("p (h c) -> p h c", c=P),
                       signal=sem("lk_squares"))
            act.wait_ge(sem("lk_normed"), 1)
            for what, dst, gname in (("q", 0, "qnn"), ("k", 2048, "knn")):
                for g in range(4):
                    drain(("l_turn", what, g), arena[:, dst + 2 * g * T:dst + (2 * g + 2) * T], (0, W),
                          params[:, col[gname]:col[gname] + 1])
            for g in range(2):
                drain(("qpe_turn", g), extra[:, 3072 + 2 * g * T:3072 + (2 * g + 2) * T], (0, W))
            attention("mla", 8, False)
            for t in range(TT):
                split_turned("mla_o", t, [(h_hi, h_lo, None, None)])
                keep_ahead("act", first_piece[("l_o", 0)])
            a.dma_start(bias1[:, 0:4 * STRIP], bias_stash[:, :]).then_inc(sem("stash_back"), 16)
            keep_ahead("act", first_piece[("l_o", 1)])
            norm("m2", [(h_hi, h_lo, params[:, col["mn2_0"]:col["mn2_0"] + KT], None)], 0,
                 after=lambda t: ("l_o", 1, "tok", t), last=last_of(("l_o", 1)))
            mlp("m2")

            norm("o", [(h_hi, h_lo, params[:, col["an2_1"]:col["an2_1"] + KT], None)], 0,
                 ready=(20, 22), last=last_of(("m2_w2", 7)))
            for c in range(4):
                to = xn if c < 2 else o_tok
                for t in range(TT):
                    key = ("o_qkv", c, "tok", t)
                    src = bank_full(act, key)
                    cc = c % 2
                    at = (0 if c < 2 else 2048) + t * D + cc * W
                    a.activation(to[:, t, cc * W:(cc + 1) * W], src, ACT.Copy).then_inc(drained[uses[key][0]], 1)
                    a.activation(extra[:, at:at + W], src, ACT.Square).then_inc(drained[uses[key][0]], 1)
            for c in (4, 5):
                for t in range(TT):
                    drain(("o_qkv", c, "tok", t), v_tok[:, t, (c - 4) * W:(c - 3) * W], (0, W))
            for what, dst, gname in (("q", 0, "mqn"), ("k", 2048, "mkn")):
                for g in range(4):
                    drain(("o_turn", what, g), arena[:, dst + 2 * g * T:dst + (2 * g + 2) * T], (0, W),
                          params[:, col[gname]:col[gname] + 1])
            attention("moba", 8, False)
            for t in range(TT):
                split_turned("moba_o", t, [(h_hi, h_lo, None, None)])
                keep_ahead("act", first_piece[("o_o", 0)])
            keep_ahead("act", first_piece[("o_o", 1)])
            norm("m3", [(h_hi, h_lo, params[:, col["mn2_1"]:col["mn2_1"] + KT], None)], 0,
                 after=lambda t: ("o_o", 1, "tok", t), last=last_of(("o_o", 1)))
            mlp("m3")

        @block.gpsimd
        def _(pool):
            g_ = nc.gpsimd
            g_.memset(mhalf[:, :], -0.5).then_inc(sem("mhalf_set"), 1)
            pool.wait_ge(sem("mhalf_set"), 1)
            squared_before = {rstd_at[(name, 0)]: tag for name, tag in (("kv", "m0"), ("final", "m1"), ("o", "m2"))}

            def roots(k):
                width, n = rstd_calls[k]
                at = (k % 4) * 16
                pool.wait_ge(ss_ready, k + 1)
                g_.tensor_scalar(rs[:, at:at + width], ss[:, at:at + width], 1.0 / n, EPS, ALU.mult,
                                 ALU.add).then_inc(sem("mean_ready"), 1)
                pool.wait_ge(sem("mean_ready"), k + 1)
                g_.tensor_tensor(rs[:, at:at + width], rs[:, at:at + width], mhalf[:, 0:width],
                                 ALU.pow).then_inc(rstd_ready, 1)

            def matvecs(keys, sums, term):
                pool.wait_ge(matvec_done, 1)
                for key, total in zip(keys, sums):
                    first = first_load[key]
                    for k in range(KT):
                        if k % 2 == 0:
                            load_wait(pool, first + k // 2)
                        w = loaded(first + k // 2)[:, k % 2, :]
                        g_.tensor_scalar(term if k else total, w, c_col[:, k:k + 1], None, ALU.mult).then_inc(
                            sem("pool_terms"), 1)
                        n_terms[0] += 1
                        if k % 2:
                            freed[first + k // 2] = (sem("pool_terms"), n_terms[0])
                        pool.wait_ge(sem("pool_terms"), n_terms[0])
                        if k:
                            ins = g_.tensor_tensor(total, term, total, ALU.add)
                            if k < KT - 1:
                                ins.then_inc(sem("pool_terms"), 1)
                                n_terms[0] += 1
                                pool.wait_ge(sem("pool_terms"), n_terms[0])
                    ins.then_inc(sem("pool_matvec"), 1)
                    n_matvecs[0] += 1
                    pool.wait_ge(sem("pool_matvec"), n_matvecs[0])

            n_terms, n_matvecs = [0], [0]

            def bucket(half, b_):
                n = half * BUCKETS + b_
                pool.wait_ge(sem("bucket_ready"), n + 1)
                if n:
                    pool.wait_ge(sem("bucket_used"), n)
                for h in range(POOL_HEADS):
                    c = b_ * 8 + 4 * half + h
                    g_.tensor_scalar(bias_term[:, h, :], onehot[:, b_ % 2, :], table2[:, c:c + 1], None,
                                     ALU.mult).then_inc(sem("bias_terms"), 1)
                for h in range(POOL_HEADS):
                    pool.wait_ge(sem("bias_terms"), POOL_HEADS * n + h + 1)
                    to = bias2[:, 4 * half + h, :]
                    ins = g_.tensor_tensor(to, bias_term[:, h, :], mask[:, :] if b_ == 0 else to, ALU.add)
                ins.then_inc(sem("bucket_used"), 1)

            def squares(tag):
                looked_up = 0
                for b in range(2 * FF // W):
                    if tag in ("m1", "m2"):
                        c = b // 2
                        while looked_up < (8 * c - 4 if c else 0) // 2 + b % 2:
                            bucket(tag == "m2", looked_up)
                            looked_up += 1
                    pool.wait_ge(sem("mlp_ghi"), 16 * int(tag[1]) + b + 1)
                    h = hidden[:, b % 3, :]
                    g_.tensor_tensor(h, h, h, ALU.mult).then_inc(sem("mlp_sq"), 1)
                if tag in ("m1", "m2"):
                    for b_ in range(looked_up, BUCKETS):
                        bucket(tag == "m2", b_)

            for k in range(len(rstd_calls)):
                if k in squared_before:
                    squares(squared_before[k])
                if k == rstd_at[("a0", 1)] + 1:
                    matvecs(*early)
                if k == rstd_at[("m1", 0)]:
                    pool.wait_ge(sem("kv_split"), 8)
                    pool.wait_ge(mod_drained, 22)
                    matvecs(*late)
                roots(k)
            squares("m3")

        @block.sync
        def _(sp):
            sp.dma_start(c_raw[:, :], dram["c"][0].rearrange("(k p) -> p k", p=P),
                         allow_slow_non_contiguous=True).then_inc(sem("c_in"), 16)
            for i, (key, (k0, k1), (n0, n1)) in enumerate(loads):
                if i >= SLOTS:
                    sp.wait_ge(*freed[i - SLOTS])
                name, k, n = chunk_of[key][1]
                if name == "cmp_w1":
                    src = dram[name][k].rearrange("(k p) n -> p k n", p=P)[:, k0:k1, :]
                else:
                    src = dram[name].rearrange("(k p) n -> p k n", p=P)[:, k + k0:k + k1, n + n0:n + n1]
                sp.dma_start(loaded(i), src).then_inc(load_in[i % SLOTS], 16)
            for t in range(TT):
                for n in range(2):
                    sp.wait_ge(x_ready, 22 + 2 * t + n + 1)
                    sp.dma_start(out[0, t * P:(t + 1) * P, n * W:(n + 1) * W],
                                 x_res[:, t, n * W:(n + 1) * W]).then_inc(sem("out_done"), 16)
            sp.wait_ge(sem("out_done"), 64)


def shape_constants():
    p = np.arange(P)
    dist = 255 - np.arange(384)
    starts = list(range(17)) + [math.ceil(16 * 8.0 ** (i / 16) - 1e-6) for i in range(1, 16)]
    bucket = np.searchsorted(np.array(starts), np.maximum(dist, 0), side="right") - 1
    onehot = (np.arange(BUCKETS)[:, None] == bucket[None, :]).astype(np.float32)
    negrow = np.broadcast_to(np.where(dist < 0, NEG, 0.0), (HEADS, 384)).astype(np.float32)
    tri = np.where(p[:, None] >= p[None, :], 0.0, NEG).astype(np.float32)
    mask = np.concatenate([tri, np.zeros((P, P), np.float32), tri], axis=1)
    q = np.arange(T).reshape(TT, P).T
    valid = (np.arange(NCMP) * 16 + 31)[None, None, :] <= q[:, :, None]
    cmask = np.stack([np.where(valid, 0.0, NEG), valid.astype(np.float64)], axis=1).astype(np.float32)
    inv = (10000.0 ** (-np.arange(0, 64, 2) / 64)).astype(np.float32)
    return {"ident": np.eye(P, dtype=np.float32), "flip": np.eye(P, dtype=np.float32)[::-1].copy(), "mask": mask,
            "negrow": negrow, "cmask": cmask.reshape(P, -1), "onehot": onehot,
            "inv_freq": np.broadcast_to(inv, (P, 32)).copy()}


def param_rows(inputs):
    source = {"c": ("c", 0), "kv_b": ("kv_ada_b", None), "kvn": ("kv_norm", None), "subln": ("a_subln", 0),
              "qan": ("mla_q_a_norm_2", 0), "kvan": ("mla_kv_a_norm_2", 0), "qnn": ("mla_q_nope_norm_2", 0),
              "knn": ("mla_k_nope_norm_2", 0), "mqn": ("moba_q_norm_2", 0), "mkn": ("moba_k_norm_2", 0),
              "ada_b0": ("ada_b", 0), "ada_b1": ("ada_b", 1), "an0": ("attn_norm", 0), "an1": ("attn_norm", 1),
              "mn0": ("mlp_norm", 0), "mn1": ("mlp_norm", 1), "an2_0": ("attn_norm_2", 0),
              "an2_1": ("attn_norm_2", 1), "mn2_0": ("mlp_norm_2", 0), "mn2_1": ("mlp_norm_2", 1)}
    rows = []
    for name, n in PARAM_ROWS:
        array, layer = source[name]
        vector = np.asarray(inputs[array])
        rows.append((vector if layer is None else vector[layer]).reshape(n, P))
    return np.concatenate(rows)


def kernel(**inputs):
    import concourse.bacc as bacc
    from concourse.bass_utils import run_bass_kernel_spmd

    nc = bacc.Bacc("TRN2", target_bir_lowering=False, num_devices=1)
    arrays = {name: np.ascontiguousarray(a) for name, a in inputs.items()}
    arrays.update(shape_constants())
    arrays["param_rows"] = param_rows(inputs)
    feed, dram = {}, {}
    for name, a in arrays.items():
        feed[f"in_{name}"] = a
        dram[name] = nc.dram_tensor(f"in_{name}", a.shape, mybir.dt.from_np(a.dtype), kind="ExternalInput").ap()
    stack_one = {"a_in": dram["a_w_in"][0], "a_out": dram["a_w_out"][0], "b_in": dram["b_w_in"][0],
                 "b_out": dram["b_w_out"][0], "ada0": dram["ada_w"][0], "ada1": dram["ada_w"][1],
                 "adakv": dram["kv_ada_w"]}
    stack_two = {"l_in": dram["mla_w_in_2"][0], "l_uq": dram["mla_w_uq_2"][0], "l_ukv": dram["mla_w_ukv_2"][0],
                 "l_o": dram["mla_w_o_2"][0], "o_qkv": dram["moba_w_qkv_2"][0], "o_o": dram["moba_w_o_2"][0]}
    for i, (w1, w2, layer) in enumerate((("mlp_w1", "mlp_w2", 0), ("mlp_w1", "mlp_w2", 1),
                                         ("mlp_w_in_2", "mlp_w_out_2", 0), ("mlp_w_in_2", "mlp_w_out_2", 1))):
        stack_two[f"m{i}_w1"] = dram[w1][layer]
        stack_two[f"m{i}_w2"] = dram[w2][layer]
    dram.update(stack_one)
    dram.update(stack_two)
    out = nc.dram_tensor("out", (1, T, D), F32, kind="ExternalOutput").ap()
    build(nc, dram, out)
    r = run_bass_kernel_spmd(nc, [feed], core_ids=[0])
    return r.results[0]["out"]
```
